# Optimizing a Trainium2 kernel written in Bass

```python
import math
import jax, jax.numpy as jnp
from jax import lax
import numpy as np

D_MODEL = 1024
BATCH = 1
SEQ = 4096
DEPTH = 1

A_HEADS = 8
A_KV_HEADS = 2
A_HEAD_DIM = 64
A_WIDTH = A_HEADS * A_HEAD_DIM
A_KV_WIDTH = A_KV_HEADS * A_HEAD_DIM
WINDOW = 128
BLOCK = 128
ROPE_THETA = 500000.0
ROPE_DIM = A_HEAD_DIM // 4
B_HEADS = 4
B_KEY_DIM = 64
B_VAL_DIM = 128
B_KEY_WIDTH = B_HEADS * B_KEY_DIM
B_WIDTH = B_HEADS * B_VAL_DIM
B_GATE_RANK = 16
B_GATE_TEMP = 16.0
B_CHUNK = 64
NORM_EPS = 1e-6
NEG_BIG = -1e30

IN_SPLITS = (A_WIDTH, A_KV_WIDTH, A_KV_WIDTH, A_WIDTH,
             B_KEY_WIDTH, B_KEY_WIDTH, B_WIDTH, B_WIDTH, B_GATE_RANK,
             D_MODEL, D_MODEL)
D_IN = 2 * A_WIDTH + 2 * A_KV_WIDTH + 2 * B_KEY_WIDTH + 2 * B_WIDTH + B_GATE_RANK + 2 * D_MODEL

kernel_name = "hybrid_swa_sink_gla_gated_merge"

def rms_norm(x, g):
    xf = x.astype(jnp.float32)
    y = xf * lax.rsqrt(jnp.mean(xf * xf, axis=-1, keepdims=True) + NORM_EPS)
    return (y * g.astype(jnp.float32)).astype(x.dtype)

def partial_rope(t, positions):
    half = ROPE_DIM // 2
    inv_freq = jnp.exp(-math.log(ROPE_THETA) * jnp.arange(half, dtype=jnp.float32) * (2.0 / ROPE_DIM))
    ang = positions.astype(jnp.float32)[..., None] * inv_freq
    cos = jnp.cos(ang)[:, :, None, :]
    sin = jnp.sin(ang)[:, :, None, :]
    tr = t[..., :ROPE_DIM].astype(jnp.float32)
    t1, t2 = tr[..., :half], tr[..., half:]
    rot = jnp.concatenate([t1 * cos - t2 * sin, t2 * cos + t1 * sin], axis=-1)
    return jnp.concatenate([rot.astype(t.dtype), t[..., ROPE_DIM:]], axis=-1)

def sliding_window_gqa_sinks(q, k, v, sinks):
    b, s = q.shape[0], q.shape[1]
    nb = s // BLOCK
    grp = A_HEADS // A_KV_HEADS
    qb = q.reshape(b, nb, BLOCK, A_KV_HEADS, grp, A_HEAD_DIM).astype(jnp.float32)
    kb = k.reshape(b, nb, BLOCK, A_KV_HEADS, A_HEAD_DIM).astype(jnp.float32)
    vb = v.reshape(b, nb, BLOCK, A_KV_HEADS, A_HEAD_DIM).astype(jnp.float32)

    def with_prev(t):
        prev = jnp.pad(t[:, :-1], ((0, 0), (1, 0), (0, 0), (0, 0), (0, 0)))
        return jnp.concatenate([prev, t], axis=2)

    kw, vw = with_prev(kb), with_prev(vb)
    scores = jnp.einsum('bnqhgd,bnkhd->bnhgqk', qb, kw) * (A_HEAD_DIM ** -0.5)
    qi = jnp.arange(BLOCK)[:, None]
    kj = jnp.arange(2 * BLOCK)[None, :] - BLOCK
    band = (kj <= qi) & (qi - kj < WINDOW)
    blk = jnp.arange(nb)[:, None, None]
    valid = band[None] & ((blk > 0) | (kj[None] >= 0))
    scores = jnp.where(valid[None, :, None, None], scores, NEG_BIG)
    sink = sinks.astype(jnp.float32).reshape(A_KV_HEADS, grp)[None, None, :, :, None, None]
    m = jnp.maximum(jnp.max(scores, axis=-1, keepdims=True), sink)
    p = jnp.exp(scores - m)
    denom = jnp.sum(p, axis=-1, keepdims=True) + jnp.exp(sink - m)
    probs = p / denom
    out = jnp.einsum('bnhgqk,bnkhd->bnqhgd', probs, vw)
    return out.reshape(b, s, A_WIDTH).astype(q.dtype)

def gla_chunked(q, k, v, log_a):
    b, s = q.shape[0], q.shape[1]
    nc = s // B_CHUNK

    def chunks(t):
        return t.astype(jnp.float32).reshape(b, nc, B_CHUNK, B_HEADS, t.shape[-1]).transpose(0, 3, 1, 2, 4)

    qc = chunks(q) * (B_KEY_DIM ** -0.5)
    kc, vc, gc = chunks(k), chunks(v), chunks(log_a)
    cum = jnp.cumsum(gc, axis=3)
    last = cum[:, :, :, -1:, :]
    mid = cum[:, :, :, B_CHUNK // 2 - 1:B_CHUNK // 2, :]
    attn = jnp.einsum('bhnid,bhnjd->bhnij', qc * jnp.exp(cum - mid), kc * jnp.exp(mid - cum))
    causal = jnp.tril(jnp.ones((B_CHUNK, B_CHUNK), dtype=bool))
    attn = jnp.where(causal, attn, 0.0)
    o_intra = jnp.einsum('bhnij,bhnjv->bhniv', attn, vc)
    inc = jnp.einsum('bhnjd,bhnjv->nbhdv', kc * jnp.exp(last - cum), vc)
    decay = jnp.exp(last[:, :, :, 0, :]).transpose(2, 0, 1, 3)

    def step(state, xs):
        dec, add = xs
        return dec[..., None] * state + add, state

    init = jnp.zeros((b, B_HEADS, B_KEY_DIM, B_VAL_DIM), jnp.float32)
    _, s_prev = lax.scan(step, init, (decay, inc))
    o_inter = jnp.einsum('bhnid,nbhdv->bhniv', qc * jnp.exp(cum), s_prev)
    o = (o_intra + o_inter).transpose(0, 2, 3, 1, 4)
    return o.reshape(b, s, B_HEADS, B_VAL_DIM)

def hybrid_layer(x, positions, g_in, w_in, w_alpha_up, b_alpha, attn_sinks, g_gla_norm,
                 w_out_a, w_out_b, w_o):
    b, s = x.shape[0], x.shape[1]
    h = rms_norm(x, g_in)
    proj = jnp.einsum('bsd,de->bse', h, w_in)
    split_points = np.cumsum(IN_SPLITS)[:-1].tolist()
    qa, ka, va, za, qb, kb, vb, zb, a_lr, gate_a, gate_b = jnp.split(proj, split_points, axis=-1)

    qa = partial_rope(qa.reshape(b, s, A_HEADS, A_HEAD_DIM), positions)
    ka = partial_rope(ka.reshape(b, s, A_KV_HEADS, A_HEAD_DIM), positions)
    va = va.reshape(b, s, A_KV_HEADS, A_HEAD_DIM)
    oa = sliding_window_gqa_sinks(qa, ka, va, attn_sinks) * jax.nn.silu(za)
    ya = jnp.einsum('bse,ed->bsd', oa, w_out_a)

    log_a = jax.nn.log_sigmoid(
        (jnp.einsum('bsr,re->bse', a_lr, w_alpha_up) + b_alpha).astype(jnp.float32)) / B_GATE_TEMP
    ob = gla_chunked(qb.reshape(b, s, B_HEADS, B_KEY_DIM),
                     kb.reshape(b, s, B_HEADS, B_KEY_DIM),
                     vb.reshape(b, s, B_HEADS, B_VAL_DIM),
                     log_a.reshape(b, s, B_HEADS, B_KEY_DIM))
    ob = ob * lax.rsqrt(jnp.mean(ob * ob, axis=-1, keepdims=True) + NORM_EPS)
    ob = (ob.reshape(b, s, B_WIDTH) * g_gla_norm.astype(jnp.float32)).astype(x.dtype) * jax.nn.silu(zb)
    yb = jnp.einsum('bse,ed->bsd', ob, w_out_b)

    merged = jax.nn.sigmoid(gate_a) * ya + jax.nn.sigmoid(gate_b) * yb
    return x + jnp.einsum('bsd,de->bse', merged, w_o)

def setup_inputs(seed: int = 0) -> dict:
    key = jax.random.key(seed)
    ks = jax.random.split(key, 12)
    nrm = jax.random.normal
    f32 = jnp.float32
    x = nrm(ks[0], (BATCH, SEQ, D_MODEL), f32)
    positions = jnp.broadcast_to(jnp.arange(SEQ, dtype=jnp.int32)[None, :], (BATCH, SEQ))
    g_in = 1.0 + 0.02 * nrm(ks[1], (DEPTH, D_MODEL), f32)
    w_in = nrm(ks[2], (DEPTH, D_MODEL, D_IN), f32) * D_MODEL ** -0.5
    w_alpha_up = nrm(ks[3], (DEPTH, B_GATE_RANK, B_KEY_WIDTH), f32) * B_GATE_RANK ** -0.5
    b_alpha = 0.1 * nrm(ks[4], (DEPTH, B_KEY_WIDTH), f32)
    attn_sinks = 0.5 * nrm(ks[5], (DEPTH, A_HEADS), f32)
    g_gla_norm = 1.0 + 0.02 * nrm(ks[6], (DEPTH, B_WIDTH), f32)
    w_out_a = nrm(ks[7], (DEPTH, A_WIDTH, D_MODEL), f32) * A_WIDTH ** -0.5
    w_out_b = nrm(ks[8], (DEPTH, B_WIDTH, D_MODEL), f32) * B_WIDTH ** -0.5
    w_o = nrm(ks[9], (DEPTH, D_MODEL, D_MODEL), f32) * D_MODEL ** -0.5
    g_final = 1.0 + 0.02 * nrm(ks[10], (D_MODEL,), f32)
    return {"x": x, "positions": positions, "g_in": g_in, "w_in": w_in,
            "w_alpha_up": w_alpha_up, "b_alpha": b_alpha, "attn_sinks": attn_sinks,
            "g_gla_norm": g_gla_norm, "w_out_a": w_out_a, "w_out_b": w_out_b,
            "w_o": w_o, "g_final": g_final}

def reference(x, positions, g_in, w_in, w_alpha_up, b_alpha, attn_sinks, g_gla_norm,
              w_out_a, w_out_b, w_o, g_final):
    h = x
    for layer in range(DEPTH):
        h = hybrid_layer(h, positions, g_in[layer], w_in[layer], w_alpha_up[layer], b_alpha[layer],
                         attn_sinks[layer], g_gla_norm[layer], w_out_a[layer], w_out_b[layer],
                         w_o[layer])
    return rms_norm(h, g_final)


_drawn_inputs = setup_inputs


def setup_inputs(seed=0):
    import zlib

    import numpy as np

    out = dict(_drawn_inputs(seed))
    spreads = {}
    factors = {'g_in': 4.035,
     'b_alpha': 4.176,
     'attn_sinks': 64.0,
     'g_gla_norm': 24.641,
     'g_final': 8.508}
    for name, (base, spread) in spreads.items():
        noise = np.random.default_rng([zlib.crc32(name.encode()), seed]).standard_normal(out[name].shape)
        drawn = base * np.exp(spread * noise) if base else spread * noise
        out[name] = __import__('jax').numpy.asarray(drawn.astype(out[name].dtype))
    for name, factor in factors.items():
        out[name] = (out[name] * factor).astype(out[name].dtype)
    return out
```

```python
from contextlib import ExitStack

import numpy as np
import concourse.bass as bass
from concourse import mybir

ALU = mybir.AluOpType
ACT = mybir.ActivationFunctionType
AX = mybir.AxisListType
F32 = mybir.dt.float32
F16 = mybir.dt.float16
I32 = mybir.dt.int32
U32 = mybir.dt.uint32
RMAX = bass.bass_isa.ReduceOp.max

P = 128
D = 1024
KT = D // P
SEQ = 4096
NBLK = SEQ // P
HEADS, KVH, HD = 8, 2, 64
GRP = HEADS // KVH
HALF = HD // 8
THETA = 500000.0
BH, BK, BV = 4, 64, 128
RANK = 16
CH = 64
EPS = 1e-6
NEG = -1e30
BIG_ARG = 40.0
MAGIC = 12582912.0
ROPE_OPS = 18

QC, KC, VC, ZAC = 0, 512, 640, 768
QBC, KBC, VBC, ZBC, ALC = 1280, 1536, 1792, 2304, 2816
NA = ALC + RANK
CHUNKS = [(c, min(c + 512, NA)) for c in range(0, NA, 512)]
NCH = len(CHUNKS)
GATE0 = NCH
OUTA, OUTB = GATE0 + 4, GATE0 + 5
WO0 = GATE0 + 6
NW = WO0 + 2


def two_pi_parts():
    rest, parts = 2 * np.pi, []
    for _ in range(2):
        e = np.floor(np.log2(rest))
        unit = 2.0 ** (e - 11)
        c = np.floor(rest / unit) * unit
        parts.append(float(c))
        rest -= c
    return parts + [float(np.float32(rest))]


def need(eng, sem, n):
    if isinstance(n, int) and n <= 0:
        return
    eng.wait_ge(sem, n)


def hybrid_block(nc, x, positions, g_in, w_in, w_alpha_up, b_alpha, attn_sinks, g_gla_norm,
                 w_out_a, w_out_b, w_o, g_final, out):
    with ExitStack() as ctx:
        def sb(name, shape, dt=F32, stack=ctx):
            return stack.enter_context(nc.sbuf_tensor(name, shape, dt))

        def sem(name):
            return ctx.enter_context(nc.semaphore(name))

        bank = [ctx.enter_context(nc.psum_tensor(f"bank{i}", [P, 512], F32)) for i in range(8)]
        hts = nc.dram_tensor("hts", [NBLK, P, 2 * KT * P], F16, kind="Internal").ap()
        ots = nc.dram_tensor("ots", [NBLK, P, 2 * KT * P], F16, kind="Internal").ap()

        ident = sb("ident", [P, P])
        ident16 = sb("ident16", [P, P], F16)
        wmax = sb("wmax", [P, NW])
        wall = sb("wall", [P, NW])
        wpow = sb("wpow", [P, NW])
        wscale = sb("wscale", [P, NW])
        winv = sb("winv", [P, NW])
        oscale = sb("oscale", [P, NBLK, 2])
        gin = sb("gin", [P, KT])
        ggla = sb("ggla", [P, BH])
        nv = sb("nv", [P, 8])
        ss = sb("ss", [P, 1])
        var = sb("var", [P, 1])
        lnv = sb("lnv", [P, 1])
        y0 = sb("y0", [P, 1])
        nt = sb("nt", [P, 2])
        rstd = sb("rstd", [P, 1])

        s_const = sem("const_loaded")
        s_raw = [sem("raw_even"), sem("raw_odd")]
        s_wg = sem("w_gained")
        s_wmax = sem("w_max")
        s_wall = sem("w_allmax")
        s_wsm = sem("w_scales")
        s_whi = sem("w_hi")
        s_wlo = sem("w_lo")
        s_id = sem("identities")
        s_msk = sem("masks")

        def gla_gain(n):
            return [ggla[:, k:k + 1] for k in range(BH)] if n == OUTB else None

        def prep_gains(n):
            if n < OUTA:
                return [gin[:, k:k + 1] for k in range(KT)]
            return gla_gain(n)

        def chunk_source(n):
            if n < NCH:
                a, b = CHUNKS[n]
                return w_in[:, a:b].rearrange("(k p) n -> p k n", p=P)
            if n < OUTA:
                a = NA + (n - GATE0) * 512
                return w_in[:, a:a + 512].rearrange("(k p) n -> p k n", p=P)
            if n == OUTA:
                return w_out_a.rearrange("(k p) n -> p k n", p=P)
            if n == OUTB:
                return w_out_b.rearrange("(k p) n -> p k n", p=P)
            a = (n - WO0) * 512
            return w_o[:, a:a + 512].rearrange("(k p) n -> p k n", p=P)

        def shaped(tile, n):
            k, w = chunk_source(n).shape[1:]
            return tile[:, 0:k * w].rearrange("p (k n) -> p k n", k=k)

        class Prep:

            def __init__(self, lo, hi, stage, dest):
                self.lo, self.hi, self.stage, self.dest = lo, hi, stage, dest
                self.gained = [n for n in range(NW) if prep_gains(n)]

            def load(self, sp, n):
                need(sp, s_wlo, n - 1)
                sp.dma_start(shaped(self.stage[n % 2], n), chunk_source(n)).then_inc(s_raw[n % 2], 16)

            def raw_here(self, eng, n):
                eng.wait_ge(s_raw[n % 2], 16 * (n // 2 + 1))

            def gain(self, act, n):
                gains = prep_gains(n)
                if not gains:
                    return
                self.raw_here(act, n)
                t = shaped(self.stage[n % 2], n)
                for k, g in enumerate(gains):
                    last = act.activation(t[:, k, :], t[:, k, :], ACT.Copy, scale=g)
                last.then_inc(s_wg, 1)

            def maximum(self, dve, n):
                if prep_gains(n):
                    dve.wait_ge(s_wg, self.gained.index(n) + 1)
                else:
                    self.raw_here(dve, n)
                k, w = chunk_source(n).shape[1:]
                dve.tensor_reduce(wmax[:, n:n + 1], self.stage[n % 2][:, 0:k * w], AX.X, ALU.max,
                                  apply_absolute_value=True).then_inc(s_wmax, 1)

            def over_partitions(self, pool, n):
                pool.wait_ge(s_wmax, n + 1)
                pool.partition_all_reduce(wall[:, n:n + 1], wmax[:, n:n + 1], P, RMAX).then_inc(s_wall, 1)

            def scales(self, dve, n):
                c = slice(n, n + 1)
                dve.wait_ge(s_wall, n + 1)
                dve.tensor_scalar(wpow[:, c], wall[:, c], 1e-30, None, ALU.max).then_inc(s_wsm, 1)
                dve.wait_ge(s_wsm, 4 * n + 1)
                dve.tensor_scalar(wpow[:, c].bitcast(U32), wpow[:, c].bitcast(U32), 0x7F800000, None,
                                  ALU.bitwise_and).then_inc(s_wsm, 1)
                dve.wait_ge(s_wsm, 4 * n + 2)
                dve.tensor_scalar(wscale[:, c], wpow[:, c], 2.0 ** -10, None, ALU.mult).then_inc(s_wsm, 1)
                dve.wait_ge(s_wsm, 4 * n + 3)
                dve.reciprocal(winv[:, c], wscale[:, c]).then_inc(s_wsm, 1)

            def split_hi(self, act, n):
                act.wait_ge(s_wsm, 4 * n + 4)
                if not prep_gains(n):
                    self.raw_here(act, n)
                hi, _ = self.dest(n)
                act.activation(hi, shaped(self.stage[n % 2], n), ACT.Copy,
                               scale=winv[:, n:n + 1]).then_inc(s_whi, 1)

            def split_lo(self, dve, n):
                dve.wait_ge(s_whi, n + 1)
                hi, lo = self.dest(n)
                dve.scalar_tensor_tensor(lo, shaped(self.stage[n % 2], n), winv[:, n:n + 1], hi,
                                         ALU.mult, ALU.subtract).then_inc(s_wlo, 1)

            def on_sync(self, sp):
                for n in range(self.lo, self.hi):
                    self.load(sp, n)

            def on_scalar(self, act):
                for n in range(self.lo, self.hi + 1):
                    if n < self.hi:
                        self.gain(act, n)
                    if n > self.lo:
                        self.split_hi(act, n - 1)

            def on_vector(self, dve):
                for n in range(self.lo, self.hi + 1):
                    if n < self.hi:
                        self.maximum(dve, n)
                    if n > self.lo:
                        self.split_lo(dve, n - 1)
                    if n < self.hi:
                        self.scales(dve, n)

            def on_gpsimd(self, pool):
                for n in range(self.lo, self.hi):
                    self.over_partitions(pool, n)

        def rsqrt_start(dve, s_ss, n, s_v, total, v, width):
            need(dve, s_ss, n)
            dve.tensor_scalar(v, total, 1.0 / width, EPS, ALU.mult, ALU.add).then_inc(s_v, 1)

        def rsqrt_table(act, s_v, n, s_t, k, v, ln, y):
            need(act, s_v, n)
            act.activation(ln, v, ACT.Ln).then_inc(s_t, 1)
            need(act, s_t, k + 1)
            act.activation(y, ln, ACT.Exp, scale=-0.5).then_inc(s_t, 1)

        def rsqrt_newton(dve, s_t, k, s_n, m, v, y, t, r):
            need(dve, s_t, k + 2)
            dve.tensor_tensor(t, y, y, ALU.mult).then_inc(s_n, 1)
            need(dve, s_n, m + 1)
            dve.tensor_tensor(t, t, v, ALU.mult).then_inc(s_n, 1)
            need(dve, s_n, m + 2)
            dve.tensor_scalar(t, t, -0.5, 1.5, ALU.mult, ALU.add).then_inc(s_n, 1)
            need(dve, s_n, m + 3)
            dve.tensor_tensor(r, y, t, ALU.mult).then_inc(s_n, 1)

        with ExitStack() as actx:
            def sa(name, shape, dt=F32):
                return sb(name, shape, dt, actx)

            wh = sa("wh", [P, KT, NA], F16)
            wl = sa("wl", [P, KT, NA], F16)
            arena = sa("arena", [P, 2, 4096])
            scs = arena[:, 0, 0:1024].rearrange("p (h k) -> p h k", h=HEADS)
            ptc = arena[:, 0, 1024:2048].rearrange("p (h k) -> p h k", h=HEADS)
            ptp = arena[:, 0, 2048:3072].rearrange("p (h k) -> p h k", h=HEADS)
            sil = arena[:, 0, 3072:4096]
            brn = arena[:, 1, 0:1024]
            e1 = arena[:, 1, 1024:1280]
            e2 = arena[:, 1, 1280:1536]
            e3 = arena[:, 1, 1536:1792]
            e4 = arena[:, 1, 1792:2048]
            e5q = arena[:, 1, 2048:2176]
            e5k = arena[:, 1, 2176:2304]
            d1 = arena[:, 1, 2304:2560]
            d3 = arena[:, 1, 2560:2816]
            d4 = arena[:, 1, 2816:3072]
            d5 = arena[:, 1, 3072:3200]
            zs = arena[:, 1, 3200:3456]
            sp_ = arena[:, 1, 3456:3712]
            gsp = arena[:, 1, 3712:3968]

            proj = [sa(f"proj{i}", [P, NA]) for i in range(2)]
            xin = [sa(f"xin{i}", [P, D]) for i in range(2)]
            x16 = sa("x16", [P, 2, D], F16)
            hT = [sa(f"hT{i}", [P, 2, KT, P], F16) for i in range(2)]
            junk = sa("junk", [P, D], F16)
            qT = sa("qT", [P, GRP, P])
            kT = [sa(f"kT{i}", [P, P]) for i in range(2)]
            aT = sa("aT", [RANK, P])
            vbuf = [sa(f"vbuf{i}", [P, P]) for i in range(2)]
            gT = sa("gT", [P, 4, P])
            q1 = sa("q1", [P, 2, 2, P])
            q5 = sa("q5", [P, 2, 2, CH])
            q3 = sa("q3", [P, 2, P])
            k1 = sa("k1", [P, 2, P])
            k4 = sa("k4", [P, 2, P])
            k5 = sa("k5", [P, 2, CH])
            k2 = sa("k2", [P, 2, P])
            cum = sa("cum", [P, 2, 2, CH])
            carry = sa("carry", [P, 2, 2])
            seg = sa("seg", [P, 4, CH])
            att = sa("att", [P, BH, P])
            state = sa("state", [P, 2, 2, BV])
            og = sa("og", [P, BH, BV])
            o16 = sa("o16", [P, 2, D], F16)
            oT = sa("oT", [P, 2, KT, P], F16)
            tri = sa("tri", [P, P])
            triT = sa("triT", [P, P])
            triN = sa("triN", [P, P])
            cosT = sa("cosT", [P, NBLK, HALF])
            sinT = sa("sinT", [P, NBLK, HALF])
            rt = sa("rt", [P, 4, HEADS + KVH, HALF])
            sinks = sa("sinks", [P, HEADS])
            wal = sa("wal", [RANK, 2 * P])
            bal = sa("bal", [P, 2])
            mx = sa("mx", [P, HEADS])
            mm = sa("mm", [P, HEADS])
            nm = sa("nm", [P, HEADS])
            dsk = sa("dsk", [P, HEADS])
            es = sa("es", [P, HEADS])
            rsum = sa("rsum", [P, HEADS])
            den = sa("den", [P, HEADS])
            rden = sa("rden", [P, HEADS])
            ss4 = sa("ss4", [P, BH])
            var4 = sa("var4", [P, BH])
            ln4 = sa("ln4", [P, BH])
            y4 = sa("y4", [P, BH])
            nt4 = sa("nt4", [P, BH])
            r4 = sa("r4", [P, BH])
            omax = sa("omax", [P, 2])
            oinv = sa("oinv", [P, 2])
            opow = sa("opow", [P, 2])
            tick = sa("tick", [P, 2])

            ang = brn[:, 0:256]
            pos_i = arena[:, 1, 1024:1024 + NBLK].bitcast(I32)
            pos_f = arena[:, 1, 1056:1056 + NBLK]

            s_x = [sem("x_even"), sem("x_odd")]
            s_xss = sem("x_square_sum")
            s_xv = sem("x_var")
            s_xt = sem("x_rsqrt_table")
            s_xn = sem("x_rsqrt_newton")
            s_x16 = sem("x_split")
            s_xtr = sem("x_transposed")
            s_hT = sem("hT_copied")
            s_hst = [sem("hT_stored_even"), sem("hT_stored_odd")]
            s_pj = sem("projected")
            s_evA = sem("evac_by_scalar")
            s_evD = sem("evac_by_vector")
            s_vb = sem("v_kept")
            s_rm = sem("rope_products")
            s_rp = sem("roped")
            s_t1 = sem("qk_transposed")
            s_qT = sem("qT_copied")
            s_kT = sem("kT_aT_copied")
            s_gT = sem("gT_copied")
            s_z = sem("forget_logits")
            s_zs = sem("forget_logits_copied")
            s_spm = sem("softplus_clamped")
            s_spt = sem("softplus_table")
            s_sp = sem("softplus")
            s_cum = sem("gate_sums")
            s_car = sem("gate_carry")
            s_dif = sem("gate_differences")
            s_e = sem("gate_exps")
            s_gq = sem("gla_factors")
            s_sc = sem("scores")
            s_pv0 = sem("previous_scores_copied")
            s_sel = sem("scores_selected")
            s_mx = sem("row_maxima")
            s_sm = sem("softmax_shift")
            s_es = sem("sink_exps")
            s_ex = sem("score_exps")
            s_den = sem("denominators")
            s_pt = sem("probs_transposed")
            s_ptm = sem("probs_masked")
            s_at = sem("gla_scores")
            s_am = sem("gla_scores_masked")
            s_pvo = sem("attention_out")
            s_kt = sem("gla_keys_turned")
            s_k2 = sem("gla_keys_copied")
            s_go = sem("gla_out")
            s_inc = sem("state_increment")
            s_st = sem("state_updated")
            s_og = sem("gla_out_copied")
            s_gss = sem("gla_square_sum")
            s_gv = sem("gla_var")
            s_gt = sem("gla_rsqrt_table")
            s_gn = sem("gla_rsqrt_newton")
            s_slm = sem("silu_clamped")
            s_slt = sem("silu_tables")
            s_sll = sem("silu_softplus")
            s_sle = sem("silu_sigmoid")
            s_sl = sem("silu")
            s_br = sem("branches_normed")
            s_gat = sem("branches_gated")
            s_om = sem("out_maxima")
            s_o16 = sem("out_split")
            s_otr = sem("out_transposed")
            s_oT = sem("oT_copied")
            s_ost = sem("oT_stored")
            s_rope = sem("rotary_angles")
            s_trig = sem("rotary_tables")
            s_zero = sem("cleared")

            def dest_a(n):
                a, b = CHUNKS[n]
                return wh[:, :, a:b], wl[:, :, a:b]

            prep = Prep(0, NCH, [arena[:, 0, :], arena[:, 1, :]], dest_a)

            def steps(eng, step):
                for t in range(4):
                    step(t, t // 2, t % 2)
                with eng.Fori(0, (NBLK - 6) // 2) as i:
                    for u in range(2):
                        step(i * 2 + (4 + u), i + 2, u)
                for t in range(NBLK - 2, NBLK + 2):
                    step(t, t // 2, t % 2)

            def known(t):
                return isinstance(t, int)

            def has_front(t):
                return not known(t) or t < NBLK

            def has_xprep(t):
                return not known(t) or t + 1 < NBLK

            def has_back(t):
                return not known(t) or 1 <= t <= NBLK

            def has_turn(t):
                return not known(t) or 2 <= t <= NBLK + 1

            block = actx.enter_context(nc.Block())

            @block.sync
            def _(sp):
                def load_x(n, h, u):
                    need(sp, s_x16, (n - 1) * 2)
                    sp.dma_start(xin[u][:, :], x[bass.ds(n * P, P), :]).then_inc(s_x[u], 16)

                load_x(0, 0, 0)
                load_x(1, 0, 1)
                sp.dma_start(gin[:, :], g_in).then_inc(s_const, 16)
                sp.dma_start(ggla[:, :], g_gla_norm).then_inc(s_const, 16)
                sp.dma_start(wal[:, :], w_alpha_up).then_inc(s_const, 16)
                sp.dma_start(bal[:, :], b_alpha).then_inc(s_const, 16)
                sp.dma_start(sinks[:, :], attn_sinks.partition_broadcast(P)).then_inc(s_const, 16)
                sp.dma_start(pos_i, positions).then_inc(s_const, 16)
                prep.load(sp, 0)
                sp.wait_ge(s_trig, 2)
                for n in range(1, NCH):
                    prep.load(sp, n)

                def step(t, h, u):
                    if not known(t) or t + 2 < NBLK:
                        load_x(t + 2, h + 1, u)
                    if has_xprep(t):
                        need(sp, s_hT, (t + 2) * 2)
                        sp.dma_start(hts[bass.ds(t + 1, 1)].rearrange("a p n -> (a p) n"),
                                     hT[1 - u][:, :, :, :].rearrange("p a k t -> p (a k t)")
                                     ).then_inc(s_hst[1 - u], 16)
                    if has_turn(t):
                        need(sp, s_oT, (t - 1) * 2)
                        sp.dma_start(ots[bass.ds(t - 2, 1)].rearrange("a p n -> (a p) n"),
                                     oT[:, :, :, :].rearrange("p a k t -> p (a k t)")
                                     ).then_inc(s_ost, 16)

                sp.wait_ge(s_hT, 2)
                sp.dma_start(hts[0], hT[0][:, :, :, :].rearrange("p a k t -> p (a k t)")).then_inc(s_hst[0], 16)
                steps(sp, step)
                for s, n in ((s_hst[0], NBLK // 2), (s_hst[1], NBLK // 2), (s_ost, NBLK)):
                    sp.wait_ge(s, 16 * n)

            @block.gpsimd
            def _(pool):
                pool.memset(ident[:, :], 0.0).then_inc(s_id, 1)
                pool.memset(ident16[:, :], 0.0).then_inc(s_id, 1)
                pool.memset(tri[:, :], 1.0).then_inc(s_id, 1)
                pool.memset(triT[:, :], 1.0).then_inc(s_id, 1)
                pool.memset(triN[:, :], 1.0).then_inc(s_id, 1)
                pool.wait_ge(s_id, 5)
                for m in (ident, ident16):
                    pool.affine_select(out=m[:, :], in_=m[:, :], compare_op=ALU.not_equal, fill=1.0, base=0,
                                       pattern=[[-1, P]], channel_multiplier=1).then_inc(s_msk, 1)
                for m, op, sign in ((tri, ALU.is_ge, 1), (triT, ALU.is_ge, -1), (triN, ALU.is_gt, 1)):
                    pool.affine_select(out=m[:, :], in_=m[:, :], compare_op=op, fill=0.0, base=0,
                                       pattern=[[-sign, P]], channel_multiplier=sign).then_inc(s_msk, 1)
                pool.memset(q1[:, :, :, :], 0.0).then_inc(s_zero, 1)
                pool.memset(q5[:, :, :, :], 0.0).then_inc(s_zero, 1)
                pool.memset(state[:, :, :, :], 0.0).then_inc(s_zero, 1)
                pool.memset(att[:, :, :], 0.0).then_inc(s_zero, 1)
                pool.memset(carry[:, :, :], 0.0).then_inc(s_zero, 1)
                pool.memset(seg[:, :, :], 1.0).then_inc(s_zero, 1)
                pool.wait_ge(s_zero, 6)
                pool.memset(seg[:, :, 0:1], 0.0).then_inc(s_zero, 1)
                prep.on_gpsimd(pool)

                def step(t, h, u):
                    if not has_back(t):
                        return
                    b, pr = t - 1, proj[1 - u]
                    pool.wait_ge(s_evA, t * 3)
                    pool.wait_ge(s_evD, t * 3)
                    need(pool, s_pvo, b)
                    pool.wait_ge(s_trig, 2)
                    qk = pr[:, 0:VC].rearrange("p (h d) -> p h d", d=HD)
                    x1, x2 = qk[:, :, 0:HALF], qk[:, :, HALF:2 * HALF]
                    c = cosT[:, bass.ds(b, 1), :].broadcast_to([P, HEADS + KVH, HALF])
                    s = sinT[:, bass.ds(b, 1), :].broadcast_to([P, HEADS + KVH, HALF])
                    for n, (a, f) in enumerate(((x1, c), (x2, s), (x2, c), (x1, s))):
                        pool.tensor_tensor(rt[:, n], a, f, ALU.mult).then_inc(s_rm, 1)
                    pool.tensor_copy(vbuf[1 - u][:, :], pr[:, VC:VC + P]).then_inc(s_vb, 1)
                    need(pool, s_rm, t * 4)
                    pool.tensor_tensor(x1, rt[:, 0], rt[:, 1], ALU.subtract).then_inc(s_rp, 1)
                    pool.tensor_tensor(x2, rt[:, 2], rt[:, 3], ALU.add).then_inc(s_rp, 1)
                    need(pool, s_sle, t)
                    pool.tensor_tensor(sil[:, 0:512], sil[:, 0:512], pr[:, ZAC:ZAC + 512], ALU.mult).then_inc(s_sl, 1)
                    pool.tensor_tensor(sil[:, 512:], sil[:, 512:], pr[:, ZBC:ZBC + 512], ALU.mult).then_inc(s_sl, 1)

                steps(pool, step)

            @block.scalar
            def _(act):
                def x_squares(n, h, u):
                    need(act, s_x[u], 16 * h + 16)
                    act.activation(junk[:, :], xin[u][:, :], ACT.Square, accum_out=ss[:, :]).then_inc(s_xss, 1)

                def x_table(n):
                    rsqrt_table(act, s_xv, n + 1, s_xt, n * 2, var[:, :], lnv[:, :], y0[:, :])

                def x_evac(n, h, u):
                    need(act, s_xtr, n + 1)
                    need(act, s_pj, (n - 1) * NCH)
                    need(act, s_hst[u], 16 * h)
                    for a in range(2):
                        act.activation(hT[u][:, a].rearrange("p k t -> p (k t)"),
                                       bank[2 + a][:, :].bitcast(F16), ACT.Copy).then_inc(s_hT, 1)

                def evac(t, u, c):
                    a, b = CHUNKS[c]
                    act.wait_ge(s_pj, t * NCH + (c + 1))
                    if c == 0:
                        need(act, s_inc, t - 1)
                        need(act, s_gat, t - 1)
                        src = bank[0][:, :].rearrange("p (g j d) -> p g j d", g=KVH, j=GRP)
                        dst = proj[u][:, 0:512].rearrange("p (j g d) -> p g j d", g=KVH, j=GRP)
                        for g in range(KVH):
                            last = act.activation(dst[:, g], src[:, g], ACT.Copy, scale=wscale[:, 0:1])
                    else:
                        last = act.activation(proj[u][:, a:b], bank[0][:, 0:b - a], ACT.Copy,
                                              scale=wscale[:, c:c + 1])
                    last.then_inc(s_evA, 1)

                act.wait_ge(s_rope, 2 + 2 * ROPE_OPS + 3)
                act.activation(sinT[:, :, :].rearrange("p n i -> p (n i)"), ang, ACT.Sin).then_inc(s_trig, 1)
                act.activation(cosT[:, :, :].rearrange("p n i -> p (n i)"), brn[:, 256:512],
                               ACT.Sin).then_inc(s_trig, 1)
                act.preload_act_table_set("natural_log_exp_and_others")
                x_squares(0, 0, 0)
                x_table(0)
                act.wait_ge(s_const, 16 * 6)
                prep.on_scalar(act)
                x_evac(0, 0, 0)

                def step(t, h, u):
                    b, pr = t - 1, proj[1 - u]
                    back = has_back(t)
                    if has_xprep(t):
                        x_squares(t + 1, h + u, 1 - u)
                        x_table(t + 1)
                    if has_front(t):
                        evac(t, u, 0)
                    if back:
                        need(act, s_t1, b * 3 + 1)
                        act.activation(qT[:, :, :].rearrange("p j t -> p (j t)"), bank[4][:, :],
                                       ACT.Copy).then_inc(s_qT, 1)
                        need(act, s_t1, b * 3 + 3)
                        act.activation(gT[:, :, :].rearrange("p j t -> p (j t)"), bank[6][:, :],
                                       ACT.Copy).then_inc(s_gT, 1)
                        need(act, s_slm, b * 2 + 2)
                        act.activation(sil, sil, ACT.Exp).then_inc(s_slt, 1)
                        need(act, s_slt, b * 2 + 1)
                        act.activation(sil, sil, ACT.Ln, bias=1.0).then_inc(s_slt, 1)
                        need(act, s_spm, b + 1)
                        act.activation(sp_, sp_, ACT.Exp).then_inc(s_spt, 1)
                        need(act, s_spt, b * 2 + 1)
                        act.activation(sp_, sp_, ACT.Ln, bias=1.0).then_inc(s_spt, 1)
                        if not (known(t) and b == 0):
                            for g in range(KVH):
                                need(act, s_sc, b * 4 + (2, 4)[g])
                                act.activation(scs[:, g * GRP:(g + 1) * GRP, :].rearrange("p h k -> p (h k)"),
                                               bank[(5, 7)[g]][:, :], ACT.Copy).then_inc(s_pv0, 1)
                        need(act, s_sll, b * 2 + 2)
                        act.activation(sil, sil, ACT.Exp, scale=-1.0).then_inc(s_sle, 1)
                        need(act, s_sm, b * 3 + 3)
                        act.activation(es[:, :], dsk[:, :], ACT.Exp).then_inc(s_es, 1)
                        for hd in range(HEADS):
                            act.activation(scs[:, hd, :], scs[:, hd, :], ACT.Exp, bias=nm[:, hd:hd + 1],
                                           scale=HD ** -0.5, accum_out=rsum[:, hd:hd + 1]).then_inc(s_ex, 1)
                        need(act, s_dif, b * 4 + 4)
                        need(act, s_gq, b * 8)
                        need(act, s_st, b * 4)
                        for o, i, sc in ((e1, d1, 1), (e2, d1, -1), (e3, d3, 1), (e4, d4, -1),
                                         (e5k, d5, -1)):
                            act.activation(o, i, ACT.Exp, scale=sc / 16.0).then_inc(s_e, 1)
                        act.activation(e5q.rearrange("p (a c) -> p a c", a=2), cum[:, :, 1, :], ACT.Exp,
                                       scale=1 / 16.0).then_inc(s_e, 1)
                    if has_front(t):
                        evac(t, u, 2)
                    if has_turn(t):
                        need(act, s_otr, t - 1)
                        need(act, s_ost, (t - 2) * 16)
                        for a in range(2):
                            act.activation(oT[:, a].rearrange("p k t -> p (k t)"),
                                           bank[2 + a][:, :].bitcast(F16), ACT.Copy).then_inc(s_oT, 1)
                    if has_front(t):
                        evac(t, u, 4)
                    if back:
                        need(act, s_kt, t)
                        act.activation(k2[:, :, :].rearrange("p a t -> p (a t)"), bank[4][:, 0:256],
                                       ACT.Copy).then_inc(s_k2, 1)
                    if has_xprep(t):
                        x_evac(t + 1, h + u, 1 - u)
                    if back:
                        need(act, s_go, t)
                        act.activation(og[:, :, :].rearrange("p h v -> p (h v)"), bank[5][:, :],
                                       ACT.Copy).then_inc(s_og, 1)
                        need(act, s_og, t)
                        for hd in range(BH):
                            act.activation(junk[:, hd * BV:(hd + 1) * BV], og[:, hd, :], ACT.Square,
                                           accum_out=ss4[:, hd:hd + 1]).then_inc(s_gss, 1)
                        rsqrt_table(act, s_gv, t, s_gt, b * 2, var4[:, :], ln4[:, :], y4[:, :])

                steps(act, step)

            @block.tensor
            def _(pe):
                def turn16(tile, s_in, n_in):
                    need(pe, s_in, n_in)
                    for a in range(2):
                        dst = bank[2 + a][:, :].bitcast(F16)
                        for k in range(KT):
                            last = pe.transpose(dst[:, k * P:(k + 1) * P], tile[:, a, k * P:(k + 1) * P],
                                                ident16[:, :])
                    return last

                def chunk(t, u, c):
                    a, b = CHUNKS[c]
                    if c == 0:
                        need(pe, s_hT, (t + 1) * 2)
                    if known(t) and t == 0:
                        pe.wait_ge(s_wlo, c + 1)
                    if c >= 2:
                        need(pe, (s_evA, s_evD)[c % 2], t * 3 + c // 2)
                    else:
                        need(pe, (s_evA, s_evD)[c % 2], t * 3)
                    o = bank[c % 2][:, 0:b - a]
                    n = 0
                    for k in range(KT):
                        for l, r in ((0, wh), (0, wl), (1, wh)):
                            last = pe.matmul(o, hT[u][:, l, k, :], r[:, k, a:b], start=n == 0,
                                             stop=n == 3 * KT - 1)
                            n += 1
                    last.then_inc(s_pj, 1)

                def qk_turn(t, b, pr):
                    need(pe, s_rp, t * 2)
                    need(pe, s_k2, b)
                    for j in range(GRP):
                        last = pe.transpose(bank[4][:, j * P:(j + 1) * P], pr[:, j * P:(j + 1) * P], ident[:, :])
                    last.then_inc(s_t1, 1)
                    need(pe, s_og, b)
                    pe.transpose(bank[5][:, 0:P], pr[:, KC:KC + P], ident[:, :])
                    pe.transpose(bank[5][0:RANK, P:2 * P], pr[:, ALC:NA], ident[:, :]).then_inc(s_t1, 1)
                    need(pe, s_st, b * 4)
                    for j in range(4):
                        last = pe.transpose(bank[6][:, j * P:(j + 1) * P], pr[:, QBC + j * P:QBC + (j + 1) * P],
                                            ident[:, :])
                    last.then_inc(s_t1, 1)

                def logits(t, b):
                    need(pe, s_kT, t * 2)
                    if has_front(t):
                        need(pe, s_hT, (t + 1) * 2)
                    else:
                        need(pe, s_oT, (t - 2) * 2)
                    for p in range(2):
                        last = pe.matmul(bank[2][:, p * P:(p + 1) * P], wal[:, p * P:(p + 1) * P], aT[:, :],
                                         start=True, stop=True)
                    last.then_inc(s_z, 1)

                def scores(t, b, u):
                    need(pe, s_qT, t)
                    need(pe, s_gT, t)
                    need(pe, s_br, b * 2)
                    for g in range(KVH):
                        rows = slice(g * HD, (g + 1) * HD)
                        for bk, keys in (((4, 6)[g], kT[1 - u]), ((5, 7)[g], kT[u])):
                            for j in range(GRP):
                                last = pe.matmul(bank[bk][:, j * P:(j + 1) * P], qT[rows, j, :], keys[rows, :],
                                                 start=True, stop=True)
                            last.then_inc(s_sc, 1)

                def scores0(t):
                    need(pe, s_qT, t)
                    need(pe, s_gT, t)
                    for g in range(KVH):
                        rows = slice(g * HD, (g + 1) * HD)
                        for j in range(GRP):
                            last = pe.matmul(bank[(4, 6)[g]][:, j * P:(j + 1) * P], qT[rows, j, :],
                                             kT[0][rows, :], start=True, stop=True)
                        last.then_inc(s_sc, 2)

                def probs_turn(t, b):
                    for g in range(KVH):
                        need(pe, s_ex, b * 8 + 4 * g + 4)
                        for j in range(GRP):
                            last = pe.transpose(bank[(4, 6)[g]][:, j * P:(j + 1) * P], scs[:, g * GRP + j, :],
                                                ident[:, :])
                        last.then_inc(s_pt, 1)

                def gla_scores(t, b):
                    need(pe, s_gq, t * 8)
                    if not (known(t) and b == 0):
                        need(pe, s_pv0, t * 2 - 1)
                    for p in range(2):
                        o = bank[5][:, p * 256:(p + 1) * 256]
                        pe.matmul(o, k1[:, p, :], q1[:, p, :, :].rearrange("p h t -> p (h t)"),
                                  start=True, stop=True)
                        o = o.rearrange("p (h t) -> p h t", h=2)[0:CH, :, CH:P]
                        last = pe.matmul(o, k5[:, p, :], q5[:, p, :, :], start=True, stop=True)
                    last.then_inc(s_at, 1)

                def values(t, b, u):
                    need(pe, s_ptm, t * 4)
                    need(pe, s_vb, t)
                    if not (known(t) and b == 0):
                        need(pe, s_pv0, t * 2)
                    for hd in range(HEADS):
                        g = hd // GRP
                        o = bank[7][:, hd * HD:(hd + 1) * HD]
                        first = known(t) and b == 0
                        last = pe.matmul(o, ptc[:, hd, :], vbuf[1 - u][:, g * HD:(g + 1) * HD], start=True,
                                         stop=first)
                        if not first:
                            last = pe.matmul(o, ptp[:, hd, :], vbuf[u][:, g * HD:(g + 1) * HD], start=False,
                                             stop=True)
                    last.then_inc(s_pvo, 1)
                    for p in range(2):
                        last = pe.transpose(bank[4][:, p * P:(p + 1) * P], k4[:, p, :], ident[:, :])
                    last.then_inc(s_kt, 1)

                def gla_out(t, b, pr):
                    need(pe, s_am, t)
                    need(pe, s_st, b * 4)
                    v = pr[:, VBC:VBC + BH * BV]
                    for p in range(2):
                        pe.matmul(bank[5][:, p * 256:(p + 1) * 256], q3[:, p, :],
                                  state[:, p].rearrange("p h v -> p (h v)"), start=p == 0, stop=False,
                                  skip_group_check=True)
                    for hd in range(BH):
                        last = pe.matmul(bank[5][:, hd * BV:(hd + 1) * BV], att[:, hd, :],
                                         v[:, hd * BV:(hd + 1) * BV], start=False, stop=hd == BH - 1,
                                         skip_group_check=True)
                    last.then_inc(s_go, 1)
                    need(pe, s_k2, t)
                    for p in range(2):
                        last = pe.matmul(bank[6][:, p * 256:(p + 1) * 256], k2[:, p, :],
                                         v[:, p * 256:(p + 1) * 256], start=True, stop=True)
                    last.then_inc(s_inc, 1)

                pe.wait_ge(s_msk, 5)
                turn16(x16, s_x16, 2).then_inc(s_xtr, 1)

                def step(t, h, u):
                    b, pr = t - 1, proj[1 - u]
                    front, back = has_front(t), has_back(t)
                    if front:
                        chunk(t, u, 0)
                    if back:
                        if known(t) and b == 0:
                            pe.wait_ge(s_const, 16 * 6)
                            pe.wait_ge(s_zero, 7)
                        qk_turn(t, b, pr)
                    if front:
                        chunk(t, u, 1)
                    if back:
                        logits(t, b)
                        if known(t) and b == 0:
                            scores0(t)
                        else:
                            scores(t, b, u)
                    if front:
                        chunk(t, u, 2)
                    if has_turn(t):
                        need(pe, s_zs, min(t, NBLK) * 2 if known(t) else t * 2)
                        need(pe, s_oT, (t - 2) * 2)
                        turn16(o16, s_o16, (t - 1) * 4).then_inc(s_otr, 1)
                    if front:
                        chunk(t, u, 3)
                    if back:
                        probs_turn(t, b)
                        gla_scores(t, b)
                    if front:
                        chunk(t, u, 4)
                    if back:
                        values(t, b, u)
                    if has_xprep(t):
                        if has_turn(t):
                            need(pe, s_oT, (t - 1) * 2)
                        elif back:
                            need(pe, s_zs, t * 2)
                        else:
                            need(pe, s_hT, 2)
                        turn16(x16, s_x16, (t + 2) * 2).then_inc(s_xtr, 1)
                    if front:
                        chunk(t, u, 5)
                    if back:
                        gla_out(t, b, pr)

                steps(pe, step)

            @block.vector
            def _(dve):
                count = [0]

                def link(ins):
                    ins.then_inc(s_rope, 1)
                    count[0] += 1
                    dve.wait_ge(s_rope, count[0])

                inv_freq = np.exp(np.float32(-np.log(THETA)) * np.arange(HALF, dtype=np.float32)
                                  * np.float32(1.0 / HALF)).astype(np.float32)
                dve.wait_ge(s_const, 16 * 6)
                link(dve.tensor_copy(pos_f, pos_i))
                a3 = ang.rearrange("p (n i) -> p n i", i=HALF)
                for i in range(HALF):
                    ins = dve.tensor_scalar(a3[:, :, i], pos_f, float(inv_freq[i]), None, ALU.mult)
                link(ins)
                turn = [brn[:, 256 * i:256 * (i + 1)] for i in range(1, 4)]
                c1, c2, c3 = two_pi_parts()
                n2, n1, n0 = turn
                ops = count[0]
                for _ in range(2):
                    link(dve.tensor_scalar(n0, ang, float(1 / (2 * np.pi)), None, ALU.mult))
                    link(dve.tensor_scalar(n2, n0, 2.0 ** -22, MAGIC, ALU.mult, ALU.add))
                    link(dve.tensor_scalar(n2, n2, MAGIC, None, ALU.subtract))
                    link(dve.scalar_tensor_tensor(n0, n2, -2.0 ** 22, n0, ALU.mult, ALU.add))
                    link(dve.tensor_scalar(n1, n0, 2.0 ** -11, MAGIC, ALU.mult, ALU.add))
                    link(dve.tensor_scalar(n1, n1, MAGIC, None, ALU.subtract))
                    link(dve.scalar_tensor_tensor(n0, n1, -2.0 ** 11, n0, ALU.mult, ALU.add))
                    link(dve.tensor_scalar(n0, n0, MAGIC, None, ALU.add))
                    link(dve.tensor_scalar(n0, n0, MAGIC, None, ALU.subtract))
                    for c in (c1, c2, c3):
                        for n, w in ((n2, 2.0 ** 22), (n1, 2.0 ** 11), (n0, 1.0)):
                            link(dve.scalar_tensor_tensor(ang, n, -w * c, ang, ALU.mult, ALU.add))
                assert count[0] - ops == 2 * ROPE_OPS
                pi = float(np.nextafter(np.float32(np.pi), np.float32(0)))
                link(dve.tensor_scalar(ang, ang, pi, -pi, ALU.min, ALU.max))
                link(dve.scalar_tensor_tensor(n2, ang, -1.0, ang, ALU.mult, ALU.max))
                link(dve.tensor_scalar(n2, n2, -1.0, float(np.pi / 2), ALU.mult, ALU.add))

                def x_start(n):
                    rsqrt_start(dve, s_xss, n + 1, s_xv, ss[:, :], var[:, :], D)

                def x_split(n, u):
                    rsqrt_newton(dve, s_xt, n * 2, s_xn, n * 4, var[:, :], y0[:, :], nt[:, 0:1], rstd[:, :])
                    need(dve, s_xn, n * 4 + 4)
                    need(dve, s_xtr, n)
                    dve.tensor_scalar(x16[:, 0], xin[u][:, :], rstd[:, 0:1], None, ALU.mult).then_inc(s_x16, 1)
                    need(dve, s_x16, n * 2 + 1)
                    dve.scalar_tensor_tensor(x16[:, 1], xin[u][:, :], rstd[:, 0:1], x16[:, 0], ALU.mult,
                                             ALU.subtract).then_inc(s_x16, 1)

                def evac(t, u, c):
                    a, b = CHUNKS[c]
                    dve.wait_ge(s_pj, t * NCH + (c + 1))
                    if c == 1:
                        need(dve, s_inc, t - 1)
                        need(dve, s_gat, t - 1)
                    dve.tensor_scalar(proj[u][:, a:b], bank[1][:, 0:b - a], wscale[:, c:c + 1], None,
                                      ALU.mult).then_inc(s_evD, 1)

                dve.memset(tick[:, :], 0.0)
                x_start(0)
                x_split(0, 0)
                prep.on_vector(dve)

                def wait_carrier():
                    dve.tensor_copy(tick[:, 0:1], tick[:, 1:2])

                def softmax_shift(t, b, first):
                    for g in range(KVH):
                        hs = slice(g * GRP, (g + 1) * GRP)
                        if first:
                            dve.memset(scs[:, hs, :], NEG).then_inc(s_pv0, 1)
                        need(dve, s_pv0, t * 2 - 1 + g)
                        need(dve, s_sc, b * 4 + 1 + 2 * g)
                        wait_carrier()
                        dve.copy_predicated(scs[:, hs, :],
                                            tri[:, :].bitcast(U32).unsqueeze(1).broadcast_to([P, GRP, P]),
                                            bank[(4, 6)[g]][:, :].rearrange("p (h k) -> p h k", h=GRP)
                                            ).then_inc(s_sel, 1)
                        need(dve, s_sel, b * 2 + 1 + g)
                        dve.tensor_reduce(mx[:, hs], scs[:, hs, :], AX.X, ALU.max).then_inc(s_mx, 1)
                    need(dve, s_mx, t * 2)
                    dve.scalar_tensor_tensor(mm[:, :], mx[:, :], HD ** -0.5, sinks[:, :], ALU.mult,
                                             ALU.max).then_inc(s_sm, 1)
                    need(dve, s_sm, b * 3 + 1)
                    dve.tensor_scalar(nm[:, :], mm[:, :], -1.0, None, ALU.mult).then_inc(s_sm, 1)
                    dve.tensor_tensor(dsk[:, :], sinks[:, :], mm[:, :], ALU.subtract).then_inc(s_sm, 1)

                def gate_sums(t, b):
                    need(dve, s_spt, b * 2 + 2)
                    dve.scalar_tensor_tensor(gsp, sp_, -1.0, zs, ALU.mult, ALU.min).then_inc(s_sp, 1)
                    need(dve, s_sp, t)
                    dve.tensor_tensor_scan(cum[:, :, :, :].rearrange("p a b c -> p (a b c)"),
                                           seg[:, :, :].rearrange("p a c -> p (a c)"), gsp, 0.0,
                                           ALU.mult, ALU.add).then_inc(s_cum, 1)
                    need(dve, s_cum, t)
                    c4 = cum[:, :, :, :].rearrange("p a b c -> p (a b) c")
                    dve.tensor_copy(carry[:, :, 1:2], cum[:, :, 0, CH - 1:CH]).then_inc(s_car, 1)
                    dve.tensor_tensor(d1.rearrange("p (a c) -> p a c", a=4), c4,
                                      c4[:, :, CH // 2 - 1:CH // 2].broadcast_to([P, 4, CH]),
                                      ALU.subtract).then_inc(s_dif, 1)
                    dve.tensor_tensor(d5.rearrange("p (a c) -> p a c", a=2), cum[:, :, 0, :],
                                      cum[:, :, 0, CH - 1:CH].broadcast_to([P, 2, CH]),
                                      ALU.subtract).then_inc(s_dif, 1)
                    need(dve, s_car, t)
                    dve.tensor_tensor(d3.rearrange("p (a c) -> p a c", a=4), c4,
                                      carry[:, :, :].rearrange("p a b -> p (a b)").unsqueeze(2)
                                      .broadcast_to([P, 4, CH]), ALU.add).then_inc(s_dif, 1)
                    need(dve, s_dif, b * 4 + 3)
                    d3v = d3.rearrange("p (a c) -> p a c", a=2)
                    dve.tensor_tensor(d4.rearrange("p (a c) -> p a c", a=2), d3v,
                                      d3v[:, :, P - 1:P].broadcast_to([P, 2, P]),
                                      ALU.subtract).then_inc(s_dif, 1)

                def gla_factors(t, b):
                    need(dve, s_gT, t)
                    need(dve, s_e, t * 6)
                    need(dve, s_inc, b)
                    v = lambda e: e.rearrange("p (a c) -> p a c", a=2)
                    sc = BK ** -0.5
                    for hh in range(2):
                        r = slice(hh * BK, (hh + 1) * BK)
                        dve.scalar_tensor_tensor(q1[r, :, hh, :], gT[r, 0:2, :], sc, v(e1)[r], ALU.mult,
                                                 ALU.mult).then_inc(s_gq, 1)
                        dve.scalar_tensor_tensor(q5[r, :, hh, :], gT[r, 0:2, CH:P], sc, v(e5q)[r], ALU.mult,
                                                 ALU.mult).then_inc(s_gq, 1)
                    dve.scalar_tensor_tensor(q3[:, :, :], gT[:, 0:2, :], sc, v(e3), ALU.mult,
                                             ALU.mult).then_inc(s_gq, 1)
                    dve.tensor_tensor(k1[:, :, :], gT[:, 2:4, :], v(e2), ALU.mult).then_inc(s_gq, 1)
                    dve.tensor_tensor(k4[:, :, :], gT[:, 2:4, :], v(e4), ALU.mult).then_inc(s_gq, 1)
                    dve.tensor_tensor(k5[:, :, :], gT[:, 2:4, 0:CH], v(e5k), ALU.mult).then_inc(s_gq, 1)

                def probs_mask(t, b):
                    need(dve, s_pvo, b)
                    for g in range(KVH):
                        hs = slice(g * GRP, (g + 1) * GRP)
                        need(dve, s_pt, b * 2 + 1 + g)
                        src = bank[(4, 6)[g]][:, :].rearrange("p (h k) -> p h k", h=GRP)
                        for dst, m in ((ptc, triT), (ptp, triN)):
                            dve.tensor_tensor(dst[:, hs, :], src, m[:, :].unsqueeze(1).broadcast_to([P, GRP, P]),
                                              ALU.mult).then_inc(s_ptm, 1)

                def step(t, h, u):
                    b, pr = t - 1, proj[1 - u]
                    front, back = has_front(t), has_back(t)
                    first = known(t) and b == 0
                    if has_xprep(t):
                        x_start(t + 1)
                    if back:
                        if first:
                            dve.wait_ge(s_zero, 7)
                            dve.wait_ge(s_msk, 5)
                        dve.wait_ge(s_evA, t * 3)
                        dve.wait_ge(s_evD, t * 3)
                        need(dve, s_gat, b)
                        for n, c in enumerate((ZAC, ZBC)):
                            dve.tensor_scalar(sil[:, n * 512:(n + 1) * 512], pr[:, c:c + 512], -1.0, BIG_ARG,
                                              ALU.mult, ALU.min).then_inc(s_slm, 1)
                        need(dve, s_t1, b * 3 + 2)
                        dve.tensor_copy(aT[:, :], bank[5][0:RANK, P:2 * P]).then_inc(s_kT, 1)
                        dve.tensor_copy(kT[1 - u][:, :], bank[5][:, 0:P]).then_inc(s_kT, 1)
                        need(dve, s_slt, b * 2 + 2)
                        for n, c in enumerate((ZAC, ZBC)):
                            dve.scalar_tensor_tensor(sil[:, n * 512:(n + 1) * 512], pr[:, c:c + 512], -1.0,
                                                     sil[:, n * 512:(n + 1) * 512], ALU.mult,
                                                     ALU.max).then_inc(s_sll, 1)
                    if front:
                        evac(t, u, 1)
                    if has_xprep(t):
                        x_split(t + 1, 1 - u)
                    if back:
                        need(dve, s_z, t)
                        for p in range(2):
                            dve.tensor_scalar(zs[:, p * P:(p + 1) * P], bank[2][:, p * P:(p + 1) * P],
                                              bal[:, p:p + 1], None, ALU.add).then_inc(s_zs, 1)
                        need(dve, s_zs, t * 2)
                        dve.tensor_scalar(sp_, zs, -1.0, BIG_ARG, ALU.mult, ALU.min).then_inc(s_spm, 1)
                        softmax_shift(t, b, first)
                        gate_sums(t, b)
                        gla_factors(t, b)
                        need(dve, s_es, t)
                        need(dve, s_ex, t * 8)
                        dve.tensor_tensor(den[:, :], rsum[:, :], es[:, :], ALU.add).then_inc(s_den, 1)
                        need(dve, s_den, b * 2 + 1)
                        dve.reciprocal(rden[:, :], den[:, :]).then_inc(s_den, 1)
                        probs_mask(t, b)
                        need(dve, s_at, t)
                        wait_carrier()
                        dve.copy_predicated(att[:, :, :],
                                            triT[:, :].bitcast(U32).unsqueeze(1).broadcast_to([P, BH, P]),
                                            bank[5][:, :].rearrange("p (h t) -> p h t", h=BH)).then_inc(s_am, 1)
                    if front:
                        evac(t, u, 3)
                    if back:
                        need(dve, s_pvo, t)
                        need(dve, s_den, t * 2)
                        dve.tensor_tensor(brn[:, 0:512].rearrange("p (h d) -> p h d", h=HEADS),
                                          bank[7][:, :].rearrange("p (h d) -> p h d", h=HEADS),
                                          rden[:, :].unsqueeze(2).broadcast_to([P, HEADS, HD]),
                                          ALU.mult).then_inc(s_br, 1)
                    if front:
                        evac(t, u, 5)
                    if back:
                        need(dve, s_inc, t)
                        for p in range(2):
                            for hh in range(2):
                                r = slice(hh * BK, (hh + 1) * BK)
                                dve.scalar_tensor_tensor(
                                    state[r, p, hh, :], state[r, p, hh, :],
                                    e3[r, p * P + P - 1:p * P + P],
                                    bank[6][r, p * 256 + hh * BV:p * 256 + (hh + 1) * BV],
                                    ALU.mult, ALU.add).then_inc(s_st, 1)
                        rsqrt_start(dve, s_gss, t * 4, s_gv, ss4[:, :], var4[:, :], BV)
                        rsqrt_newton(dve, s_gt, b * 2, s_gn, b * 4, var4[:, :], y4[:, :], nt4[:, :], r4[:, :])
                        need(dve, s_gn, t * 4)
                        dve.tensor_tensor(brn[:, 512:].rearrange("p (h d) -> p h d", h=BH), og[:, :, :],
                                          r4[:, :].unsqueeze(2).broadcast_to([P, BH, BV]),
                                          ALU.mult).then_inc(s_br, 1)
                        need(dve, s_br, t * 2)
                        need(dve, s_sl, t * 2)
                        dve.tensor_tensor(brn, brn, sil, ALU.mult).then_inc(s_gat, 1)
                        need(dve, s_gat, t)
                        b2 = brn.rearrange("p (a n) -> p a n", a=2)
                        osc = oscale[:, bass.ds(b, 1), :].rearrange("p a b -> p (a b)")
                        dve.tensor_reduce(omax[:, :], b2, AX.X, ALU.max, apply_absolute_value=True
                                          ).then_inc(s_om, 1)
                        need(dve, s_om, b * 5 + 1)
                        dve.tensor_scalar(omax[:, :], omax[:, :], 1e-30, None, ALU.max).then_inc(s_om, 1)
                        need(dve, s_om, b * 5 + 2)
                        dve.tensor_scalar(omax[:, :].bitcast(U32), omax[:, :].bitcast(U32), 0x7F800000, None,
                                          ALU.bitwise_and).then_inc(s_om, 1)
                        need(dve, s_om, b * 5 + 3)
                        dve.tensor_scalar(opow[:, :], omax[:, :], 2.0 ** -10, None, ALU.mult).then_inc(s_om, 1)
                        need(dve, s_om, b * 5 + 4)
                        dve.tensor_copy(osc, opow[:, :])
                        dve.reciprocal(oinv[:, :], opow[:, :]).then_inc(s_om, 1)
                        need(dve, s_om, t * 5)
                        need(dve, s_otr, b)
                        for a in range(2):
                            dve.tensor_scalar(o16[:, 0, a * 512:(a + 1) * 512], b2[:, a], oinv[:, a:a + 1],
                                              None, ALU.mult).then_inc(s_o16, 1)
                        need(dve, s_o16, b * 4 + 2)
                        for a in range(2):
                            dve.scalar_tensor_tensor(o16[:, 1, a * 512:(a + 1) * 512], b2[:, a],
                                                     oinv[:, a:a + 1], o16[:, 0, a * 512:(a + 1) * 512],
                                                     ALU.mult, ALU.subtract).then_inc(s_o16, 1)

                steps(dve, step)

        with ExitStack() as bctx:
            def sc_(name, shape, dt=F32):
                return sb(name, shape, dt, bctx)

            gh = sc_("gh", [P, 2, KT, 2 * D], F16)
            wa = sc_("wa", [P, 2, 2, BH, D], F16)
            wo = sc_("wo", [P, 2, KT, D], F16)
            barena = sc_("barena", [P, 2, 4096])
            sg = [[barena[:, 0, (2 * j + a) * 512:(2 * j + a + 1) * 512] for a in range(2)] for j in range(2)]
            ta = barena[:, 0, 2048:2560]
            tb = barena[:, 0, 2560:3072]
            gfin = barena[:, 0, 3072:4096]
            mg = barena[:, 1, 0:1024]
            res = barena[:, 1, 1024:2048]
            fin = [barena[:, 1, 2048:3072], barena[:, 1, 3072:4096]]
            hb = [sc_(f"hb{i}", [P, 2, KT, P], F16) for i in range(2)]
            ob = [sc_(f"ob{i}", [P, 2, KT, P], F16) for i in range(2)]
            xb = [sc_(f"xb{i}", [P, D]) for i in range(2)]
            m16 = sc_("m16", [P, 2, D], F16)
            mT = sc_("mT", [P, 2, KT, P], F16)
            junkb = sc_("junkb", [P, D], F16)
            ysc = sc_("ysc", [P, 2])
            mmax = sc_("mmax", [P, 1])
            msc = sc_("msc", [P, 1])
            minv = sc_("minv", [P, 1])
            rsc = sc_("rsc", [P, 2])

            s_hb = [sem("hb_even"), sem("hb_odd")]
            s_ob = [sem("ob_even"), sem("ob_odd")]
            s_xb = [sem("xb_even"), sem("xb_odd")]
            s_gf = sem("gfin_loaded")
            s_ng = sem("gate_scales_negated")
            s_g = sem("gates")
            s_gm = sem("gates_clamped")
            s_gx = sem("gate_tables")
            s_gl = sem("gates_softplus")
            s_sg = sem("gates_sigmoid")
            s_y = sem("branch_products")
            s_ys = sem("branch_scales")
            s_yt = sem("branches_merging")
            s_mg = sem("merged")
            s_ms = sem("merged_scales")
            s_m16 = sem("merged_split")
            s_mt = sem("merged_transposed")
            s_mT = sem("mT_copied")
            s_rs = sem("out_scales")
            s_w = sem("out_products")
            s_r = sem("residual_added")
            s_fss = sem("final_square_sum")
            s_fv = sem("final_var")
            s_ft = sem("final_rsqrt_table")
            s_fn = sem("final_rsqrt_newton")
            s_fin = sem("finished")
            s_out = [sem("stored_even"), sem("stored_odd")]

            def dest_b(n):
                if n < OUTA:
                    a = (n - GATE0) * 512
                    return gh[:, 0, :, a:a + 512], gh[:, 1, :, a:a + 512]
                if n < WO0:
                    return wa[:, n - OUTA, 0], wa[:, n - OUTA, 1]
                a = (n - WO0) * 512
                return wo[:, 0, :, a:a + 512], wo[:, 1, :, a:a + 512]

            prepb = Prep(GATE0, NW, [barena[:, 0, :], barena[:, 1, :]], dest_b)

            def stepsb(eng, step):
                for t in range(3):
                    step(t, t // 2, t % 2)
                with eng.Fori(0, (NBLK - 4) // 2) as i:
                    step(i * 2 + 3, i + 1, 1)
                    step(i * 2 + 4, i + 2, 0)
                step(NBLK - 1, NBLK // 2 - 1, 1)
                step(NBLK, NBLK // 2, 0)

            def frontb(t):
                return not isinstance(t, int) or t < NBLK

            def tailb(t):
                return not isinstance(t, int) or t >= 1

            block = bctx.enter_context(nc.Block())

            @block.sync
            def _(sp):
                prepb.on_sync(sp)
                sp.wait_ge(s_wlo, NW)
                sp.dma_start(gfin, g_final.partition_broadcast(P)).then_inc(s_gf, 16)

                def load(t, h, u):
                    need(sp, s_y, (t - 1) * 4)
                    sp.dma_start(hb[u][:, :, :, :].rearrange("p a k t -> p (a k t)"),
                                 hts[bass.ds(t, 1)].rearrange("a p n -> (a p) n")).then_inc(s_hb[u], 16)
                    sp.dma_start(ob[u][:, :, :, :].rearrange("p a k t -> p (a k t)"),
                                 ots[bass.ds(t, 1)].rearrange("a p n -> (a p) n")).then_inc(s_ob[u], 16)
                    need(sp, s_r, (t - 1) * 2)
                    sp.dma_start(xb[u][:, :], x[bass.ds(t * P, P), :]).then_inc(s_xb[u], 16)

                load(0, 0, 0)

                def step(t, h, u):
                    if not isinstance(t, int) or t + 1 < NBLK:
                        load(t + 1, h + u, 1 - u)
                    if tailb(t):
                        need(sp, s_fin, t)
                        sp.dma_start(out[bass.ds((t - 1) * P, P), :], fin[1 - u]).then_inc(s_out[1 - u], 16)

                stepsb(sp, step)
                for s in s_out:
                    sp.wait_ge(s, 16 * (NBLK // 2))

            @block.gpsimd
            def _(pool):
                prepb.on_gpsimd(pool)

                def step(t, h, u):
                    if frontb(t):
                        for j in range(2):
                            need(pool, s_yt, t * 4 + 2 * j + 2)
                            need(pool, s_m16, t * 2)
                            pool.tensor_tensor(mg[:, j * 512:(j + 1) * 512], ta, tb, ALU.add).then_inc(s_mg, 1)

                stepsb(pool, step)

            @block.scalar
            def _(act):
                act.preload_act_table_set("natural_log_exp_and_others")
                prepb.on_scalar(act)

                def sigmoids(t, j):
                    for a in range(2):
                        n = 2 * j + a
                        need(act, s_gm, t * 4 + n + 1)
                        act.activation(sg[j][a], sg[j][a], ACT.Exp).then_inc(s_gx, 1)
                        need(act, s_gx, t * 8 + 2 * n + 1)
                        act.activation(sg[j][a], sg[j][a], ACT.Ln, bias=1.0).then_inc(s_gx, 1)
                    for a in range(2):
                        need(act, s_gl, t * 4 + 2 * j + a + 1)
                        act.activation(sg[j][a], sg[j][a], ACT.Exp, scale=-1.0).then_inc(s_sg, 1)

                def step(t, h, u):
                    if frontb(t):
                        sigmoids(t, 0)
                    if tailb(t):
                        need(act, s_mt, t)
                        need(act, s_w, (t - 1) * 2)
                        for a in range(2):
                            act.activation(mT[:, a].rearrange("p k t -> p (k t)"),
                                           bank[4 + a][:, :].bitcast(F16), ACT.Copy).then_inc(s_mT, 1)
                    if frontb(t):
                        sigmoids(t, 1)
                    if tailb(t):
                        need(act, s_r, t * 2)
                        act.activation(junkb[:, :], res, ACT.Square, accum_out=ss[:, :]).then_inc(s_fss, 1)
                        rsqrt_table(act, s_fv, t, s_ft, (t - 1) * 2, var[:, :], lnv[:, :], y0[:, :])

                stepsb(act, step)

            @block.tensor
            def _(pe):
                pe.wait_ge(s_wlo, NW)

                def gate(t, u, j, a):
                    n = 2 * j + a
                    need(pe, s_gl, t * 4 + n - 1 if n >= 2 else (t - 1) * 4 + n + 3)
                    col = a * D + j * 512
                    for i in range(3 * KT):
                        k, s = divmod(i, 3)
                        l, r = ((0, 0), (0, 1), (1, 0))[s]
                        last = pe.matmul(bank[a][:, :], hb[u][:, l, k, :], gh[:, r, k, col:col + 512],
                                         start=i == 0, stop=i == 3 * KT - 1)
                    last.then_inc(s_g, 1)

                def branch(t, u, j, a):
                    n = 2 * j + a
                    need(pe, s_yt, t * 4 + n - 1 if n >= 2 else (t - 1) * 4 + n + 3)
                    for i in range(3 * BH):
                        k, s = divmod(i, 3)
                        l, r = ((0, 0), (0, 1), (1, 0))[s]
                        last = pe.matmul(bank[2 + a][:, :], ob[u][:, l, a * BH + k, :],
                                         wa[:, a, r, k, j * 512:(j + 1) * 512], start=i == 0,
                                         stop=i == 3 * BH - 1)
                    last.then_inc(s_y, 1)

                def merged_turn(t):
                    need(pe, s_m16, t * 2)
                    need(pe, s_mT, (t - 1) * 2)
                    for a in range(2):
                        dst = bank[4 + a][:, :].bitcast(F16)
                        for k in range(KT):
                            last = pe.transpose(dst[:, k * P:(k + 1) * P], m16[:, a, k * P:(k + 1) * P],
                                                ident16[:, :])
                    last.then_inc(s_mt, 1)

                def final(t, j):
                    need(pe, s_mT, t * 2)
                    need(pe, s_r, (t - 1) * 2)
                    for i in range(3 * KT):
                        k, s = divmod(i, 3)
                        l, r = ((0, 0), (0, 1), (1, 0))[s]
                        last = pe.matmul(bank[6 + j][:, :], mT[:, l, k, :], wo[:, r, k, j * 512:(j + 1) * 512],
                                         start=i == 0, stop=i == 3 * KT - 1)
                    last.then_inc(s_w, 1)

                def step(t, h, u):
                    if frontb(t):
                        need(pe, s_hb[u], 16 * h + 16)
                        gate(t, u, 0, 0)
                        gate(t, u, 0, 1)
                    if tailb(t):
                        merged_turn(t)
                    if frontb(t):
                        need(pe, s_ob[u], 16 * h + 16)
                        branch(t, u, 0, 0)
                        branch(t, u, 0, 1)
                    if tailb(t):
                        final(t, 0)
                        final(t, 1)
                    if frontb(t):
                        for a in range(2):
                            gate(t, u, 1, a)
                        for a in range(2):
                            branch(t, u, 1, a)

                stepsb(pe, step)

            @block.vector
            def _(dve):
                prepb.on_vector(dve)
                dve.wait_ge(s_wsm, 4 * NW)
                dve.tensor_scalar(wpow[:, GATE0:GATE0 + 4], wscale[:, GATE0:GATE0 + 4], -1.0, None,
                                  ALU.mult).then_inc(s_ng, 1)
                dve.wait_ge(s_ng, 1)
                dve.wait_ge(s_gf, 16)

                def softplus_gates(t, j):
                    for a in range(2):
                        n = 2 * j + a
                        need(dve, s_g, t * 4 + n + 1)
                        need(dve, s_yt, (t - 1) * 4 + n + 1)
                        ng = wpow[:, GATE0 + 2 * a + j:GATE0 + 2 * a + j + 1]
                        dve.tensor_scalar(sg[j][a], bank[a][:, :], ng, BIG_ARG, ALU.mult,
                                          ALU.min).then_inc(s_gm, 1)
                    for a in range(2):
                        n = 2 * j + a
                        ng = wpow[:, GATE0 + 2 * a + j:GATE0 + 2 * a + j + 1]
                        need(dve, s_gx, t * 8 + 2 * n + 2)
                        dve.scalar_tensor_tensor(sg[j][a], bank[a][:, :], ng, sg[j][a], ALU.mult,
                                                 ALU.max).then_inc(s_gl, 1)

                def merge(t, j):
                    for a, o in ((0, ta), (1, tb)):
                        n = 2 * j + a
                        need(dve, s_y, t * 4 + n + 1)
                        need(dve, s_sg, t * 4 + n + 1)
                        need(dve, s_mg, t * 2 + j)
                        dve.scalar_tensor_tensor(o, bank[2 + a][:, :], ysc[:, a:a + 1], sg[j][a], ALU.mult,
                                                 ALU.mult).then_inc(s_yt, 1)

                def step(t, h, u):
                    front, tail = frontb(t), tailb(t)
                    if front:
                        softplus_gates(t, 0)
                        dve.tensor_tensor(ysc[:, :], oscale[:, bass.ds(t, 1), :].rearrange("p a b -> p (a b)"),
                                          wscale[:, OUTA:OUTB + 1], ALU.mult).then_inc(s_ys, 1)
                        need(dve, s_ys, t + 1)
                        merge(t, 0)
                    if tail:
                        dve.tensor_scalar(rsc[:, :], wscale[:, WO0:WO0 + 2], msc[:, 0:1], None,
                                          ALU.mult).then_inc(s_rs, 1)
                        need(dve, s_rs, t)
                        need(dve, s_xb[1 - u], 16 * (h + u))
                        need(dve, s_fn, (t - 1) * 4)
                        need(dve, s_fin, t - 1)
                        for j in range(2):
                            need(dve, s_w, (t - 1) * 2 + j + 1)
                            dve.scalar_tensor_tensor(res[:, j * 512:(j + 1) * 512], bank[6 + j][:, :],
                                                     rsc[:, j:j + 1], xb[1 - u][:, j * 512:(j + 1) * 512],
                                                     ALU.mult, ALU.add).then_inc(s_r, 1)
                    if front:
                        softplus_gates(t, 1)
                        merge(t, 1)
                        need(dve, s_mg, t * 2 + 2)
                        dve.tensor_reduce(mmax[:, :], mg, AX.X, ALU.max, apply_absolute_value=True
                                          ).then_inc(s_ms, 1)
                        need(dve, s_ms, t * 5 + 1)
                        dve.tensor_scalar(mmax[:, :], mmax[:, :], 1e-30, None, ALU.max).then_inc(s_ms, 1)
                        need(dve, s_ms, t * 5 + 2)
                        dve.tensor_scalar(mmax[:, :].bitcast(U32), mmax[:, :].bitcast(U32), 0x7F800000, None,
                                          ALU.bitwise_and).then_inc(s_ms, 1)
                        need(dve, s_ms, t * 5 + 3)
                        dve.tensor_scalar(msc[:, :], mmax[:, :], 2.0 ** -10, None, ALU.mult).then_inc(s_ms, 1)
                        need(dve, s_ms, t * 5 + 4)
                        dve.reciprocal(minv[:, :], msc[:, :]).then_inc(s_ms, 1)
                        need(dve, s_ms, t * 5 + 5)
                        need(dve, s_mt, t)
                        dve.tensor_scalar(m16[:, 0], mg, minv[:, 0:1], None, ALU.mult).then_inc(s_m16, 1)
                        need(dve, s_m16, t * 2 + 1)
                        dve.scalar_tensor_tensor(m16[:, 1], mg, minv[:, 0:1], m16[:, 0], ALU.mult,
                                                 ALU.subtract).then_inc(s_m16, 1)
                    if tail:
                        rsqrt_start(dve, s_fss, t, s_fv, ss[:, :], var[:, :], D)
                        rsqrt_newton(dve, s_ft, (t - 1) * 2, s_fn, (t - 1) * 4, var[:, :], y0[:, :],
                                     nt[:, 0:1], rstd[:, :])
                        need(dve, s_fn, t * 4)
                        need(dve, s_out[1 - u], 16 * (h - 1 + u))
                        dve.scalar_tensor_tensor(fin[1 - u], res, rstd[:, 0:1], gfin, ALU.mult,
                                                 ALU.mult).then_inc(s_fin, 1)

                stepsb(dve, step)


_INS = ["x", "positions", "g_in", "w_in", "w_alpha_up", "b_alpha", "attn_sinks", "g_gla_norm",
        "w_out_a", "w_out_b", "w_o", "g_final"]


def kernel(**inputs):
    import numpy as _np
    import concourse.bacc as _bacc
    from concourse import mybir as _mybir
    from concourse.bass_utils import run_bass_kernel_spmd as _run

    nc = _bacc.Bacc("TRN2", target_bir_lowering=False, num_devices=1)
    arrays, args = {}, []
    for name in _INS:
        a = _np.ascontiguousarray(inputs[name])
        a = a if name == "g_final" else a.reshape(a.shape[1:])
        if name in ("positions", "g_in", "g_gla_norm", "b_alpha"):
            a = _np.ascontiguousarray(a.reshape(-1, P).T)
        arrays[f"in_{name}_dram"] = a
        args.append(nc.dram_tensor(f"in_{name}_dram", a.shape, _mybir.dt.from_np(a.dtype),
                                   kind="ExternalInput").ap())
    out = nc.dram_tensor("out_0_dram", (SEQ, D), _mybir.dt.float32, kind="ExternalOutput").ap()
    hybrid_block(nc, *args, out)
    r = _run(nc, [arrays], core_ids=[0])
    return r.results[0]["out_0_dram"].reshape(1, SEQ, D)
```

```python
from contextlib import ExitStack

import numpy as np
import concourse.bass as bass
from concourse import mybir

ALU = mybir.AluOpType
ACT = mybir.ActivationFunctionType
AX = mybir.AxisListType
F32 = mybir.dt.float32
F16 = mybir.dt.float16
I32 = mybir.dt.int32
U32 = mybir.dt.uint32
RADD = bass.bass_isa.ReduceOp.add

P = 128
D = 1024
KT = D // P
SEQ = 4096
NBLK = SEQ // P
HEADS, KVH, HD = 8, 2, 64
GRP = HEADS // KVH
HALF = HD // 8
THETA = 500000.0
BH, BK, BV = 4, 64, 128
RANK = 16
CH = 64
EPS = 1e-6
NEG = -1e30
BIG_ARG = 40.0
MAGIC = 12582912.0
ROPE_OPS = 18

QC, KC, VC, ZAC = 0, 512, 640, 768
QBC, KBC, VBC, ZBC, ALC = 1280, 1536, 1792, 2304, 2816
NA = ALC + RANK
NCONST = 5
CHUNKS = [(c, min(c + 512, NA)) for c in range(0, NA, 512)]
NCH = len(CHUNKS)
GATE_U, OUT_U, WO_U, NU = 0, 2 * KT, 2 * KT + 8, 3 * KT + 8
GA, GB, OA, OB, WO = range(5)
MAT_UNITS = {GA: (0, KT), GB: (KT, KT), OA: (OUT_U, 4), OB: (OUT_U + 4, 4), WO: (WO_U, KT)}
PIECES = ([(m, j, q) for j in range(2) for m, n in ((GA, 2), (GB, 2), (OA, 1), (OB, 1)) for q in range(n)]
          + [(WO, j, q) for j in range(2) for q in range(2)])
PK = 4


def two_pi_parts():
    rest, parts = 2 * np.pi, []
    for _ in range(2):
        e = np.floor(np.log2(rest))
        unit = 2.0 ** (e - 11)
        c = np.floor(rest / unit) * unit
        parts.append(float(c))
        rest -= c
    return parts + [float(np.float32(rest))]


def need(eng, sem, n):
    if isinstance(n, int) and n <= 0:
        return
    eng.wait_ge(sem, n)


def hybrid_block(nc, x, positions, g_in, w_branch, w_units, w_alpha_up, b_alpha, attn_sinks, g_gla_norm,
                 g_final, out):
    with ExitStack() as ctx:
        def sb(name, shape, dt=F32, stack=ctx):
            return stack.enter_context(nc.sbuf_tensor(name, shape, dt))

        def sem(name):
            return ctx.enter_context(nc.semaphore(name))

        bank = [ctx.enter_context(nc.psum_tensor(f"bank{i}", [P, 512], F32)) for i in range(8)]
        hts = nc.dram_tensor("hts", [NBLK, P, 2 * KT * P], F16, kind="Internal").ap()
        ots = nc.dram_tensor("ots", [NBLK, P, 2 * KT * P], F16, kind="Internal").ap()

        ident = sb("ident", [P, P])
        ident16 = sb("ident16", [P, P], F16)
        gain = sb("gain", [P, NU])
        wscale = sb("wscale", [P, NCH])
        usq = sb("usq", [P, NU])
        oscale = sb("oscale", [P, NBLK, 2])
        ss = sb("ss", [P, 1])
        var = sb("var", [P, 1])
        lnv = sb("lnv", [P, 1])
        y0 = sb("y0", [P, 1])
        nt = sb("nt", [P, 2])
        rstd = sb("rstd", [P, 1])

        weights = sb("weights", [P, 2 * KT * NA], F16)
        tiles = sb("tiles", [P, 3, PK * 512])
        usum = sb("usum", [P, 5])
        uall = sb("uall", [P, 5])
        upow = sb("upow", [P, 5])
        uscale = sb("uscale", [P, 5])
        uinv = sb("uinv", [P, 5])
        ngs = sb("ngs", [P, 2])
        ugi = sb("ugi", [P, NU])

        def fp16_parts(ap):
            return ap.bitcast(F16).rearrange("p (a k t) -> p a k t", a=2, k=KT)

        GH, WA, OPER = 2 * KT * 2 * D, 2 * BH * D, 2 * KT * P
        gh = weights[:, 0:GH].rearrange("p (a k n) -> p a k n", a=2, k=KT)
        wa0 = weights[:, GH:GH + WA].rearrange("p (a k n) -> p a k n", a=2, k=BH)
        hb0 = weights[:, GH + WA:GH + WA + OPER].rearrange("p (a k t) -> p a k t", a=2, k=KT)
        ob0 = weights[:, GH + WA + OPER:GH + WA + 2 * OPER].rearrange("p (a k t) -> p a k t", a=2, k=KT)

        s_usq = sem("unit_squares")
        s_pj = sem("projected")
        s_us = sem("unit_sums")
        s_ua = sem("unit_sums_over_rows")
        s_uc = sem("unit_scales")
        s_pr = [sem(f"piece_loaded_{i}") for i in range(3)]
        s_phi = [sem("piece_hi_by_scalar"), sem("piece_hi_by_vector")]
        s_pps = sem("piece_scaled_by_pool")
        s_plo = [sem("piece_lo_by_vector"), sem("piece_lo_by_pool")]
        s_hb = [sem("hb_even"), sem("hb_odd")]
        s_ob = [sem("ob_even"), sem("ob_odd")]

        s_const = sem("const_loaded")
        s_gin = sem("g_in_loaded")
        s_pos = sem("positions_loaded")
        s_id = sem("identities")
        s_msk = sem("masks")
        s_gain = sem("gains")

        def power_of_two(dve, total, pw, scale, inv, s, n):
            dve.tensor_scalar(pw, total, 1e-30, None, ALU.max).then_inc(s, 1)
            dve.wait_ge(s, n + 1)
            dve.tensor_scalar(pw.bitcast(U32), pw.bitcast(U32), 1, 0x7F800000, ALU.logical_shift_right,
                              ALU.bitwise_and).then_inc(s, 1)
            dve.wait_ge(s, n + 2)
            dve.tensor_scalar(scale, pw, 2.0 ** (64 - 14), None, ALU.mult).then_inc(s, 1)
            dve.wait_ge(s, n + 3)
            dve.reciprocal(inv, scale).then_inc(s, 1)

        def rsqrt_start(dve, s_ss, n, s_v, total, v, width):
            need(dve, s_ss, n)
            dve.tensor_scalar(v, total, 1.0 / width, EPS, ALU.mult, ALU.add).then_inc(s_v, 1)

        def rsqrt_table(act, s_v, n, s_t, k, v, ln, y):
            need(act, s_v, n)
            act.activation(ln, v, ACT.Ln).then_inc(s_t, 1)
            need(act, s_t, k + 1)
            act.activation(y, ln, ACT.Exp, scale=-0.5).then_inc(s_t, 1)

        def rsqrt_newton(dve, s_t, k, s_n, m, v, y, t, r):
            need(dve, s_t, k + 2)
            dve.tensor_tensor(t, y, y, ALU.mult).then_inc(s_n, 1)
            need(dve, s_n, m + 1)
            dve.tensor_tensor(t, t, v, ALU.mult).then_inc(s_n, 1)
            need(dve, s_n, m + 2)
            dve.tensor_scalar(t, t, -0.5, 1.5, ALU.mult, ALU.add).then_inc(s_n, 1)
            need(dve, s_n, m + 3)
            dve.tensor_tensor(r, y, t, ALU.mult).then_inc(s_n, 1)

        def raw_piece(i):
            return tiles[:, i % 3, :].rearrange("p (k n) -> p k n", k=PK)

        late = [None, None]

        def piece_parts(i):
            m, j, q = PIECES[i]
            c, ks = slice(j * 512, (j + 1) * 512), slice(q * PK, (q + 1) * PK)
            if m in (GA, GB):
                c = slice(m * D + j * 512, m * D + (j + 1) * 512)
                w = gh
            else:
                w = {OA: wa0, OB: late[0], WO: late[1]}[m]
            return MAT_UNITS[m][0] + q * PK, w[:, 0, ks, c], w[:, 1, ks, c]

        def load_piece(sp, i):
            m, j, q = PIECES[i]
            u0 = MAT_UNITS[m][0] + q * PK
            for s in s_plo:
                need(sp, s, i - 2)
            sp.dma_start(raw_piece(i), w_units[u0:u0 + PK, :, j * 512:(j + 1) * 512]
                         .rearrange("k p n -> p k n")).then_inc(s_pr[i % 3], 16)

        def split_piece(eng, i, hi_ks, lo_ks):
            u0, hi, lo = piece_parts(i)
            eng.wait_ge(s_pr[i % 3], 16 * (i // 3 + 1))
            if i == 0:
                eng.wait_ge(s_uc, 8)
                eng.wait_ge(s_pj, NBLK * NCH)
            for k in hi_ks:
                g = ugi[:, u0 + k:u0 + k + 1]
                if hi_ks is ACT_K:
                    last = eng.activation(hi[:, k], raw_piece(i)[:, k, :], ACT.Copy, scale=g)
                else:
                    last = eng.tensor_scalar(hi[:, k], raw_piece(i)[:, k, :], g, None, ALU.mult)
            if hi_ks:
                last.then_inc(s_phi[0 if hi_ks is ACT_K else 1], 1)
            if lo_ks:
                eng.wait_ge(s_phi[0], i + 1)
                eng.wait_ge(s_phi[1], i + 1)
                for k in lo_ks:
                    last = eng.scalar_tensor_tensor(lo[:, k], raw_piece(i)[:, k, :],
                                                    ugi[:, u0 + k:u0 + k + 1], hi[:, k], ALU.mult,
                                                    ALU.subtract)
                last.then_inc(s_plo[0], 1)

        def split_piece_pool(pool, i):
            u0, hi, lo = piece_parts(i)
            k = PK - 1
            pool.wait_ge(s_phi[1], i + 1)
            pool.tensor_scalar(raw_piece(i)[:, k, :], raw_piece(i)[:, k, :], ugi[:, u0 + k:u0 + k + 1], None,
                               ALU.mult).then_inc(s_pps, 1)
            pool.wait_ge(s_pps, i + 1)
            pool.tensor_tensor(lo[:, k], raw_piece(i)[:, k, :], hi[:, k], ALU.subtract).then_inc(s_plo[1], 1)

        ACT_K, DVE_K = (0, 1), (2, 3)
        NP_ = len(PIECES)
        NPRE = 5

        def unit_scales(dve):
            dve.wait_ge(s_usq, NU)
            dve.tensor_reduce(usum[:, GA:GB + 1], usq[:, 0:OUT_U].rearrange("p (m k) -> p m k", k=KT),
                              AX.X, ALU.add).then_inc(s_us, 1)
            dve.tensor_reduce(usum[:, OA:OB + 1], usq[:, OUT_U:WO_U].rearrange("p (m k) -> p m k", k=4),
                              AX.X, ALU.add).then_inc(s_us, 1)
            dve.tensor_reduce(usum[:, WO:WO + 1], usq[:, WO_U:NU], AX.X, ALU.add).then_inc(s_us, 1)
            dve.wait_ge(s_ua, 1)
            power_of_two(dve, uall[:, :], upow[:, :], uscale[:, :], uinv[:, :], s_uc, 0)
            dve.wait_ge(s_uc, 4)
            dve.tensor_scalar(ngs[:, :], uscale[:, GA:GB + 1], -1.0, None, ALU.mult).then_inc(s_uc, 1)
            for m, w in ((GA, KT), (OA, 4)):
                u0, n = MAT_UNITS[m][0], 2 * w
                dve.tensor_tensor(ugi[:, u0:u0 + n].rearrange("p (m k) -> p m k", m=2),
                                  gain[:, u0:u0 + n].rearrange("p (m k) -> p m k", m=2),
                                  uinv[:, m:m + 2].unsqueeze(2).broadcast_to([P, 2, w]),
                                  ALU.mult).then_inc(s_uc, 1)
            dve.tensor_tensor(ugi[:, WO_U:NU], gain[:, WO_U:NU],
                              uinv[:, WO:WO + 1].broadcast_to([P, KT]), ALU.mult).then_inc(s_uc, 1)

        with ExitStack() as actx:
            def sa(name, shape, dt=F32):
                return sb(name, shape, dt, actx)

            wh = weights[:, 0:KT * NA].rearrange("p (k n) -> p k n", k=KT)
            wl = weights[:, KT * NA:].rearrange("p (k n) -> p k n", k=KT)
            arena = sa("arena", [P, 2, 4096])
            scs = arena[:, 0, 0:1024].rearrange("p (h k) -> p h k", h=HEADS)
            ptc = arena[:, 0, 1024:2048].rearrange("p (h k) -> p h k", h=HEADS)
            ptp = arena[:, 0, 2048:3072].rearrange("p (h k) -> p h k", h=HEADS)
            sil = arena[:, 0, 3072:4096]
            brn = arena[:, 1, 0:1024]
            e1 = arena[:, 1, 1024:1280]
            e2 = arena[:, 1, 1280:1536]
            e3 = arena[:, 1, 1536:1792]
            e4 = arena[:, 1, 1792:2048]
            e5q = arena[:, 1, 2048:2176]
            e5k = arena[:, 1, 2176:2304]
            d1 = arena[:, 1, 2304:2560]
            d3 = arena[:, 1, 2560:2816]
            d4 = arena[:, 1, 2816:3072]
            d5 = arena[:, 1, 3072:3200]
            zs = arena[:, 1, 3200:3456]
            sp_ = arena[:, 1, 3456:3712]
            gsp = arena[:, 1, 3712:3968]

            proj = [sa(f"proj{i}", [P, NA]) for i in range(2)]
            xin = [tiles[:, 0, 0:D], tiles[:, 0, D:2 * D]]
            hT = [fp16_parts(tiles[:, 1, 0:D]), fp16_parts(tiles[:, 2, 0:D])]
            x16 = tiles[:, 1, D:2 * D].bitcast(F16).rearrange("p (a n) -> p a n", a=2)
            unit = tiles[:, 2, D:2 * D]
            junk = sa("junk", [P, D], F16)
            qT = sa("qT", [P, GRP, P])
            kT = [sa(f"kT{i}", [P, P]) for i in range(2)]
            aT = sa("aT", [RANK, P])
            vbuf = [sa(f"vbuf{i}", [P, P]) for i in range(2)]
            gT = sa("gT", [P, 4, P])
            q1 = sa("q1", [P, 2, 2, P])
            q5 = sa("q5", [P, 2, 2, CH])
            q3 = sa("q3", [P, 2, P])
            k1 = sa("k1", [P, 2, P])
            k4 = sa("k4", [P, 2, P])
            k5 = sa("k5", [P, 2, CH])
            k2 = sa("k2", [P, 2, P])
            cum = sa("cum", [P, 2, 2, CH])
            carry = sa("carry", [P, 2, 2])
            seg = sa("seg", [P, 4, CH])
            att = sa("att", [P, BH, P])
            state = sa("state", [P, 2, 2, BV])
            og = sa("og", [P, BH, BV])
            o16 = sa("o16", [P, 2, D], F16)
            oT = sa("oT", [P, 2, KT, P], F16)
            tri = sa("tri", [P, P])
            triT = sa("triT", [P, P])
            triN = sa("triN", [P, P])
            cosT = sa("cosT", [P, NBLK, HALF])
            sinT = sa("sinT", [P, NBLK, HALF])
            rt = sa("rt", [P, 4, HEADS + KVH, HALF])
            sinks = sa("sinks", [P, HEADS])
            wal = sa("wal", [RANK, 2 * P])
            bal = sa("bal", [P, 2])
            mx = sa("mx", [P, HEADS])
            mm = sa("mm", [P, HEADS])
            nm = sa("nm", [P, HEADS])
            dsk = sa("dsk", [P, HEADS])
            es = sa("es", [P, HEADS])
            rsum = sa("rsum", [P, HEADS])
            den = sa("den", [P, HEADS])
            rden = sa("rden", [P, HEADS])
            ss4 = sa("ss4", [P, BH])
            var4 = sa("var4", [P, BH])
            ln4 = sa("ln4", [P, BH])
            y4 = sa("y4", [P, BH])
            nt4 = sa("nt4", [P, BH])
            r4 = sa("r4", [P, BH])
            omax = sa("omax", [P, 2])
            oinv = sa("oinv", [P, 2])
            opow = sa("opow", [P, 2])
            tick = sa("tick", [P, 2])

            ang = proj[1][:, 0:256]
            turns = [proj[1][:, 256 * i:256 * (i + 1)] for i in range(1, 4)]
            pos_i = proj[1][:, 1024:1024 + NBLK].bitcast(I32)
            pos_f = proj[1][:, 1056:1056 + NBLK]
            wsq = sa("wsq", [P, NCH, KT])
            wsum = sa("wsum", [P, NCH])
            wall = sa("wall", [P, NCH])
            wpow = sa("wpow", [P, NCH])
            winv = sa("winv", [P, NCH])
            wgi = sa("wgi", [P, NCH, KT])

            s_raw = [[sem(f"raw_{e}_{half}") for half in ("first", "last")] for e in ("even", "odd")]
            s_wsq = sem("w_squares")
            s_wsum = sem("w_square_sum")
            s_wall = sem("w_sum_over_rows")
            s_wsm = sem("w_scales")
            s_whi = [sem("w_hi_by_scalar"), sem("w_hi_by_vector")]
            s_wps = sem("w_scaled_by_pool")
            s_wlo = [sem("w_lo_by_vector"), sem("w_lo_by_pool")]
            s_ub = sem("unit_loaded")
            s_x = [sem("x_even"), sem("x_odd")]
            s_xss = sem("x_square_sum")
            s_xv = sem("x_var")
            s_xt = sem("x_rsqrt_table")
            s_xn = sem("x_rsqrt_newton")
            s_x16 = sem("x_split")
            s_xtr = sem("x_transposed")
            s_hT = sem("hT_copied")
            s_hst = [sem("hT_stored_even"), sem("hT_stored_odd")]
            s_evA = sem("evac_by_scalar")
            s_evD = sem("evac_by_vector")
            s_vb = sem("v_kept")
            s_rm = sem("rope_products")
            s_rp = sem("roped")
            s_t1 = sem("qk_transposed")
            s_qT = sem("qT_copied")
            s_kT = sem("kT_aT_copied")
            s_gT = sem("gT_copied")
            s_z = sem("forget_logits")
            s_zs = sem("forget_logits_copied")
            s_spm = sem("softplus_clamped")
            s_spt = sem("softplus_table")
            s_sp = sem("softplus")
            s_cum = sem("gate_sums")
            s_car = sem("gate_carry")
            s_dif = sem("gate_differences")
            s_e = sem("gate_exps")
            s_gq = sem("gla_factors")
            s_sc = sem("scores")
            s_pv0 = sem("previous_scores_copied")
            s_sel = sem("scores_selected")
            s_mx = sem("row_maxima")
            s_sm = sem("softmax_shift")
            s_es = sem("sink_exps")
            s_ex = sem("score_exps")
            s_den = sem("denominators")
            s_pt = sem("probs_transposed")
            s_ptm = sem("probs_masked")
            s_at = sem("gla_scores")
            s_am = sem("gla_scores_masked")
            s_pvo = sem("attention_out")
            s_kt = sem("gla_keys_turned")
            s_k2 = sem("gla_keys_copied")
            s_go = sem("gla_out")
            s_inc = sem("state_increment")
            s_st = sem("state_updated")
            s_og = sem("gla_out_copied")
            s_gss = sem("gla_square_sum")
            s_gv = sem("gla_var")
            s_gt = sem("gla_rsqrt_table")
            s_gn = sem("gla_rsqrt_newton")
            s_slm = sem("silu_clamped")
            s_slt = sem("silu_tables")
            s_sll = sem("silu_softplus")
            s_sle = sem("silu_sigmoid")
            s_sl = sem("silu")
            s_br = sem("branches_normed")
            s_gat = sem("branches_gated")
            s_om = sem("out_maxima")
            s_o16 = sem("out_split")
            s_otr = sem("out_transposed")
            s_oT = sem("oT_copied")
            s_ost = sem("oT_stored")
            s_rope = sem("rotary_angles")
            s_trig = sem("rotary_tables")
            s_zero = sem("cleared")

            stage = [arena[:, i, :] for i in range(2)]

            def raw(n):
                a, b = CHUNKS[n]
                return stage[n % 2][:, 0:KT * (b - a)].rearrange("p (k n) -> p k n", k=KT)

            def load_chunk(sp, n):
                a, b = CHUNKS[n]
                for s in s_wlo:
                    need(sp, s, n - 1)
                for half in range(2):
                    k = slice(half * KT // 2, (half + 1) * KT // 2)
                    sp.dma_start(raw(n)[:, k], w_branch[half * D // 2:(half + 1) * D // 2, a:b]
                                 .rearrange("(k p) n -> p k n", p=P)).then_inc(s_raw[n % 2][half], 16)

            def chunk_squares(act, n):
                a, b = CHUNKS[n]
                for k in range(KT):
                    if k % (KT // 2) == 0:
                        act.wait_ge(s_raw[n % 2][2 * k // KT], 16 * (n // 2 + 1))
                    last = act.activation(wh[:, k, a:b], raw(n)[:, k, :], ACT.Square, scale=gain[:, k:k + 1],
                                          accum_out=wsq[:, n, k:k + 1])
                last.then_inc(s_wsq, 1)

            def chunk_sum(dve, n):
                dve.wait_ge(s_wsq, n + 1)
                dve.tensor_reduce(wsum[:, n:n + 1], wsq[:, n, :], AX.X, ALU.add).then_inc(s_wsum, 1)

            def chunk_over_rows(pool, n):
                pool.wait_ge(s_wsum, n + 1)
                pool.partition_all_reduce(wall[:, n:n + 1], wsum[:, n:n + 1], P, RADD).then_inc(s_wall, 1)

            def chunk_scale(dve, n):
                c = slice(n, n + 1)
                dve.wait_ge(s_wall, n + 1)
                power_of_two(dve, wall[:, c], wpow[:, c], wscale[:, c], winv[:, c], s_wsm, 5 * n)
                dve.wait_ge(s_wsm, 5 * n + 4)
                dve.tensor_scalar(wgi[:, n, :], gain[:, 0:KT], winv[:, c], None, ALU.mult).then_inc(s_wsm, 1)

            ACT_HI = range(0, 3)
            DVE_HI = range(3, KT)
            DVE_LO = range(0, 7)
            POOL_LO = range(7, KT)

            def chunk_hi(eng, n, ks):
                a, b = CHUNKS[n]
                eng.wait_ge(s_wsm, 5 * n + 5)
                for k in ks:
                    if ks is ACT_HI:
                        last = eng.activation(wh[:, k, a:b], raw(n)[:, k, :], ACT.Copy, scale=wgi[:, n, k:k + 1])
                    else:
                        last = eng.tensor_scalar(wh[:, k, a:b], raw(n)[:, k, :], wgi[:, n, k:k + 1], None,
                                                 ALU.mult)
                last.then_inc(s_whi[0 if ks is ACT_HI else 1], 1)

            def chunk_lo(dve, n):
                a, b = CHUNKS[n]
                dve.wait_ge(s_whi[0], n + 1)
                dve.wait_ge(s_whi[1], n + 1)
                for k in DVE_LO:
                    last = dve.scalar_tensor_tensor(wl[:, k, a:b], raw(n)[:, k, :], wgi[:, n, k:k + 1],
                                                    wh[:, k, a:b], ALU.mult, ALU.subtract)
                last.then_inc(s_wlo[0], 1)

            def chunk_lo_pool(pool, n):
                a, b = CHUNKS[n]
                pool.wait_ge(s_whi[1], n + 1)
                for k in POOL_LO:
                    last = pool.tensor_scalar(raw(n)[:, k, :], raw(n)[:, k, :], wgi[:, n, k:k + 1], None,
                                              ALU.mult)
                last.then_inc(s_wps, 1)
                pool.wait_ge(s_wps, n + 1)
                k = slice(POOL_LO[0], KT)
                pool.tensor_tensor(wl[:, k, a:b], raw(n)[:, k, :], wh[:, k, a:b],
                                   ALU.subtract).then_inc(s_wlo[1], 1)

            def steps(eng, step):
                for t in range(4):
                    step(t, t // 2, t % 2)
                with eng.Fori(0, (NBLK - 6) // 2) as i:
                    for u in range(2):
                        step(i * 2 + (4 + u), i + 2, u)
                for t in range(NBLK - 2, NBLK + 2):
                    step(t, t // 2, t % 2)

            def known(t):
                return isinstance(t, int)

            def has_front(t):
                return not known(t) or t < NBLK

            def has_xprep(t):
                return not known(t) or t + 1 < NBLK

            def has_back(t):
                return not known(t) or 1 <= t <= NBLK

            def has_turn(t):
                return not known(t) or 2 <= t <= NBLK + 1

            block = actx.enter_context(nc.Block())

            @block.sync
            def _(sp):
                def load_x(n, h, u):
                    need(sp, s_x16, (n - 1) * 2)
                    sp.dma_start(xin[u][:, :], x[bass.ds(n * P, P), :]).then_inc(s_x[u], 16)

                load_x(0, 0, 0)
                sp.dma_start(gain[:, 0:KT], g_in).then_inc(s_gin, 16)
                load_chunk(sp, 0)
                sp.dma_start(pos_i, positions).then_inc(s_pos, 16)
                load_chunk(sp, 1)
                sp.dma_start(gain[:, KT:2 * KT], g_in).then_inc(s_const, 16)
                sp.dma_start(gain[:, OUT_U + 4:WO_U], g_gla_norm).then_inc(s_const, 16)
                sp.dma_start(wal[:, :], w_alpha_up).then_inc(s_const, 16)
                sp.dma_start(bal[:, :], b_alpha).then_inc(s_const, 16)
                sp.dma_start(sinks[:, :], attn_sinks.partition_broadcast(P)).then_inc(s_const, 16)
                load_x(1, 0, 1)
                for n in range(2, NCH):
                    load_chunk(sp, n)

                def step(t, h, u):
                    if not known(t) or t + 2 < NBLK:
                        load_x(t + 2, h + 1, u)
                    if has_front(t):
                        need(sp, s_usq, t)
                        sp.dma_start(unit[:, :], w_units[bass.ds(t, 1)].rearrange("a p n -> (a p) n")
                                     ).then_inc(s_ub, 16)
                    if has_xprep(t):
                        need(sp, s_hT, (t + 2) * 2)
                        sp.dma_start(hts[bass.ds(t + 1, 1)].rearrange("a p n -> (a p) n"),
                                     hT[1 - u][:, :, :, :].rearrange("p a k t -> p (a k t)")
                                     ).then_inc(s_hst[1 - u], 16)
                    if known(t) and t == NBLK:
                        sp.wait_ge(s_x16, NBLK * 2)
                        load_piece(sp, 0)
                        sp.wait_ge(s_xtr, NBLK)
                        sp.wait_ge(s_pj, (NBLK - 1) * NCH)
                        sp.wait_ge(s_hst[0], 16 * (NBLK // 2))
                        load_piece(sp, 1)
                        sp.wait_ge(s_usq, NU)
                        sp.wait_ge(s_pj, NBLK * NCH)
                        sp.wait_ge(s_hst[1], 16 * (NBLK // 2))
                        load_piece(sp, 2)
                        sp.wait_ge(s_ost, 16)
                        sp.dma_start(hb0.rearrange("p a k t -> p (a k t)"), hts[0]).then_inc(s_hb[0], 16)
                        sp.dma_start(ob0.rearrange("p a k t -> p (a k t)"), ots[0]).then_inc(s_ob[0], 16)
                        load_piece(sp, 3)
                        load_piece(sp, 4)
                    if has_turn(t):
                        need(sp, s_oT, (t - 1) * 2)
                        sp.dma_start(ots[bass.ds(t - 2, 1)].rearrange("a p n -> (a p) n"),
                                     oT[:, :, :, :].rearrange("p a k t -> p (a k t)")
                                     ).then_inc(s_ost, 16)

                sp.wait_ge(s_hT, 2)
                sp.dma_start(hts[0], hT[0][:, :, :, :].rearrange("p a k t -> p (a k t)")).then_inc(s_hst[0], 16)
                steps(sp, step)
                for i in range(5, NPRE + 3):
                    load_piece(sp, i)
                for s, n in ((s_hst[0], NBLK // 2), (s_hst[1], NBLK // 2), (s_ost, NBLK)):
                    sp.wait_ge(s, 16 * n)

            @block.gpsimd
            def _(pool):
                pool.memset(ident[:, :], 0.0).then_inc(s_id, 1)
                pool.memset(ident16[:, :], 0.0).then_inc(s_id, 1)
                pool.memset(tri[:, :], 1.0).then_inc(s_id, 1)
                pool.memset(triT[:, :], 1.0).then_inc(s_id, 1)
                pool.memset(triN[:, :], 1.0).then_inc(s_id, 1)
                pool.wait_ge(s_id, 5)
                for m in (ident, ident16):
                    pool.affine_select(out=m[:, :], in_=m[:, :], compare_op=ALU.not_equal, fill=1.0, base=0,
                                       pattern=[[-1, P]], channel_multiplier=1).then_inc(s_msk, 1)
                for m, op, sign in ((tri, ALU.is_ge, 1), (triT, ALU.is_ge, -1), (triN, ALU.is_gt, 1)):
                    pool.affine_select(out=m[:, :], in_=m[:, :], compare_op=op, fill=0.0, base=0,
                                       pattern=[[-sign, P]], channel_multiplier=sign).then_inc(s_msk, 1)
                pool.memset(gain[:, OUT_U:OUT_U + 4], 1.0).then_inc(s_gain, 1)
                pool.memset(gain[:, WO_U:NU], 1.0).then_inc(s_gain, 1)
                pool.memset(q1[:, :, :, :], 0.0).then_inc(s_zero, 1)
                pool.memset(q5[:, :, :, :], 0.0).then_inc(s_zero, 1)
                pool.memset(state[:, :, :, :], 0.0).then_inc(s_zero, 1)
                pool.memset(att[:, :, :], 0.0).then_inc(s_zero, 1)
                pool.memset(carry[:, :, :], 0.0).then_inc(s_zero, 1)
                pool.memset(seg[:, :, :], 1.0).then_inc(s_zero, 1)
                pool.wait_ge(s_zero, 6)
                pool.memset(seg[:, :, 0:1], 0.0).then_inc(s_zero, 1)
                for n in range(NCH):
                    chunk_over_rows(pool, n)
                    chunk_lo_pool(pool, n)

                def step(t, h, u):
                    if not has_back(t):
                        return
                    b, pr = t - 1, proj[1 - u]
                    pool.wait_ge(s_evA, t * 3)
                    pool.wait_ge(s_evD, t * 3)
                    need(pool, s_pvo, b)
                    pool.wait_ge(s_trig, 2)
                    qk = pr[:, 0:VC].rearrange("p (h d) -> p h d", d=HD)
                    x1, x2 = qk[:, :, 0:HALF], qk[:, :, HALF:2 * HALF]
                    c = cosT[:, bass.ds(b, 1), :].broadcast_to([P, HEADS + KVH, HALF])
                    s = sinT[:, bass.ds(b, 1), :].broadcast_to([P, HEADS + KVH, HALF])
                    for n, (a, f) in enumerate(((x1, c), (x2, s), (x2, c), (x1, s))):
                        pool.tensor_tensor(rt[:, n], a, f, ALU.mult).then_inc(s_rm, 1)
                    pool.tensor_copy(vbuf[1 - u][:, :], pr[:, VC:VC + P]).then_inc(s_vb, 1)
                    need(pool, s_rm, t * 4)
                    pool.tensor_tensor(x1, rt[:, 0], rt[:, 1], ALU.subtract).then_inc(s_rp, 1)
                    pool.tensor_tensor(x2, rt[:, 2], rt[:, 3], ALU.add).then_inc(s_rp, 1)
                    if known(t) and t == NBLK:
                        pool.wait_ge(s_us, 3)
                        pool.partition_all_reduce(uall[:, :], usum[:, :], P, RADD).then_inc(s_ua, 1)
                        for i in range(2):
                            split_piece_pool(pool, i)
                    need(pool, s_sle, t)
                    pool.tensor_tensor(sil[:, 0:512], sil[:, 0:512], pr[:, ZAC:ZAC + 512], ALU.mult).then_inc(s_sl, 1)
                    pool.tensor_tensor(sil[:, 512:], sil[:, 512:], pr[:, ZBC:ZBC + 512], ALU.mult).then_inc(s_sl, 1)
                    if known(t) and t == NBLK:
                        for i in range(2, NPRE):
                            split_piece_pool(pool, i)

                steps(pool, step)

            @block.scalar
            def _(act):
                def x_squares(n, h, u):
                    need(act, s_x[u], 16 * h + 16)
                    act.activation(junk[:, :], xin[u][:, :], ACT.Square, accum_out=ss[:, :]).then_inc(s_xss, 1)

                def x_table(n):
                    rsqrt_table(act, s_xv, n + 1, s_xt, n * 2, var[:, :], lnv[:, :], y0[:, :])

                def x_evac(n, h, u):
                    need(act, s_xtr, n + 1)
                    need(act, s_pj, (n - 1) * NCH)
                    need(act, s_hst[u], 16 * h)
                    for a in range(2):
                        act.activation(hT[u][:, a].rearrange("p k t -> p (k t)"),
                                       bank[2 + a][:, :].bitcast(F16), ACT.Copy).then_inc(s_hT, 1)

                def evac(t, u, c):
                    a, b = CHUNKS[c]
                    act.wait_ge(s_pj, t * NCH + (c + 1))
                    if c == 0:
                        need(act, s_inc, t - 1)
                        need(act, s_gat, t - 1)
                        src = bank[0][:, :].rearrange("p (g j d) -> p g j d", g=KVH, j=GRP)
                        dst = proj[u][:, 0:512].rearrange("p (j g d) -> p g j d", g=KVH, j=GRP)
                        for g in range(KVH):
                            last = act.activation(dst[:, g], src[:, g], ACT.Copy, scale=wscale[:, 0:1])
                    else:
                        last = act.activation(proj[u][:, a:b], bank[0][:, 0:b - a], ACT.Copy,
                                              scale=wscale[:, c:c + 1])
                    last.then_inc(s_evA, 1)

                act.preload_act_table_set("natural_log_exp_and_others")
                x_squares(0, 0, 0)
                x_table(0)
                act.wait_ge(s_gin, 16)
                for n in range(NCH):
                    chunk_squares(act, n)
                    if n == 0:
                        x_evac(0, 0, 0)
                    if n in (2, 4):
                        evac(0, 0, n - 2)
                    chunk_hi(act, n, ACT_HI)
                act.wait_ge(s_rope, 2 + 2 * ROPE_OPS + 3)
                act.activation(sinT[:, :, :].rearrange("p n i -> p (n i)"), ang, ACT.Sin).then_inc(s_trig, 1)
                act.activation(cosT[:, :, :].rearrange("p n i -> p (n i)"), turns[0],
                               ACT.Sin).then_inc(s_trig, 1)
                act.preload_act_table_set("natural_log_exp_and_others")

                def step(t, h, u):
                    b, pr = t - 1, proj[1 - u]
                    back = has_back(t)
                    if has_xprep(t):
                        x_squares(t + 1, h + u, 1 - u)
                    if has_front(t) and not (known(t) and t == 0):
                        evac(t, u, 0)
                    if back:
                        need(act, s_t1, b * 3 + 1)
                        act.activation(qT[:, :, :].rearrange("p j t -> p (j t)"), bank[4][:, :],
                                       ACT.Copy).then_inc(s_qT, 1)
                        need(act, s_t1, b * 3 + 3)
                        act.activation(gT[:, :, :].rearrange("p j t -> p (j t)"), bank[6][:, :],
                                       ACT.Copy).then_inc(s_gT, 1)
                    if has_xprep(t):
                        x_table(t + 1)
                    if has_front(t):
                        if known(t) and t == 0:
                            act.wait_ge(s_gain, 2)
                            act.wait_ge(s_const, 16 * NCONST)
                        need(act, s_ub, (t + 1) * 16)
                        act.activation(unit[:, :], unit[:, :], ACT.Square, scale=gain[:, bass.ds(t, 1)],
                                       accum_out=usq[:, bass.ds(t, 1)]).then_inc(s_usq, 1)
                    if back:
                        need(act, s_slm, b * 2 + 2)
                        act.activation(sil, sil, ACT.Exp).then_inc(s_slt, 1)
                        need(act, s_slt, b * 2 + 1)
                        act.activation(sil, sil, ACT.Ln, bias=1.0).then_inc(s_slt, 1)
                        if known(t) and t == NBLK:
                            split_piece(act, 0, ACT_K, ())
                        need(act, s_spm, b + 1)
                        act.activation(sp_, sp_, ACT.Exp).then_inc(s_spt, 1)
                        need(act, s_spt, b * 2 + 1)
                        act.activation(sp_, sp_, ACT.Ln, bias=1.0).then_inc(s_spt, 1)
                        if not (known(t) and b == 0):
                            for g in range(KVH):
                                need(act, s_sc, b * 4 + (2, 4)[g])
                                act.activation(scs[:, g * GRP:(g + 1) * GRP, :].rearrange("p h k -> p (h k)"),
                                               bank[(5, 7)[g]][:, :], ACT.Copy).then_inc(s_pv0, 1)
                        need(act, s_sll, b * 2 + 2)
                        act.activation(sil, sil, ACT.Exp, scale=-1.0).then_inc(s_sle, 1)
                        need(act, s_sm, b * 3 + 3)
                        act.activation(es[:, :], dsk[:, :], ACT.Exp).then_inc(s_es, 1)
                        for hd in range(HEADS):
                            act.activation(scs[:, hd, :], scs[:, hd, :], ACT.Exp, bias=nm[:, hd:hd + 1],
                                           scale=HD ** -0.5, accum_out=rsum[:, hd:hd + 1]).then_inc(s_ex, 1)
                    if has_front(t) and not (known(t) and t == 0):
                        evac(t, u, 2)
                    if back:
                        need(act, s_dif, b * 4 + 4)
                        need(act, s_gq, b * 8)
                        need(act, s_st, b * 4)
                        for o, i, sc in ((e1, d1, 1), (e2, d1, -1), (e3, d3, 1), (e4, d4, -1),
                                         (e5k, d5, -1)):
                            act.activation(o, i, ACT.Exp, scale=sc / 16.0).then_inc(s_e, 1)
                        act.activation(e5q.rearrange("p (a c) -> p a c", a=2), cum[:, :, 1, :], ACT.Exp,
                                       scale=1 / 16.0).then_inc(s_e, 1)
                        if known(t) and t == NBLK:
                            split_piece(act, 1, ACT_K, ())
                    if has_turn(t):
                        need(act, s_otr, t - 1)
                        need(act, s_ost, (t - 2) * 16)
                        for a in range(2):
                            act.activation(oT[:, a].rearrange("p k t -> p (k t)"),
                                           bank[2 + a][:, :].bitcast(F16), ACT.Copy).then_inc(s_oT, 1)
                    if has_front(t):
                        evac(t, u, 4)
                    if back:
                        need(act, s_kt, t)
                        act.activation(k2[:, :, :].rearrange("p a t -> p (a t)"), bank[4][:, 0:256],
                                       ACT.Copy).then_inc(s_k2, 1)
                        if known(t) and t == NBLK:
                            split_piece(act, 2, ACT_K, ())
                    if has_xprep(t):
                        x_evac(t + 1, h + u, 1 - u)
                    if back:
                        need(act, s_go, t)
                        act.activation(og[:, :, :].rearrange("p h v -> p (h v)"), bank[5][:, :],
                                       ACT.Copy).then_inc(s_og, 1)
                        need(act, s_og, t)
                        for hd in range(BH):
                            act.activation(junk[:, hd * BV:(hd + 1) * BV], og[:, hd, :], ACT.Square,
                                           accum_out=ss4[:, hd:hd + 1]).then_inc(s_gss, 1)
                        rsqrt_table(act, s_gv, t, s_gt, b * 2, var4[:, :], ln4[:, :], y4[:, :])
                        if known(t) and t == NBLK:
                            for i in range(3, NPRE):
                                split_piece(act, i, ACT_K, ())

                steps(act, step)

            @block.tensor
            def _(pe):
                def turn16(tile, s_in, n_in):
                    need(pe, s_in, n_in)
                    for a in range(2):
                        dst = bank[2 + a][:, :].bitcast(F16)
                        for k in range(KT):
                            last = pe.transpose(dst[:, k * P:(k + 1) * P], tile[:, a, k * P:(k + 1) * P],
                                                ident16[:, :])
                    return last

                def chunk(t, u, c):
                    a, b = CHUNKS[c]
                    if c == 0:
                        need(pe, s_hT, (t + 1) * 2)
                    if known(t) and t == 0:
                        for s in s_wlo:
                            pe.wait_ge(s, c + 1)
                    if c >= 2:
                        need(pe, (s_evA, s_evD)[c % 2], t * 3 + c // 2)
                    else:
                        need(pe, (s_evA, s_evD)[c % 2], t * 3)
                    o = bank[c % 2][:, 0:b - a]
                    n = 0
                    for k in range(KT):
                        for l, r in ((0, wh), (0, wl), (1, wh)):
                            last = pe.matmul(o, hT[u][:, l, k, :], r[:, k, a:b], start=n == 0,
                                             stop=n == 3 * KT - 1)
                            n += 1
                    last.then_inc(s_pj, 1)

                def qk_turn(t, b, pr):
                    need(pe, s_rp, t * 2)
                    need(pe, s_k2, b)
                    for j in range(GRP):
                        last = pe.transpose(bank[4][:, j * P:(j + 1) * P], pr[:, j * P:(j + 1) * P], ident[:, :])
                    last.then_inc(s_t1, 1)
                    need(pe, s_og, b)
                    pe.transpose(bank[5][:, 0:P], pr[:, KC:KC + P], ident[:, :])
                    pe.transpose(bank[5][0:RANK, P:2 * P], pr[:, ALC:NA], ident[:, :]).then_inc(s_t1, 1)
                    need(pe, s_st, b * 4)
                    for j in range(4):
                        last = pe.transpose(bank[6][:, j * P:(j + 1) * P], pr[:, QBC + j * P:QBC + (j + 1) * P],
                                            ident[:, :])
                    last.then_inc(s_t1, 1)

                def logits(t, b):
                    need(pe, s_kT, t * 2)
                    if has_front(t):
                        need(pe, s_hT, (t + 1) * 2)
                    else:
                        need(pe, s_oT, (t - 2) * 2)
                    for p in range(2):
                        last = pe.matmul(bank[2][:, p * P:(p + 1) * P], wal[:, p * P:(p + 1) * P], aT[:, :],
                                         start=True, stop=True)
                    last.then_inc(s_z, 1)

                def scores(t, b, u):
                    need(pe, s_qT, t)
                    need(pe, s_gT, t)
                    need(pe, s_br, b * 2)
                    for g in range(KVH):
                        rows = slice(g * HD, (g + 1) * HD)
                        for bk, keys in (((4, 6)[g], kT[1 - u]), ((5, 7)[g], kT[u])):
                            for j in range(GRP):
                                last = pe.matmul(bank[bk][:, j * P:(j + 1) * P], qT[rows, j, :], keys[rows, :],
                                                 start=True, stop=True)
                            last.then_inc(s_sc, 1)

                def scores0(t):
                    need(pe, s_qT, t)
                    need(pe, s_gT, t)
                    for g in range(KVH):
                        rows = slice(g * HD, (g + 1) * HD)
                        for j in range(GRP):
                            last = pe.matmul(bank[(4, 6)[g]][:, j * P:(j + 1) * P], qT[rows, j, :],
                                             kT[0][rows, :], start=True, stop=True)
                        last.then_inc(s_sc, 2)

                def probs_turn(t, b):
                    for g in range(KVH):
                        need(pe, s_ex, b * 8 + 4 * g + 4)
                        for j in range(GRP):
                            last = pe.transpose(bank[(4, 6)[g]][:, j * P:(j + 1) * P], scs[:, g * GRP + j, :],
                                                ident[:, :])
                        last.then_inc(s_pt, 1)

                def gla_scores(t, b):
                    need(pe, s_gq, t * 8)
                    if not (known(t) and b == 0):
                        need(pe, s_pv0, t * 2 - 1)
                    for p in range(2):
                        o = bank[5][:, p * 256:(p + 1) * 256]
                        pe.matmul(o, k1[:, p, :], q1[:, p, :, :].rearrange("p h t -> p (h t)"),
                                  start=True, stop=True)
                        o = o.rearrange("p (h t) -> p h t", h=2)[0:CH, :, CH:P]
                        last = pe.matmul(o, k5[:, p, :], q5[:, p, :, :], start=True, stop=True)
                    last.then_inc(s_at, 1)

                def values(t, b, u):
                    need(pe, s_ptm, t * 4)
                    need(pe, s_vb, t)
                    if not (known(t) and b == 0):
                        need(pe, s_pv0, t * 2)
                    for hd in range(HEADS):
                        g = hd // GRP
                        o = bank[7][:, hd * HD:(hd + 1) * HD]
                        first = known(t) and b == 0
                        last = pe.matmul(o, ptc[:, hd, :], vbuf[1 - u][:, g * HD:(g + 1) * HD], start=True,
                                         stop=first)
                        if not first:
                            last = pe.matmul(o, ptp[:, hd, :], vbuf[u][:, g * HD:(g + 1) * HD], start=False,
                                             stop=True)
                    last.then_inc(s_pvo, 1)

                def keys_turn(t):
                    for p in range(2):
                        last = pe.transpose(bank[4][:, p * P:(p + 1) * P], k4[:, p, :], ident[:, :])
                    last.then_inc(s_kt, 1)

                def gla_out(t, b, pr):
                    need(pe, s_am, t)
                    need(pe, s_st, b * 4)
                    v = pr[:, VBC:VBC + BH * BV]
                    for p in range(2):
                        pe.matmul(bank[5][:, p * 256:(p + 1) * 256], q3[:, p, :],
                                  state[:, p].rearrange("p h v -> p (h v)"), start=p == 0, stop=False,
                                  skip_group_check=True)
                    for hd in range(BH):
                        last = pe.matmul(bank[5][:, hd * BV:(hd + 1) * BV], att[:, hd, :],
                                         v[:, hd * BV:(hd + 1) * BV], start=False, stop=hd == BH - 1,
                                         skip_group_check=True)
                    last.then_inc(s_go, 1)
                    need(pe, s_k2, t)
                    for p in range(2):
                        last = pe.matmul(bank[6][:, p * 256:(p + 1) * 256], k2[:, p, :],
                                         v[:, p * 256:(p + 1) * 256], start=True, stop=True)
                    last.then_inc(s_inc, 1)

                pe.wait_ge(s_msk, 5)
                turn16(x16, s_x16, 2).then_inc(s_xtr, 1)

                def step(t, h, u):
                    b, pr = t - 1, proj[1 - u]
                    front, back = has_front(t), has_back(t)
                    if front:
                        chunk(t, u, 0)
                    if back:
                        if known(t) and b == 0:
                            pe.wait_ge(s_const, 16 * NCONST)
                            pe.wait_ge(s_zero, 7)
                        qk_turn(t, b, pr)
                    if front:
                        chunk(t, u, 1)
                    if back:
                        logits(t, b)
                        if known(t) and b == 0:
                            scores0(t)
                        else:
                            scores(t, b, u)
                    if front:
                        chunk(t, u, 2)
                    if has_turn(t):
                        need(pe, s_zs, min(t, NBLK) * 2 if known(t) else t * 2)
                        need(pe, s_oT, (t - 2) * 2)
                        turn16(o16, s_o16, (t - 1) * 4).then_inc(s_otr, 1)
                    if front:
                        chunk(t, u, 3)
                    if back:
                        probs_turn(t, b)
                    if front:
                        chunk(t, u, 4)
                    if back:
                        values(t, b, u)
                        gla_scores(t, b)
                        keys_turn(t)
                    if has_xprep(t):
                        if has_turn(t):
                            need(pe, s_oT, (t - 1) * 2)
                        elif back:
                            need(pe, s_zs, t * 2)
                        else:
                            need(pe, s_hT, 2)
                        turn16(x16, s_x16, (t + 2) * 2).then_inc(s_xtr, 1)
                    if front:
                        chunk(t, u, 5)
                    if back:
                        gla_out(t, b, pr)

                steps(pe, step)

            @block.vector
            def _(dve):
                count = [0]

                def link(ins):
                    ins.then_inc(s_rope, 1)
                    count[0] += 1
                    dve.wait_ge(s_rope, count[0])

                n2, n1, n0 = turns

                def angles():
                    inv_freq = np.exp(np.float32(-np.log(THETA)) * np.arange(HALF, dtype=np.float32)
                                      * np.float32(1.0 / HALF)).astype(np.float32)
                    dve.wait_ge(s_pos, 16)
                    link(dve.tensor_copy(pos_f, pos_i))
                    a3 = ang.rearrange("p (n i) -> p n i", i=HALF)
                    for i in range(HALF):
                        ins = dve.tensor_scalar(a3[:, :, i], pos_f, float(inv_freq[i]), None, ALU.mult)
                    link(ins)

                def whole_turns():
                    link(dve.tensor_scalar(n0, ang, float(1 / (2 * np.pi)), None, ALU.mult))
                    link(dve.tensor_scalar(n2, n0, 2.0 ** -22, MAGIC, ALU.mult, ALU.add))
                    link(dve.tensor_scalar(n2, n2, MAGIC, None, ALU.subtract))
                    link(dve.scalar_tensor_tensor(n0, n2, -2.0 ** 22, n0, ALU.mult, ALU.add))
                    link(dve.tensor_scalar(n1, n0, 2.0 ** -11, MAGIC, ALU.mult, ALU.add))
                    link(dve.tensor_scalar(n1, n1, MAGIC, None, ALU.subtract))
                    link(dve.scalar_tensor_tensor(n0, n1, -2.0 ** 11, n0, ALU.mult, ALU.add))
                    link(dve.tensor_scalar(n0, n0, MAGIC, None, ALU.add))
                    link(dve.tensor_scalar(n0, n0, MAGIC, None, ALU.subtract))

                def take_turns_off():
                    for c in two_pi_parts():
                        for n, w in ((n2, 2.0 ** 22), (n1, 2.0 ** 11), (n0, 1.0)):
                            link(dve.scalar_tensor_tensor(ang, n, -w * c, ang, ALU.mult, ALU.add))

                def sine_arguments():
                    pi = float(np.nextafter(np.float32(np.pi), np.float32(0)))
                    link(dve.tensor_scalar(ang, ang, pi, -pi, ALU.min, ALU.max))
                    link(dve.scalar_tensor_tensor(n2, ang, -1.0, ang, ALU.mult, ALU.max))
                    link(dve.tensor_scalar(n2, n2, -1.0, float(np.pi / 2), ALU.mult, ALU.add))
                    assert count[0] == 2 + 2 * ROPE_OPS + 3

                def x_start(n):
                    rsqrt_start(dve, s_xss, n + 1, s_xv, ss[:, :], var[:, :], D)

                def x_split(n, u):
                    rsqrt_newton(dve, s_xt, n * 2, s_xn, n * 4, var[:, :], y0[:, :], nt[:, 0:1], rstd[:, :])
                    need(dve, s_xn, n * 4 + 4)
                    need(dve, s_xtr, n)
                    dve.tensor_scalar(x16[:, 0], xin[u][:, :], rstd[:, 0:1], None, ALU.mult).then_inc(s_x16, 1)
                    need(dve, s_x16, n * 2 + 1)
                    dve.scalar_tensor_tensor(x16[:, 1], xin[u][:, :], rstd[:, 0:1], x16[:, 0], ALU.mult,
                                             ALU.subtract).then_inc(s_x16, 1)

                def evac(t, u, c):
                    a, b = CHUNKS[c]
                    dve.wait_ge(s_pj, t * NCH + (c + 1))
                    if c == 1:
                        need(dve, s_inc, t - 1)
                        need(dve, s_gat, t - 1)
                    dve.tensor_scalar(proj[u][:, a:b], bank[1][:, 0:b - a], wscale[:, c:c + 1], None,
                                      ALU.mult).then_inc(s_evD, 1)

                dve.memset(tick[:, :], 0.0)
                x_start(0)
                x_split(0, 0)
                dve.wait_ge(s_gin, 16)
                for n in range(NCH):
                    chunk_sum(dve, n)
                    chunk_scale(dve, n)
                    chunk_hi(dve, n, DVE_HI)
                    if n in (3, 5):
                        evac(0, 0, n - 2)
                    chunk_lo(dve, n)
                    if n == 0:
                        angles()
                    elif n in (1, 3):
                        whole_turns()
                    elif n in (2, 4):
                        take_turns_off()
                    else:
                        sine_arguments()

                def wait_carrier():
                    dve.tensor_copy(tick[:, 0:1], tick[:, 1:2])

                def softmax_shift(t, b, first):
                    for g in range(KVH):
                        hs = slice(g * GRP, (g + 1) * GRP)
                        if first:
                            dve.memset(scs[:, hs, :], NEG).then_inc(s_pv0, 1)
                        need(dve, s_pv0, t * 2 - 1 + g)
                        need(dve, s_sc, b * 4 + 1 + 2 * g)
                        wait_carrier()
                        dve.copy_predicated(scs[:, hs, :],
                                            tri[:, :].bitcast(U32).unsqueeze(1).broadcast_to([P, GRP, P]),
                                            bank[(4, 6)[g]][:, :].rearrange("p (h k) -> p h k", h=GRP)
                                            ).then_inc(s_sel, 1)
                        need(dve, s_sel, b * 2 + 1 + g)
                        dve.tensor_reduce(mx[:, hs], scs[:, hs, :], AX.X, ALU.max).then_inc(s_mx, 1)
                    need(dve, s_mx, t * 2)
                    dve.scalar_tensor_tensor(mm[:, :], mx[:, :], HD ** -0.5, sinks[:, :], ALU.mult,
                                             ALU.max).then_inc(s_sm, 1)
                    need(dve, s_sm, b * 3 + 1)
                    dve.tensor_scalar(nm[:, :], mm[:, :], -1.0, None, ALU.mult).then_inc(s_sm, 1)
                    dve.tensor_tensor(dsk[:, :], sinks[:, :], mm[:, :], ALU.subtract).then_inc(s_sm, 1)

                def gate_sums(t, b):
                    need(dve, s_spt, b * 2 + 2)
                    dve.scalar_tensor_tensor(gsp, sp_, -1.0, zs, ALU.mult, ALU.min).then_inc(s_sp, 1)
                    need(dve, s_sp, t)
                    dve.tensor_tensor_scan(cum[:, :, :, :].rearrange("p a b c -> p (a b c)"),
                                           seg[:, :, :].rearrange("p a c -> p (a c)"), gsp, 0.0,
                                           ALU.mult, ALU.add).then_inc(s_cum, 1)
                    need(dve, s_cum, t)
                    c4 = cum[:, :, :, :].rearrange("p a b c -> p (a b) c")
                    dve.tensor_copy(carry[:, :, 1:2], cum[:, :, 0, CH - 1:CH]).then_inc(s_car, 1)
                    dve.tensor_tensor(d1.rearrange("p (a c) -> p a c", a=4), c4,
                                      c4[:, :, CH // 2 - 1:CH // 2].broadcast_to([P, 4, CH]),
                                      ALU.subtract).then_inc(s_dif, 1)
                    dve.tensor_tensor(d5.rearrange("p (a c) -> p a c", a=2), cum[:, :, 0, :],
                                      cum[:, :, 0, CH - 1:CH].broadcast_to([P, 2, CH]),
                                      ALU.subtract).then_inc(s_dif, 1)
                    need(dve, s_car, t)
                    dve.tensor_tensor(d3.rearrange("p (a c) -> p a c", a=4), c4,
                                      carry[:, :, :].rearrange("p a b -> p (a b)").unsqueeze(2)
                                      .broadcast_to([P, 4, CH]), ALU.add).then_inc(s_dif, 1)
                    need(dve, s_dif, b * 4 + 3)
                    d3v = d3.rearrange("p (a c) -> p a c", a=2)
                    dve.tensor_tensor(d4.rearrange("p (a c) -> p a c", a=2), d3v,
                                      d3v[:, :, P - 1:P].broadcast_to([P, 2, P]),
                                      ALU.subtract).then_inc(s_dif, 1)

                def gla_factors(t, b):
                    need(dve, s_gT, t)
                    need(dve, s_e, t * 6)
                    need(dve, s_inc, b)
                    v = lambda e: e.rearrange("p (a c) -> p a c", a=2)
                    sc = BK ** -0.5
                    for hh in range(2):
                        r = slice(hh * BK, (hh + 1) * BK)
                        dve.scalar_tensor_tensor(q1[r, :, hh, :], gT[r, 0:2, :], sc, v(e1)[r], ALU.mult,
                                                 ALU.mult).then_inc(s_gq, 1)
                        dve.scalar_tensor_tensor(q5[r, :, hh, :], gT[r, 0:2, CH:P], sc, v(e5q)[r], ALU.mult,
                                                 ALU.mult).then_inc(s_gq, 1)
                    dve.scalar_tensor_tensor(q3[:, :, :], gT[:, 0:2, :], sc, v(e3), ALU.mult,
                                             ALU.mult).then_inc(s_gq, 1)
                    dve.tensor_tensor(k1[:, :, :], gT[:, 2:4, :], v(e2), ALU.mult).then_inc(s_gq, 1)
                    dve.tensor_tensor(k4[:, :, :], gT[:, 2:4, :], v(e4), ALU.mult).then_inc(s_gq, 1)
                    dve.tensor_tensor(k5[:, :, :], gT[:, 2:4, 0:CH], v(e5k), ALU.mult).then_inc(s_gq, 1)

                def probs_mask(t, b):
                    need(dve, s_pvo, b)
                    for g in range(KVH):
                        hs = slice(g * GRP, (g + 1) * GRP)
                        need(dve, s_pt, b * 2 + 1 + g)
                        src = bank[(4, 6)[g]][:, :].rearrange("p (h k) -> p h k", h=GRP)
                        for dst, m in ((ptc, triT), (ptp, triN)):
                            dve.tensor_tensor(dst[:, hs, :], src, m[:, :].unsqueeze(1).broadcast_to([P, GRP, P]),
                                              ALU.mult).then_inc(s_ptm, 1)

                def step(t, h, u):
                    b, pr = t - 1, proj[1 - u]
                    front, back = has_front(t), has_back(t)
                    first = known(t) and b == 0
                    if has_xprep(t):
                        x_start(t + 1)
                    if back:
                        if first:
                            dve.wait_ge(s_zero, 7)
                            dve.wait_ge(s_msk, 5)
                        dve.wait_ge(s_evA, t * 3)
                        dve.wait_ge(s_evD, t * 3)
                        need(dve, s_gat, b)
                        for n, c in enumerate((ZAC, ZBC)):
                            dve.tensor_scalar(sil[:, n * 512:(n + 1) * 512], pr[:, c:c + 512], -1.0, BIG_ARG,
                                              ALU.mult, ALU.min).then_inc(s_slm, 1)
                        need(dve, s_t1, b * 3 + 2)
                        dve.tensor_copy(aT[:, :], bank[5][0:RANK, P:2 * P]).then_inc(s_kT, 1)
                        dve.tensor_copy(kT[1 - u][:, :], bank[5][:, 0:P]).then_inc(s_kT, 1)
                        if known(t) and t == NBLK:
                            unit_scales(dve)
                        need(dve, s_slt, b * 2 + 2)
                        for n, c in enumerate((ZAC, ZBC)):
                            dve.scalar_tensor_tensor(sil[:, n * 512:(n + 1) * 512], pr[:, c:c + 512], -1.0,
                                                     sil[:, n * 512:(n + 1) * 512], ALU.mult,
                                                     ALU.max).then_inc(s_sll, 1)
                    if front and not (known(t) and t == 0):
                        evac(t, u, 1)
                    if back:
                        need(dve, s_z, t)
                        for p in range(2):
                            dve.tensor_scalar(zs[:, p * P:(p + 1) * P], bank[2][:, p * P:(p + 1) * P],
                                              bal[:, p:p + 1], None, ALU.add).then_inc(s_zs, 1)
                        need(dve, s_zs, t * 2)
                        dve.tensor_scalar(sp_, zs, -1.0, BIG_ARG, ALU.mult, ALU.min).then_inc(s_spm, 1)
                        softmax_shift(t, b, first)
                    if has_xprep(t):
                        x_split(t + 1, 1 - u)
                    if back:
                        gate_sums(t, b)
                        if known(t) and t == NBLK:
                            split_piece(dve, 0, DVE_K, (0, 1, 2))
                        need(dve, s_es, t)
                        need(dve, s_ex, t * 8)
                        dve.tensor_tensor(den[:, :], rsum[:, :], es[:, :], ALU.add).then_inc(s_den, 1)
                        need(dve, s_den, b * 2 + 1)
                        dve.reciprocal(rden[:, :], den[:, :]).then_inc(s_den, 1)
                        probs_mask(t, b)
                        gla_factors(t, b)
                        if known(t) and t == NBLK:
                            split_piece(dve, 1, DVE_K, (0, 1, 2))
                    if front and not (known(t) and t == 0):
                        evac(t, u, 3)
                    if back:
                        need(dve, s_pvo, t)
                        need(dve, s_den, t * 2)
                        dve.tensor_tensor(brn[:, 0:512].rearrange("p (h d) -> p h d", h=HEADS),
                                          bank[7][:, :].rearrange("p (h d) -> p h d", h=HEADS),
                                          rden[:, :].unsqueeze(2).broadcast_to([P, HEADS, HD]),
                                          ALU.mult).then_inc(s_br, 1)
                        need(dve, s_at, t)
                        wait_carrier()
                        dve.copy_predicated(att[:, :, :],
                                            triT[:, :].bitcast(U32).unsqueeze(1).broadcast_to([P, BH, P]),
                                            bank[5][:, :].rearrange("p (h t) -> p h t", h=BH)).then_inc(s_am, 1)
                        if known(t) and t == NBLK:
                            split_piece(dve, 2, DVE_K, (0, 1, 2))
                    if front:
                        evac(t, u, 5)
                    if back:
                        need(dve, s_inc, t)
                        for p in range(2):
                            for hh in range(2):
                                r = slice(hh * BK, (hh + 1) * BK)
                                dve.scalar_tensor_tensor(
                                    state[r, p, hh, :], state[r, p, hh, :],
                                    e3[r, p * P + P - 1:p * P + P],
                                    bank[6][r, p * 256 + hh * BV:p * 256 + (hh + 1) * BV],
                                    ALU.mult, ALU.add).then_inc(s_st, 1)
                        rsqrt_start(dve, s_gss, t * 4, s_gv, ss4[:, :], var4[:, :], BV)
                        rsqrt_newton(dve, s_gt, b * 2, s_gn, b * 4, var4[:, :], y4[:, :], nt4[:, :], r4[:, :])
                        need(dve, s_gn, t * 4)
                        dve.tensor_tensor(brn[:, 512:].rearrange("p (h d) -> p h d", h=BH), og[:, :, :],
                                          r4[:, :].unsqueeze(2).broadcast_to([P, BH, BV]),
                                          ALU.mult).then_inc(s_br, 1)
                        need(dve, s_br, t * 2)
                        need(dve, s_sl, t * 2)
                        dve.tensor_tensor(brn, brn, sil, ALU.mult).then_inc(s_gat, 1)
                        need(dve, s_gat, t)
                        b2 = brn.rearrange("p (a n) -> p a n", a=2)
                        osc = oscale[:, bass.ds(b, 1), :].rearrange("p a b -> p (a b)")
                        dve.tensor_reduce(omax[:, :], b2, AX.X, ALU.max, apply_absolute_value=True
                                          ).then_inc(s_om, 1)
                        need(dve, s_om, b * 5 + 1)
                        dve.tensor_scalar(omax[:, :], omax[:, :], 1e-30, None, ALU.max).then_inc(s_om, 1)
                        need(dve, s_om, b * 5 + 2)
                        dve.tensor_scalar(omax[:, :].bitcast(U32), omax[:, :].bitcast(U32), 0x7F800000, None,
                                          ALU.bitwise_and).then_inc(s_om, 1)
                        need(dve, s_om, b * 5 + 3)
                        dve.tensor_scalar(opow[:, :], omax[:, :], 2.0 ** -10, None, ALU.mult).then_inc(s_om, 1)
                        need(dve, s_om, b * 5 + 4)
                        dve.tensor_copy(osc, opow[:, :])
                        dve.reciprocal(oinv[:, :], opow[:, :]).then_inc(s_om, 1)
                        need(dve, s_om, t * 5)
                        need(dve, s_otr, b)
                        for a in range(2):
                            dve.tensor_scalar(o16[:, 0, a * 512:(a + 1) * 512], b2[:, a], oinv[:, a:a + 1],
                                              None, ALU.mult).then_inc(s_o16, 1)
                        need(dve, s_o16, b * 4 + 2)
                        for a in range(2):
                            dve.scalar_tensor_tensor(o16[:, 1, a * 512:(a + 1) * 512], b2[:, a],
                                                     oinv[:, a:a + 1], o16[:, 0, a * 512:(a + 1) * 512],
                                                     ALU.mult, ALU.subtract).then_inc(s_o16, 1)

                steps(dve, step)
                for i in range(3, NPRE):
                    split_piece(dve, i, DVE_K, (0, 1, 2))

        with ExitStack() as bctx:
            def sc_(name, shape, dt=F32):
                return sb(name, shape, dt, bctx)

            fin = [tiles[:, 0, 0:D], tiles[:, 0, D:2 * D]]
            res = tiles[:, 1, 0:D]
            mT = fp16_parts(tiles[:, 1, D:2 * D])
            sg = [[sc_(f"sg{j}{a}", [P, 512])[:, :] for a in range(2)] for j in range(2)]
            ta = sc_("ta", [P, 512])[:, :]
            tb = sc_("tb", [P, 512])[:, :]
            gfin = sc_("gfin", [P, D])[:, :]
            mg = sc_("mg", [P, D])[:, :]
            wa1 = sc_("wa1", [P, 2, BH, D], F16)
            wo = sc_("wo", [P, 2, KT, D], F16)
            late[:] = [wa1, wo]
            hb = [hb0, sc_("hb1", [P, 2, KT, P], F16)]
            ob = [ob0, sc_("ob1", [P, 2, KT, P], F16)]
            xb = [sc_(f"xb{i}", [P, D]) for i in range(2)]
            m16 = sc_("m16", [P, 2, D], F16)
            junkb = sc_("junkb", [P, D], F16)
            ysc = sc_("ysc", [P, 2])
            mmax = sc_("mmax", [P, 1])
            msc = sc_("msc", [P, 1])
            minv = sc_("minv", [P, 1])
            rsc = sc_("rsc", [P, 1])

            s_xb = [sem("xb_even"), sem("xb_odd")]
            s_gf = sem("gfin_loaded")
            s_g = sem("gates")
            s_gm = sem("gates_clamped")
            s_gx = sem("gate_tables")
            s_gl = sem("gates_softplus")
            s_sg = sem("gates_sigmoid")
            s_y = sem("branch_products")
            s_ys = sem("branch_scales")
            s_yt = sem("branches_merging")
            s_mg = sem("merged")
            s_ms = sem("merged_scales")
            s_m16 = sem("merged_split")
            s_mt = sem("merged_transposed")
            s_mT = sem("mT_copied")
            s_rs = sem("out_scales")
            s_w = sem("out_products")
            s_r = sem("residual_added")
            s_fss = sem("final_square_sum")
            s_fv = sem("final_var")
            s_ft = sem("final_rsqrt_table")
            s_fn = sem("final_rsqrt_newton")
            s_fin = sem("finished")
            s_out = [sem("stored_even"), sem("stored_odd")]

            def stepsb(eng, step):
                for t in range(3):
                    step(t, t // 2, t % 2)
                with eng.Fori(0, (NBLK - 4) // 2) as i:
                    step(i * 2 + 3, i + 1, 1)
                    step(i * 2 + 4, i + 2, 0)
                step(NBLK - 1, NBLK // 2 - 1, 1)
                step(NBLK, NBLK // 2, 0)

            def frontb(t):
                return not isinstance(t, int) or t < NBLK

            def last_front(t):
                return isinstance(t, int) and t == NBLK - 1

            def tailb(t):
                return not isinstance(t, int) or t >= 1

            block = bctx.enter_context(nc.Block())

            @block.sync
            def _(sp):
                def load(t, h, u):
                    need(sp, s_y, (t - 1) * 4)
                    if not (known(t) and t == 0):
                        sp.dma_start(hb[u][:, :, :, :].rearrange("p a k t -> p (a k t)"),
                                     hts[bass.ds(t, 1)].rearrange("a p n -> (a p) n")).then_inc(s_hb[u], 16)
                        sp.dma_start(ob[u][:, :, :, :].rearrange("p a k t -> p (a k t)"),
                                     ots[bass.ds(t, 1)].rearrange("a p n -> (a p) n")).then_inc(s_ob[u], 16)
                    need(sp, s_r, (t - 1) * 2)
                    sp.dma_start(xb[u][:, :], x[bass.ds(t * P, P), :]).then_inc(s_xb[u], 16)

                load(0, 0, 0)
                load(1, 0, 1)
                for i in range(NPRE + 3, NP_):
                    load_piece(sp, i)
                sp.dma_start(gfin, g_final.partition_broadcast(P)).then_inc(s_gf, 16)

                def step(t, h, u):
                    if not isinstance(t, int) or 2 <= t + 1 < NBLK:
                        load(t + 1, h + u, 1 - u)
                    if tailb(t):
                        need(sp, s_fin, t)
                        sp.dma_start(out[bass.ds((t - 1) * P, P), :], fin[1 - u]).then_inc(s_out[1 - u], 16)

                stepsb(sp, step)
                for s in s_out:
                    sp.wait_ge(s, 16 * (NBLK // 2))

            @block.gpsimd
            def _(pool):
                def merge_sum(t, j):
                    need(pool, s_yt, t * 4 + 2 * j + 2)
                    need(pool, s_m16, t * 2)
                    pool.tensor_tensor(mg[:, j * 512:(j + 1) * 512], ta, tb, ALU.add).then_inc(s_mg, 1)

                def step(t, h, u):
                    if isinstance(t, int) and t == 0:
                        for i in range(NPRE, NP_):
                            split_piece_pool(pool, i)
                            if i in (9, 12):
                                merge_sum(0, i // 12)
                    elif frontb(t):
                        for j in range(2):
                            merge_sum(t, j)

                stepsb(pool, step)

            @block.scalar
            def _(act):
                act.preload_act_table_set("natural_log_exp_and_others")

                def sigmoids(t, j):
                    for a in range(2):
                        n = 2 * j + a
                        need(act, s_gm, t * 4 + n + 1)
                        act.activation(sg[j][a], sg[j][a], ACT.Exp).then_inc(s_gx, 1)
                        need(act, s_gx, t * 8 + 2 * n + 1)
                        act.activation(sg[j][a], sg[j][a], ACT.Ln, bias=1.0).then_inc(s_gx, 1)
                    for a in range(2):
                        need(act, s_gl, t * 4 + 2 * j + a + 1)
                        act.activation(sg[j][a], sg[j][a], ACT.Exp, scale=-1.0).then_inc(s_sg, 1)

                def step(t, h, u):
                    if isinstance(t, int) and t == 0:
                        for i in range(NPRE, NP_):
                            split_piece(act, i, ACT_K, ())
                            if i == 7:
                                sigmoids(0, 0)
                            elif i == 11:
                                sigmoids(0, 1)
                        return
                    if frontb(t):
                        sigmoids(t, 0)
                    if tailb(t):
                        if known(t) and t == 1:
                            act.wait_ge(s_plo[1], 14)
                        need(act, s_mt, t)
                        need(act, s_w, (t - 1) * 2)
                        for a in range(2):
                            act.activation(mT[:, a].rearrange("p k t -> p (k t)"),
                                           bank[4 + a][:, :].bitcast(F16), ACT.Copy).then_inc(s_mT, 1)
                    if frontb(t):
                        sigmoids(t, 1)
                    if tailb(t):
                        need(act, s_r, t * 2)
                        act.activation(junkb[:, :], res, ACT.Square, accum_out=ss[:, :]).then_inc(s_fss, 1)
                        rsqrt_table(act, s_fv, t, s_ft, (t - 1) * 2, var[:, :], lnv[:, :], y0[:, :])

                stepsb(act, step)

            @block.tensor
            def _(pe):
                def split(m, j):
                    for s in s_plo:
                        pe.wait_ge(s, max(i + 1 for i, p in enumerate(PIECES) if p[:2] == (m, j)))

                def gate(t, u, j, a):
                    if isinstance(t, int) and t == 0:
                        split(GA + a, j)
                    n = 2 * j + a
                    need(pe, s_gl, t * 4 + n - 1 if n >= 2 else (t - 1) * 4 + n + 3)
                    col = a * D + j * 512
                    for i in range(3 * KT):
                        k, s = divmod(i, 3)
                        l, r = ((0, 0), (0, 1), (1, 0))[s]
                        last = pe.matmul(bank[a][:, :], hb[u][:, l, k, :], gh[:, r, k, col:col + 512],
                                         start=i == 0, stop=i == 3 * KT - 1)
                    last.then_inc(s_g, 1)

                def branch(t, u, j, a):
                    if isinstance(t, int) and t == 0:
                        split(OA + a, j)
                    n = 2 * j + a
                    need(pe, s_yt, t * 4 + n - 1 if n >= 2 else (t - 1) * 4 + n + 3)
                    for i in range(3 * BH):
                        k, s = divmod(i, 3)
                        l, r = ((0, 0), (0, 1), (1, 0))[s]
                        last = pe.matmul(bank[2 + a][:, :], ob[u][:, l, a * BH + k, :],
                                         (wa0, wa1)[a][:, r, k, j * 512:(j + 1) * 512], start=i == 0,
                                         stop=i == 3 * BH - 1)
                    last.then_inc(s_y, 1)

                def merged_turn(t):
                    need(pe, s_m16, t * 2)
                    need(pe, s_mT, (t - 1) * 2)
                    for a in range(2):
                        dst = bank[4 + a][:, :].bitcast(F16)
                        for k in range(KT):
                            last = pe.transpose(dst[:, k * P:(k + 1) * P], m16[:, a, k * P:(k + 1) * P],
                                                ident16[:, :])
                    last.then_inc(s_mt, 1)

                def final(t, j):
                    if isinstance(t, int) and t == 1:
                        split(WO, j)
                    need(pe, s_mT, t * 2)
                    need(pe, s_r, (t - 1) * 2)
                    for i in range(3 * KT):
                        k, s = divmod(i, 3)
                        l, r = ((0, 0), (0, 1), (1, 0))[s]
                        last = pe.matmul(bank[6 + j][:, :], mT[:, l, k, :], wo[:, r, k, j * 512:(j + 1) * 512],
                                         start=i == 0, stop=i == 3 * KT - 1)
                    last.then_inc(s_w, 1)

                def step(t, h, u):
                    if frontb(t):
                        need(pe, s_hb[u], 16 * h + 16)
                        gate(t, u, 0, 0)
                        gate(t, u, 0, 1)
                    if tailb(t):
                        merged_turn(t)
                    if frontb(t):
                        need(pe, s_ob[u], 16 * h + 16)
                        branch(t, u, 0, 0)
                        branch(t, u, 0, 1)
                    if tailb(t) and not last_front(t):
                        final(t, 0)
                        final(t, 1)
                    if frontb(t):
                        for a in range(2):
                            gate(t, u, 1, a)
                        for a in range(2):
                            branch(t, u, 1, a)
                    if last_front(t):
                        final(t, 0)
                        final(t, 1)

                stepsb(pe, step)

            @block.vector
            def _(dve):
                def softplus_gates(t, j):
                    for a in range(2):
                        n = 2 * j + a
                        need(dve, s_g, t * 4 + n + 1)
                        need(dve, s_yt, (t - 1) * 4 + n + 1)
                        ng = ngs[:, a:a + 1]
                        dve.tensor_scalar(sg[j][a], bank[a][:, :], ng, BIG_ARG, ALU.mult,
                                          ALU.min).then_inc(s_gm, 1)
                    for a in range(2):
                        n = 2 * j + a
                        ng = ngs[:, a:a + 1]
                        need(dve, s_gx, t * 8 + 2 * n + 2)
                        dve.scalar_tensor_tensor(sg[j][a], bank[a][:, :], ng, sg[j][a], ALU.mult,
                                                 ALU.max).then_inc(s_gl, 1)

                def merge(t, j):
                    for a, o in ((0, ta), (1, tb)):
                        n = 2 * j + a
                        need(dve, s_y, t * 4 + n + 1)
                        need(dve, s_sg, t * 4 + n + 1)
                        need(dve, s_mg, t * 2 + j)
                        dve.scalar_tensor_tensor(o, bank[2 + a][:, :], ysc[:, a:a + 1], sg[j][a], ALU.mult,
                                                 ALU.mult).then_inc(s_yt, 1)

                def split_merged(t):
                    need(dve, s_mg, t * 2 + 2)
                    dve.tensor_reduce(mmax[:, :], mg, AX.X, ALU.max, apply_absolute_value=True
                                      ).then_inc(s_ms, 1)
                    need(dve, s_ms, t * 5 + 1)
                    dve.tensor_scalar(mmax[:, :], mmax[:, :], 1e-30, None, ALU.max).then_inc(s_ms, 1)
                    need(dve, s_ms, t * 5 + 2)
                    dve.tensor_scalar(mmax[:, :].bitcast(U32), mmax[:, :].bitcast(U32), 0x7F800000, None,
                                      ALU.bitwise_and).then_inc(s_ms, 1)
                    need(dve, s_ms, t * 5 + 3)
                    dve.tensor_scalar(msc[:, :], mmax[:, :], 2.0 ** -10, None, ALU.mult).then_inc(s_ms, 1)
                    need(dve, s_ms, t * 5 + 4)
                    dve.reciprocal(minv[:, :], msc[:, :]).then_inc(s_ms, 1)
                    need(dve, s_ms, t * 5 + 5)
                    need(dve, s_mt, t)
                    dve.tensor_scalar(m16[:, 0], mg, minv[:, 0:1], None, ALU.mult).then_inc(s_m16, 1)
                    need(dve, s_m16, t * 2 + 1)
                    dve.scalar_tensor_tensor(m16[:, 1], mg, minv[:, 0:1], m16[:, 0], ALU.mult,
                                             ALU.subtract).then_inc(s_m16, 1)

                def branch_scales(t):
                    dve.tensor_tensor(ysc[:, :], oscale[:, bass.ds(t, 1), :].rearrange("p a b -> p (a b)"),
                                      uscale[:, OA:OB + 1], ALU.mult).then_inc(s_ys, 1)
                    need(dve, s_ys, t + 1)

                def add_residual(t, h, u):
                    need(dve, s_rs, t)
                    need(dve, s_xb[1 - u], 16 * (h + u))
                    need(dve, s_fn, (t - 1) * 4)
                    need(dve, s_fin, t - 1)
                    for j in range(2):
                        need(dve, s_w, (t - 1) * 2 + j + 1)
                        dve.scalar_tensor_tensor(res[:, j * 512:(j + 1) * 512], bank[6 + j][:, :],
                                                 rsc[:, 0:1], xb[1 - u][:, j * 512:(j + 1) * 512],
                                                 ALU.mult, ALU.add).then_inc(s_r, 1)

                def step0():
                    for i in range(NPRE, NP_):
                        split_piece(dve, i, DVE_K, (0, 1, 2))
                        if i == 7:
                            softplus_gates(0, 0)
                        elif i == 9:
                            branch_scales(0)
                            merge(0, 0)
                        elif i == 11:
                            softplus_gates(0, 1)
                        elif i == 12:
                            merge(0, 1)
                        elif i == 13:
                            split_merged(0)

                def step(t, h, u):
                    if isinstance(t, int) and t == 0:
                        step0()
                        return
                    front, tail = frontb(t), tailb(t)
                    if front:
                        softplus_gates(t, 0)
                        branch_scales(t)
                        merge(t, 0)
                    if tail:
                        dve.tensor_tensor(rsc[:, :], uscale[:, WO:WO + 1], msc[:, :], ALU.mult).then_inc(s_rs, 1)
                    if tail and not last_front(t):
                        add_residual(t, h, u)
                    if front:
                        softplus_gates(t, 1)
                        merge(t, 1)
                        split_merged(t)
                    if last_front(t):
                        add_residual(t, h, u)
                    if tail:
                        rsqrt_start(dve, s_fss, t, s_fv, ss[:, :], var[:, :], D)
                        rsqrt_newton(dve, s_ft, (t - 1) * 2, s_fn, (t - 1) * 4, var[:, :], y0[:, :],
                                     nt[:, 0:1], rstd[:, :])
                        need(dve, s_fn, t * 4)
                        need(dve, s_out[1 - u], 16 * (h - 1 + u))
                        if isinstance(t, int) and t == 1:
                            dve.wait_ge(s_gf, 16)
                        dve.scalar_tensor_tensor(fin[1 - u], res, rstd[:, 0:1], gfin, ALU.mult,
                                                 ALU.mult).then_inc(s_fin, 1)

                stepsb(dve, step)


_INS = ["x", "positions", "g_in", "w_branch", "w_units", "w_alpha_up", "b_alpha", "attn_sinks",
        "g_gla_norm", "g_final"]


def kernel(**inputs):
    import numpy as _np
    import concourse.bacc as _bacc
    from concourse import mybir as _mybir
    from concourse.bass_utils import run_bass_kernel_spmd as _run

    nc = _bacc.Bacc("TRN2", target_bir_lowering=False, num_devices=1)
    arrays, args = {}, []
    laid = {k: _np.asarray(v) if k == "g_final" else _np.asarray(v)[0] for k, v in inputs.items()}
    for k in ("positions", "g_in", "g_gla_norm", "b_alpha"):
        laid[k] = laid[k].reshape(-1, P).T
    w_in = laid["w_in"]
    laid["w_branch"] = w_in[:, :NA]
    laid["w_units"] = _np.concatenate([w_in[:, NA:NA + D], w_in[:, NA + D:], laid["w_out_a"],
                                       laid["w_out_b"], laid["w_o"]]).reshape(NU, P, D)
    for name in _INS:
        a = _np.ascontiguousarray(laid[name])
        arrays[f"in_{name}_dram"] = a
        args.append(nc.dram_tensor(f"in_{name}_dram", a.shape, _mybir.dt.from_np(a.dtype),
                                   kind="ExternalInput").ap())
    out = nc.dram_tensor("out_0_dram", (SEQ, D), _mybir.dt.float32, kind="ExternalOutput").ap()
    hybrid_block(nc, *args, out)
    r = _run(nc, [arrays], core_ids=[0])
    return r.results[0]["out_0_dram"].reshape(1, SEQ, D)
```

```python
from contextlib import ExitStack

import numpy as np
import concourse.bass as bass
from concourse import mybir

ALU = mybir.AluOpType
ACT = mybir.ActivationFunctionType
AX = mybir.AxisListType
F32 = mybir.dt.float32
F16 = mybir.dt.float16
I32 = mybir.dt.int32
U32 = mybir.dt.uint32
RADD = bass.bass_isa.ReduceOp.add

P = 128
D = 1024
KT = D // P
SEQ = 4096
NBLK = SEQ // P
HEADS, KVH, HD = 8, 2, 64
GRP = HEADS // KVH
HALF = HD // 8
THETA = 500000.0
BH, BK, BV = 4, 64, 128
RANK = 16
CH = 64
EPS = 1e-6
NEG = -3e38
PSCALE = 2.0 ** 14
BIG_ARG = 40.0
MAGIC = 12582912.0
ROPE_OPS = 18

QC, KC, VC, ZAC = 0, 512, 640, 768
QBC, KBC, VBC, ZBC, ALC = 1280, 1536, 1792, 2304, 2816
NA = ALC + RANK
NCONST = 5
CHUNKS = [(c, min(c + 512, NA)) for c in range(0, NA, 512)]
NCH = len(CHUNKS)
GATE_U, OUT_U, WO_U, NU = 0, 2 * KT, 2 * KT + 8, 3 * KT + 8
GA, GB, OA, OB, WO = range(5)
MAT_UNITS = {GA: (0, KT), GB: (KT, KT), OA: (OUT_U, 4), OB: (OUT_U + 4, 4), WO: (WO_U, KT)}
PIECES = [(GA, 0, 0), (GA, 0, 1), (GB, 0, 0), (GB, 0, 1), (OA, 0, 0), (GA, 1, 0), (GA, 1, 1),
          (OB, 0, 0), (GB, 1, 0), (GB, 1, 1), (OA, 1, 0), (OB, 1, 0),
          (WO, 0, 0), (WO, 0, 1), (WO, 1, 0), (WO, 1, 1)]
PK = 4


def two_pi_parts():
    rest, parts = 2 * np.pi, []
    for _ in range(2):
        e = np.floor(np.log2(rest))
        unit = 2.0 ** (e - 11)
        c = np.floor(rest / unit) * unit
        parts.append(float(c))
        rest -= c
    return parts + [float(np.float32(rest))]


def need(eng, sem, n):
    if isinstance(n, int) and n <= 0:
        return
    eng.wait_ge(sem, n)


def hybrid_block(nc, x, positions, g_in, w_branch, w_units, w_alpha_up, b_alpha, attn_sinks, g_gla_norm,
                 g_final, out):
    with ExitStack() as ctx:
        def sb(name, shape, dt=F32, stack=ctx):
            return stack.enter_context(nc.sbuf_tensor(name, shape, dt))

        def sem(name):
            return ctx.enter_context(nc.semaphore(name))

        bank = [ctx.enter_context(nc.psum_tensor(f"bank{i}", [P, 512], F32)) for i in range(8)]
        hts = nc.dram_tensor("hts", [NBLK, P, 2 * KT * P], F16, kind="Internal").ap()
        ots = nc.dram_tensor("ots", [NBLK, P, 2 * D], F16, kind="Internal").ap()

        ident = sb("ident", [P, P])
        gain = sb("gain", [P, NU])
        wscale = sb("wscale", [P, NCH])
        usq = sb("usq", [P, NU])
        oscale = sb("oscale", [P, NBLK, 2])
        ss = sb("ss", [P, 1])
        var = sb("var", [P, 1])
        lnv = sb("lnv", [P, 1])
        y0 = sb("y0", [P, 1])
        nt = sb("nt", [P, 2])
        rstd = sb("rstd", [P, 1])

        weights = sb("weights", [P, 2 * KT * NA], F16)
        tiles = sb("tiles", [P, 3, PK * 512])
        usum = sb("usum", [P, 5])
        uall = sb("uall", [P, 5])
        upow = sb("upow", [P, 5])
        uscale = sb("uscale", [P, 5])
        uinv = sb("uinv", [P, 5])
        ngs = sb("ngs", [P, 2])
        ugi = sb("ugi", [P, NU])

        def fp16_parts(ap):
            return ap.bitcast(F16).rearrange("p (a k t) -> p a k t", a=2, k=KT)

        GH, WA, OPER = 2 * KT * 2 * D, 2 * BH * D, 2 * KT * P
        gh = weights[:, 0:GH].rearrange("p (a k n) -> p a k n", a=2, k=KT)
        wa0 = weights[:, GH:GH + WA].rearrange("p (a k n) -> p a k n", a=2, k=BH)
        hb0 = weights[:, GH + WA:GH + WA + OPER].rearrange("p (a k t) -> p a k t", a=2, k=KT)
        ob0 = weights[:, GH + WA + OPER:GH + WA + 2 * OPER].rearrange("p (a k t) -> p a k t", a=2, k=KT)

        s_usq = sem("unit_squares")
        s_pj = sem("projected")
        s_us = sem("unit_sums")
        s_ua = sem("unit_sums_over_rows")
        s_uc = sem("unit_scales")
        s_pr = [sem(f"piece_loaded_{i}") for i in range(3)]
        s_phi = [sem("piece_hi_by_scalar"), sem("piece_hi_by_vector")]
        s_pps = sem("piece_scaled_by_pool")
        s_plo = [sem("piece_lo_by_vector"), sem("piece_lo_by_pool")]
        s_g = sem("gates")
        s_hb = [sem("hb_even"), sem("hb_odd")]
        s_ob = [sem("ob_even"), sem("ob_odd")]

        s_const = sem("const_loaded")
        s_gin = sem("g_in_loaded")
        s_pos = sem("positions_loaded")
        s_id = sem("identities")
        s_msk = sem("masks")
        s_gain = sem("gains")

        def power_of_two(dve, total, pw, scale, inv, s, n):
            dve.tensor_scalar(pw, total, 1e-30, None, ALU.max).then_inc(s, 1)
            dve.wait_ge(s, n + 1)
            dve.tensor_scalar(pw.bitcast(U32), pw.bitcast(U32), 1, 0x7F800000, ALU.logical_shift_right,
                              ALU.bitwise_and).then_inc(s, 1)
            dve.wait_ge(s, n + 2)
            dve.tensor_scalar(scale, pw, 2.0 ** (64 - 14), None, ALU.mult).then_inc(s, 1)
            dve.wait_ge(s, n + 3)
            dve.reciprocal(inv, scale).then_inc(s, 1)

        def rsqrt_start(dve, s_ss, n, s_v, total, v, width):
            need(dve, s_ss, n)
            dve.tensor_scalar(v, total, 1.0 / width, EPS, ALU.mult, ALU.add).then_inc(s_v, 1)

        def rsqrt_table(act, s_v, n, s_t, k, v, ln, y):
            need(act, s_v, n)
            act.activation(ln, v, ACT.Ln).then_inc(s_t, 1)
            need(act, s_t, k + 1)
            act.activation(y, ln, ACT.Exp, scale=-0.5).then_inc(s_t, 1)

        def rsqrt_newton(dve, s_t, k, s_n, m, v, y, t, r):
            need(dve, s_t, k + 2)
            dve.tensor_tensor(t, y, y, ALU.mult).then_inc(s_n, 1)
            need(dve, s_n, m + 1)
            dve.tensor_tensor(t, t, v, ALU.mult).then_inc(s_n, 1)
            need(dve, s_n, m + 2)
            dve.tensor_scalar(t, t, -0.5, 1.5, ALU.mult, ALU.add).then_inc(s_n, 1)
            need(dve, s_n, m + 3)
            dve.tensor_tensor(r, y, t, ALU.mult).then_inc(s_n, 1)

        def raw_piece(i):
            return tiles[:, i % 3, :].rearrange("p (k n) -> p k n", k=PK)

        late = [None, None]

        def piece_parts(i):
            m, j, q = PIECES[i]
            c, ks = slice(j * 512, (j + 1) * 512), slice(q * PK, (q + 1) * PK)
            if m in (GA, GB):
                c = slice(m * D + j * 512, m * D + (j + 1) * 512)
                w = gh
            else:
                w = {OA: wa0, OB: late[0], WO: late[1]}[m]
            return MAT_UNITS[m][0] + q * PK, w[:, 0, ks, c], w[:, 1, ks, c]

        def load_piece(sp, i):
            m, j, q = PIECES[i]
            u0 = MAT_UNITS[m][0] + q * PK
            for s in s_plo:
                need(sp, s, i - 2)
            sp.dma_start(raw_piece(i), w_units[u0:u0 + PK, :, j * 512:(j + 1) * 512]
                         .rearrange("k p n -> p k n")).then_inc(s_pr[i % 3], 16)

        def split_piece(eng, i, hi_ks, lo_ks):
            u0, hi, lo = piece_parts(i)
            eng.wait_ge(s_pr[i % 3], 16 * (i // 3 + 1))
            if i == 0:
                eng.wait_ge(s_uc, 8)
                eng.wait_ge(s_pj, NBLK * NCH)
            for k in hi_ks:
                g = ugi[:, u0 + k:u0 + k + 1]
                if hi_ks is ACT_K:
                    last = eng.activation(hi[:, k], raw_piece(i)[:, k, :], ACT.Copy, scale=g)
                else:
                    last = eng.tensor_scalar(hi[:, k], raw_piece(i)[:, k, :], g, None, ALU.mult)
            if hi_ks:
                last.then_inc(s_phi[0 if hi_ks is ACT_K else 1], 1)
            if lo_ks:
                eng.wait_ge(s_phi[0], i + 1)
                eng.wait_ge(s_phi[1], i + 1)
                for k in lo_ks:
                    last = eng.scalar_tensor_tensor(lo[:, k], raw_piece(i)[:, k, :],
                                                    ugi[:, u0 + k:u0 + k + 1], hi[:, k], ALU.mult,
                                                    ALU.subtract)
                last.then_inc(s_plo[0], 1)

        def split_piece_pool(pool, i):
            u0, hi, lo = piece_parts(i)
            k = PK - 1
            pool.wait_ge(s_phi[1], i + 1)
            pool.tensor_scalar(raw_piece(i)[:, k, :], raw_piece(i)[:, k, :], ugi[:, u0 + k:u0 + k + 1], None,
                               ALU.mult).then_inc(s_pps, 1)
            pool.wait_ge(s_pps, i + 1)
            pool.tensor_tensor(lo[:, k], raw_piece(i)[:, k, :], hi[:, k], ALU.subtract).then_inc(s_plo[1], 1)

        ACT_K, DVE_K = (0, 1), (2, 3)

        def pieces_split(pe, m, j):
            for s in s_plo:
                pe.wait_ge(s, max(i + 1 for i, p in enumerate(PIECES) if p[:2] == (m, j)))

        def gate_products(pe, operand, j, a):
            col = a * D + j * 512
            for i in range(3 * KT):
                k, s = divmod(i, 3)
                l, r = ((0, 0), (0, 1), (1, 0))[s]
                last = pe.matmul(bank[a][:, :], operand[:, l, k, :], gh[:, r, k, col:col + 512],
                                 start=i == 0, stop=i == 3 * KT - 1)
            last.then_inc(s_g, 1)
        NP_ = len(PIECES)
        NPRE = 7

        def unit_scales(dve):
            dve.wait_ge(s_usq, NU)
            dve.tensor_reduce(usum[:, GA:GB + 1], usq[:, 0:OUT_U].rearrange("p (m k) -> p m k", k=KT),
                              AX.X, ALU.add).then_inc(s_us, 1)
            dve.tensor_reduce(usum[:, OA:OB + 1], usq[:, OUT_U:WO_U].rearrange("p (m k) -> p m k", k=4),
                              AX.X, ALU.add).then_inc(s_us, 1)
            dve.tensor_reduce(usum[:, WO:WO + 1], usq[:, WO_U:NU], AX.X, ALU.add).then_inc(s_us, 1)
            dve.wait_ge(s_ua, 1)
            power_of_two(dve, uall[:, :], upow[:, :], uscale[:, :], uinv[:, :], s_uc, 0)
            dve.wait_ge(s_uc, 4)
            dve.tensor_scalar(ngs[:, :], uscale[:, GA:GB + 1], -1.0, None, ALU.mult).then_inc(s_uc, 1)
            for m, w in ((GA, KT), (OA, 4)):
                u0, n = MAT_UNITS[m][0], 2 * w
                dve.tensor_tensor(ugi[:, u0:u0 + n].rearrange("p (m k) -> p m k", m=2),
                                  gain[:, u0:u0 + n].rearrange("p (m k) -> p m k", m=2),
                                  uinv[:, m:m + 2].unsqueeze(2).broadcast_to([P, 2, w]),
                                  ALU.mult).then_inc(s_uc, 1)
            dve.tensor_tensor(ugi[:, WO_U:NU], gain[:, WO_U:NU],
                              uinv[:, WO:WO + 1].broadcast_to([P, KT]), ALU.mult).then_inc(s_uc, 1)

        with ExitStack() as actx:
            def sa(name, shape, dt=F32):
                return sb(name, shape, dt, actx)

            wh = weights[:, 0:KT * NA].rearrange("p (k n) -> p k n", k=KT)
            wl = weights[:, KT * NA:].rearrange("p (k n) -> p k n", k=KT)
            arena = sa("arena", [P, 2, 4096])
            scs = arena[:, 0, 0:1024].rearrange("p (h k) -> p h k", h=HEADS)
            ptc = arena[:, 0, 1024:2048].bitcast(F16).rearrange("p (a h k) -> p a h k", a=2, h=HEADS)
            ptp = arena[:, 0, 2048:3072].bitcast(F16).rearrange("p (a h k) -> p a h k", a=2, h=HEADS)
            sil = arena[:, 0, 3072:4096]
            brn = arena[:, 1, 0:1024]
            e1 = arena[:, 1, 1024:1280]
            e2 = arena[:, 1, 1280:1536]
            e3 = arena[:, 1, 1536:1792]
            e4 = arena[:, 1, 1792:2048]
            e5q = arena[:, 1, 2048:2176]
            e5k = arena[:, 1, 2176:2304]
            d1 = arena[:, 1, 2304:2560]
            d3 = arena[:, 1, 2560:2816]
            d4 = arena[:, 1, 2816:3072]
            d5 = arena[:, 1, 3072:3200]
            zs = arena[:, 1, 3200:3456]
            sp_ = arena[:, 1, 3456:3712]
            gsp = arena[:, 1, 3712:3968]
            k5 = arena[:, 1, 3968:4096].rearrange("p (a c) -> p a c", a=2)

            proj = [sa(f"proj{i}", [P, NA]) for i in range(2)]
            xin = [tiles[:, 0, 0:D], tiles[:, 0, D:2 * D]]
            hT = [fp16_parts(tiles[:, 1, 0:D]), fp16_parts(tiles[:, 2, 0:D])]
            x16 = tiles[:, 1, D:2 * D].bitcast(F16).rearrange("p (a n) -> p a n", a=2)
            unit = tiles[:, 2, D:2 * D]
            junk = sa("junk", [P, D], F16)
            qs = sa("qs", [P, KVH, GRP, P], F16)
            ks = [sa(f"ks{i}", [P, KVH, P], F16) for i in range(2)]
            kl = [sa(f"kl{i}", [P, P], F16) for i in range(2)]
            qkin = sa("qkin", [P, 2])
            ssc = sa("ssc", [P, 1])
            ssh = sa("ssh", [P, 2])
            pvsc = sa("pvsc", [P, 1])
            aT = sa("aT", [RANK, P])
            vbuf = [sa(f"vbuf{i}", [P, 2, P], F16) for i in range(2)]
            gT = sa("gT", [P, 4, P])
            q1 = sa("q1", [P, 2, 2, P])
            q5 = sa("q5", [P, 2, 2, CH])
            q3 = sa("q3", [P, 2, P])
            k1 = sa("k1", [P, 2, P])
            k4 = sa("k4", [P, 2, P])
            k2 = sa("k2", [P, 2, P])
            cum = sa("cum", [P, 2, 2, CH])
            carry = sa("carry", [P, 2, 2])
            seg = sa("seg", [P, 4, CH])
            att = sa("att", [P, BH, P])
            state = sa("state", [P, 2, 2, BV])
            og = sa("og", [P, BH, BV])
            o16 = sa("o16", [P, 2, D], F16)
            tri = sa("tri", [P, P])
            triT = sa("triT", [P, P])
            triT16 = sa("triT16", [P, P], F16)
            triN16 = sa("triN16", [P, P], F16)
            cosT = sa("cosT", [P, NBLK, HALF])
            sinT = sa("sinT", [P, NBLK, HALF])
            rt = sa("rt", [P, 4, HEADS + KVH, HALF])
            sinks = sa("sinks", [P, HEADS])
            wal = sa("wal", [RANK, 2 * P])
            bal = sa("bal", [P, 2])
            mx = sa("mx", [P, HEADS])
            mm = sa("mm", [P, HEADS])
            nm = sa("nm", [P, HEADS])
            dsk = sa("dsk", [P, HEADS])
            es = sa("es", [P, HEADS])
            rsum = sa("rsum", [P, HEADS])
            den = sa("den", [P, HEADS])
            rden = sa("rden", [P, HEADS])
            ss4 = sa("ss4", [P, BH])
            var4 = sa("var4", [P, BH])
            ln4 = sa("ln4", [P, BH])
            y4 = sa("y4", [P, BH])
            nt4 = sa("nt4", [P, BH])
            r4 = sa("r4", [P, BH])
            omax = sa("omax", [P, 2])
            oinv = sa("oinv", [P, 2])
            opow = sa("opow", [P, 2])
            tick = sa("tick", [P, 2])

            ang = proj[1][:, 0:256]
            turns = [proj[1][:, 256 * i:256 * (i + 1)] for i in range(1, 4)]
            pos_i = proj[1][:, 1024:1024 + NBLK].bitcast(I32)
            pos_f = proj[1][:, 1056:1056 + NBLK]
            wsq = sa("wsq", [P, NCH, KT])
            wsum = sa("wsum", [P, NCH])
            wall = sa("wall", [P, NCH])
            wpow = sa("wpow", [P, NCH])
            winv = sa("winv", [P, NCH])
            wgi = sa("wgi", [P, NCH, KT])

            s_raw = [[sem(f"raw_{e}_{half}") for half in ("first", "last")] for e in ("even", "odd")]
            s_wsq = sem("w_squares")
            s_wsum = sem("w_square_sum")
            s_wall = sem("w_sum_over_rows")
            s_wsm = sem("w_scales")
            s_whi = [sem("w_hi_by_scalar"), sem("w_hi_by_vector")]
            s_wps = sem("w_scaled_by_pool")
            s_wlo = [sem("w_lo_by_vector"), sem("w_lo_by_pool")]
            s_ub = sem("unit_loaded")
            s_x = [sem("x_even"), sem("x_odd")]
            s_xss = sem("x_square_sum")
            s_xv = sem("x_var")
            s_xt = sem("x_rsqrt_table")
            s_xn = sem("x_rsqrt_newton")
            s_x16 = sem("x_split")
            s_hT = sem("x_transposed")
            s_hst = [sem("hT_stored_even"), sem("hT_stored_odd")]
            s_evA = sem("evac_by_scalar")
            s_evD = sem("evac_by_vector")
            s_vh = sem("v_hi")
            s_vb = sem("v_lo")
            s_rm = sem("rope_products")
            s_rp = sem("roped")
            s_t1 = sem("qk_transposed")
            s_qk = sem("qk_scales")
            s_qT = sem("q_hi")
            s_kh = sem("k_hi")
            s_ql = sem("q_lo")
            s_kT = sem("aT_copied_k_lo")
            s_gT = sem("gT_copied")
            s_z = sem("forget_logits")
            s_zs = sem("forget_logits_copied")
            s_spm = sem("softplus_clamped")
            s_spt = sem("softplus_table")
            s_sp = sem("softplus")
            s_cum = sem("gate_sums")
            s_car = sem("gate_carry")
            s_dif = sem("gate_differences")
            s_e = sem("gate_exps")
            s_gq = sem("gla_queries")
            s_gk = sem("gla_keys")
            s_sc = sem("scores")
            s_pv0 = sem("previous_scores_copied")
            s_sel = sem("scores_selected")
            s_mx = sem("row_maxima")
            s_sm = sem("softmax_shift")
            s_es = sem("sink_exps")
            s_ex = sem("score_exps")
            s_den = sem("denominators")
            s_pt = sem("probs_transposed")
            s_pth = sem("probs_hi")
            s_ptl = sem("probs_lo")
            s_ptm = sem("probs_masked")
            s_at = sem("gla_scores")
            s_am = sem("gla_scores_masked")
            s_pvo = sem("attention_out")
            s_kt = sem("gla_keys_turned")
            s_k2 = sem("gla_keys_copied")
            s_go = sem("gla_out")
            s_inc = sem("state_increment")
            s_st = sem("state_updated")
            s_og = sem("gla_out_copied")
            s_gss = sem("gla_square_sum")
            s_gv = sem("gla_var")
            s_gt = sem("gla_rsqrt_table")
            s_gn = sem("gla_rsqrt_newton")
            s_slm = sem("silu_clamped")
            s_slt = sem("silu_tables")
            s_sll = sem("silu_softplus")
            s_sle = sem("silu_sigmoid")
            s_sl = sem("silu")
            s_br = sem("branches_normed")
            s_gat = sem("branches_gated")
            s_om = sem("out_maxima")
            s_o16 = sem("out_split")
            s_ost = sem("out_stored")
            s_rope = sem("rotary_angles")
            s_trig = sem("rotary_tables")
            s_zero = sem("cleared")

            stage = [arena[:, i, :] for i in range(2)]

            def raw(n):
                a, b = CHUNKS[n]
                return stage[n % 2][:, 0:KT * (b - a)].rearrange("p (k n) -> p k n", k=KT)

            def load_chunk(sp, n):
                a, b = CHUNKS[n]
                for s in s_wlo:
                    need(sp, s, n - 1)
                for half in range(2):
                    k = slice(half * KT // 2, (half + 1) * KT // 2)
                    sp.dma_start(raw(n)[:, k], w_branch[half * D // 2:(half + 1) * D // 2, a:b]
                                 .rearrange("(k p) n -> p k n", p=P)).then_inc(s_raw[n % 2][half], 16)

            def chunk_squares(act, n):
                a, b = CHUNKS[n]
                for k in range(KT):
                    if k % (KT // 2) == 0:
                        act.wait_ge(s_raw[n % 2][2 * k // KT], 16 * (n // 2 + 1))
                    last = act.activation(wh[:, k, a:b], raw(n)[:, k, :], ACT.Square, scale=gain[:, k:k + 1],
                                          accum_out=wsq[:, n, k:k + 1])
                last.then_inc(s_wsq, 1)

            def chunk_sum(dve, n):
                dve.wait_ge(s_wsq, n + 1)
                dve.tensor_reduce(wsum[:, n:n + 1], wsq[:, n, :], AX.X, ALU.add).then_inc(s_wsum, 1)

            def chunk_over_rows(pool, n):
                pool.wait_ge(s_wsum, n + 1)
                pool.partition_all_reduce(wall[:, n:n + 1], wsum[:, n:n + 1], P, RADD).then_inc(s_wall, 1)

            def chunk_scale(dve, n):
                c = slice(n, n + 1)
                dve.wait_ge(s_wall, n + 1)
                power_of_two(dve, wall[:, c], wpow[:, c], wscale[:, c], winv[:, c], s_wsm, 5 * n)
                dve.wait_ge(s_wsm, 5 * n + 4)
                dve.tensor_scalar(wgi[:, n, :], gain[:, 0:KT], winv[:, c], None, ALU.mult).then_inc(s_wsm, 1)

            ACT_HI = range(0, 3)
            DVE_HI = range(3, KT)
            DVE_LO = range(0, 7)
            POOL_LO = range(7, KT)

            def chunk_hi(eng, n, ks):
                a, b = CHUNKS[n]
                eng.wait_ge(s_wsm, 5 * n + 5)
                for k in ks:
                    if ks is ACT_HI:
                        last = eng.activation(wh[:, k, a:b], raw(n)[:, k, :], ACT.Copy, scale=wgi[:, n, k:k + 1])
                    else:
                        last = eng.tensor_scalar(wh[:, k, a:b], raw(n)[:, k, :], wgi[:, n, k:k + 1], None,
                                                 ALU.mult)
                last.then_inc(s_whi[0 if ks is ACT_HI else 1], 1)

            def chunk_lo(dve, n):
                a, b = CHUNKS[n]
                dve.wait_ge(s_whi[0], n + 1)
                dve.wait_ge(s_whi[1], n + 1)
                for k in DVE_LO:
                    last = dve.scalar_tensor_tensor(wl[:, k, a:b], raw(n)[:, k, :], wgi[:, n, k:k + 1],
                                                    wh[:, k, a:b], ALU.mult, ALU.subtract)
                last.then_inc(s_wlo[0], 1)

            def chunk_lo_pool(pool, n):
                a, b = CHUNKS[n]
                pool.wait_ge(s_whi[1], n + 1)
                for k in POOL_LO:
                    last = pool.tensor_scalar(raw(n)[:, k, :], raw(n)[:, k, :], wgi[:, n, k:k + 1], None,
                                              ALU.mult)
                last.then_inc(s_wps, 1)
                pool.wait_ge(s_wps, n + 1)
                k = slice(POOL_LO[0], KT)
                pool.tensor_tensor(wl[:, k, a:b], raw(n)[:, k, :], wh[:, k, a:b],
                                   ALU.subtract).then_inc(s_wlo[1], 1)

            def steps(eng, step):
                for t in range(4):
                    step(t, t // 2, t % 2)
                with eng.Fori(0, (NBLK - 6) // 2) as i:
                    for u in range(2):
                        step(i * 2 + (4 + u), i + 2, u)
                for t in range(NBLK - 2, NBLK + 2):
                    step(t, t // 2, t % 2)

            def known(t):
                return isinstance(t, int)

            def has_front(t):
                return not known(t) or t < NBLK

            def has_xprep(t):
                return not known(t) or 1 <= t < NBLK - 1

            def has_back(t):
                return not known(t) or 1 <= t <= NBLK

            def has_store(t):
                return not known(t) or 2 <= t <= NBLK + 1

            block = actx.enter_context(nc.Block())

            @block.sync
            def _(sp):
                def turn_x(n, h, u):
                    sp.dma_start(hT[u].rearrange("p a k t -> p (a k) t"), x16.rearrange("p a n -> p (a n)"),
                                 transpose=True).then_inc(s_hT, 16)

                def load_x(n, h, u):
                    sp.dma_start(xin[u][:, :], x[bass.ds(n * P, P), :]).then_inc(s_x[u], 16)

                load_x(0, 0, 0)
                sp.dma_start(gain[:, 0:KT], g_in).then_inc(s_gin, 16)
                load_chunk(sp, 0)
                sp.dma_start(pos_i, positions).then_inc(s_pos, 16)
                load_chunk(sp, 1)
                sp.dma_start(gain[:, KT:2 * KT], g_in).then_inc(s_const, 16)
                sp.dma_start(gain[:, OUT_U + 4:WO_U], g_gla_norm).then_inc(s_const, 16)
                sp.dma_start(wal[:, :], w_alpha_up).then_inc(s_const, 16)
                sp.dma_start(bal[:, :], b_alpha).then_inc(s_const, 16)
                sp.dma_start(sinks[:, :], attn_sinks.partition_broadcast(P)).then_inc(s_const, 16)
                load_x(1, 0, 1)
                sp.wait_ge(s_x16, 2)
                turn_x(0, 0, 0)
                load_chunk(sp, 2)
                sp.wait_ge(s_hT, 16)
                sp.dma_start(hts[0], hT[0][:, :, :, :].rearrange("p a k t -> p (a k t)")).then_inc(s_hst[0], 16)
                load_chunk(sp, 3)
                load_chunk(sp, 4)
                sp.wait_ge(s_x16, 4)
                load_x(2, 1, 0)
                turn_x(1, 0, 1)
                load_chunk(sp, 5)
                sp.wait_ge(s_hT, 32)
                sp.dma_start(hts[1], hT[1][:, :, :, :].rearrange("p a k t -> p (a k t)")).then_inc(s_hst[1], 16)

                def step(t, h, u):
                    if has_front(t):
                        if known(t):
                            need(sp, s_usq, t)
                        need(sp, s_hst[1 - u], 16 * (h + u))
                        sp.dma_start(unit[:, :], w_units[bass.ds(t, 1)].rearrange("a p n -> (a p) n")
                                     ).then_inc(s_ub, 16)
                    if has_store(t):
                        need(sp, s_o16, (t - 1) * 4)
                        sp.dma_start(ots[bass.ds(t - 2, 1)].rearrange("a p n -> (a p) n"),
                                     o16[:, :, :].rearrange("p a n -> p (a n)")).then_inc(s_ost, 16)
                    if has_xprep(t):
                        need(sp, s_x16, (t + 2) * 2)
                        if not known(t) or t + 2 < NBLK:
                            load_x(t + 2, h + 1, u)
                        turn_x(t + 1, h + u, 1 - u)
                        need(sp, s_hT, (t + 2) * 16)
                        sp.dma_start(hts[bass.ds(t + 1, 1)].rearrange("a p n -> (a p) n"),
                                     hT[1 - u][:, :, :, :].rearrange("p a k t -> p (a k t)")
                                     ).then_inc(s_hst[1 - u], 16)
                    if known(t) and t == NBLK:
                        sp.wait_ge(s_x16, NBLK * 2)
                        load_piece(sp, 0)
                        sp.wait_ge(s_hT, 16 * NBLK)
                        sp.wait_ge(s_pj, (NBLK - 1) * NCH)
                        sp.wait_ge(s_hst[0], 16 * (NBLK // 2))
                        load_piece(sp, 1)
                        sp.wait_ge(s_usq, NU)
                        sp.wait_ge(s_pj, NBLK * NCH)
                        sp.wait_ge(s_hst[1], 16 * (NBLK // 2))
                        load_piece(sp, 2)
                        sp.wait_ge(s_ost, 16)
                        sp.dma_start(hb0.rearrange("p a k t -> p (a k t)"), hts[0]).then_inc(s_hb[0], 16)
                        sp.dma_start(ob0.rearrange("p a k t -> p (a k) t"), ots[0], transpose=True
                                     ).then_inc(s_ob[0], 16)
                        load_piece(sp, 3)
                        load_piece(sp, 4)

                steps(sp, step)
                for i in range(5, NPRE + 3):
                    load_piece(sp, i)
                for s, n in ((s_hst[0], NBLK // 2), (s_hst[1], NBLK // 2), (s_ost, NBLK)):
                    sp.wait_ge(s, 16 * n)

            @block.gpsimd
            def _(pool):
                pool.memset(ident[:, :], 0.0).then_inc(s_id, 1)
                pool.memset(tri[:, :], 1.0).then_inc(s_id, 1)
                pool.memset(triT[:, :], 1.0).then_inc(s_id, 1)
                pool.memset(triT16[:, :], 1.0).then_inc(s_id, 1)
                pool.memset(triN16[:, :], 1.0).then_inc(s_id, 1)
                pool.wait_ge(s_id, 5)
                pool.affine_select(out=ident[:, :], in_=ident[:, :], compare_op=ALU.not_equal, fill=1.0,
                                   base=0, pattern=[[-1, P]], channel_multiplier=1).then_inc(s_msk, 1)
                for m, op, sign in ((tri, ALU.is_ge, 1), (triT, ALU.is_ge, -1), (triT16, ALU.is_ge, -1),
                                    (triN16, ALU.is_gt, 1)):
                    pool.affine_select(out=m[:, :], in_=m[:, :], compare_op=op, fill=0.0, base=0,
                                       pattern=[[-sign, P]], channel_multiplier=sign).then_inc(s_msk, 1)
                pool.memset(gain[:, OUT_U:OUT_U + 4], 1.0).then_inc(s_gain, 1)
                pool.memset(gain[:, WO_U:NU], 1.0).then_inc(s_gain, 1)
                pool.memset(q1[:, :, :, :], 0.0).then_inc(s_zero, 1)
                pool.memset(q5[:, :, :, :], 0.0).then_inc(s_zero, 1)
                pool.memset(state[:, :, :, :], 0.0).then_inc(s_zero, 1)
                pool.memset(att[:, :, :], 0.0).then_inc(s_zero, 1)
                pool.memset(carry[:, :, :], 0.0).then_inc(s_zero, 1)
                pool.memset(seg[:, :, :], 1.0).then_inc(s_zero, 1)
                pool.wait_ge(s_zero, 6)
                pool.memset(seg[:, :, 0:1], 0.0).then_inc(s_zero, 1)
                for n in range(NCH):
                    chunk_over_rows(pool, n)
                    chunk_lo_pool(pool, n)

                def step(t, h, u):
                    if not has_back(t):
                        return
                    b, pr = t - 1, proj[1 - u]
                    pool.wait_ge(s_evA, t * 3)
                    pool.wait_ge(s_evD, t * 3)
                    pool.wait_ge(s_trig, 2)
                    qk = pr[:, 0:VC].rearrange("p (h d) -> p h d", d=HD)
                    x1, x2 = qk[:, :, 0:HALF], qk[:, :, HALF:2 * HALF]
                    c = cosT[:, bass.ds(b, 1), :].broadcast_to([P, HEADS + KVH, HALF])
                    s = sinT[:, bass.ds(b, 1), :].broadcast_to([P, HEADS + KVH, HALF])
                    for n, (a, f) in enumerate(((x1, c), (x2, s), (x2, c), (x1, s))):
                        pool.tensor_tensor(rt[:, n], a, f, ALU.mult).then_inc(s_rm, 1)
                    need(pool, s_rm, t * 4)
                    pool.tensor_tensor(x1, rt[:, 0], rt[:, 1], ALU.subtract).then_inc(s_rp, 1)
                    pool.tensor_tensor(x2, rt[:, 2], rt[:, 3], ALU.add).then_inc(s_rp, 1)
                    if known(t) and t == NBLK:
                        pool.wait_ge(s_us, 3)
                        pool.partition_all_reduce(uall[:, :], usum[:, :], P, RADD).then_inc(s_ua, 1)
                    v = lambda e: e.rearrange("p (a c) -> p a c", a=2)
                    need(pool, s_gT, t)
                    need(pool, s_e, t * 6)
                    need(pool, s_inc, b)
                    pool.tensor_tensor(k1[:, :, :], gT[:, 2:4, :], v(e2), ALU.mult).then_inc(s_gk, 1)
                    pool.tensor_tensor(k5[:, :, :], gT[:, 2:4, 0:CH], v(e5k), ALU.mult).then_inc(s_gk, 1)
                    pool.tensor_tensor(k4[:, :, :], gT[:, 2:4, :], v(e4), ALU.mult).then_inc(s_gk, 1)
                    if known(t) and t == NBLK:
                        split_piece_pool(pool, 0)
                    need(pool, s_sle, t)
                    pool.tensor_tensor(sil[:, 0:512], sil[:, 0:512], pr[:, ZAC:ZAC + 512], ALU.mult).then_inc(s_sl, 1)
                    pool.tensor_tensor(sil[:, 512:], sil[:, 512:], pr[:, ZBC:ZBC + 512], ALU.mult).then_inc(s_sl, 1)
                    if known(t) and t == NBLK:
                        for i in range(1, NPRE):
                            split_piece_pool(pool, i)

                steps(pool, step)

            @block.scalar
            def _(act):
                def x_squares(n, h, u):
                    need(act, s_x[u], 16 * h + 16)
                    act.activation(junk[:, :], xin[u][:, :], ACT.Square, accum_out=ss[:, :]).then_inc(s_xss, 1)

                def x_table(n):
                    rsqrt_table(act, s_xv, n + 1, s_xt, n * 2, var[:, :], lnv[:, :], y0[:, :])

                def evac(t, u, c):
                    a, b = CHUNKS[c]
                    act.wait_ge(s_pj, t * NCH + (c + 1))
                    if c == 0:
                        need(act, s_inc, t - 1)
                        need(act, s_gat, t - 1)
                        src = bank[0][:, :].rearrange("p (g j d) -> p g j d", g=KVH, j=GRP)
                        dst = proj[u][:, 0:512].rearrange("p (j g d) -> p g j d", g=KVH, j=GRP)
                        for g in range(KVH):
                            last = act.activation(dst[:, g], src[:, g], ACT.Copy, scale=wscale[:, 0:1])
                    else:
                        last = act.activation(proj[u][:, a:b], bank[0][:, 0:b - a], ACT.Copy,
                                              scale=wscale[:, c:c + 1])
                    last.then_inc(s_evA, 1)

                act.preload_act_table_set("natural_log_exp_and_others")
                x_squares(0, 0, 0)
                x_table(0)
                act.wait_ge(s_gin, 16)
                for n in range(NCH):
                    chunk_squares(act, n)
                    if n in (2, 4):
                        evac(0, 0, n - 2)
                    if n == 3:
                        x_squares(1, 0, 1)
                    chunk_hi(act, n, ACT_HI)
                    if n == 3:
                        x_table(1)
                act.wait_ge(s_rope, 2 + 2 * ROPE_OPS + 3)
                act.activation(sinT[:, :, :].rearrange("p n i -> p (n i)"), ang, ACT.Sin).then_inc(s_trig, 1)
                act.activation(cosT[:, :, :].rearrange("p n i -> p (n i)"), turns[0],
                               ACT.Sin).then_inc(s_trig, 1)
                act.preload_act_table_set("natural_log_exp_and_others")

                def step(t, h, u):
                    b, pr = t - 1, proj[1 - u]
                    back = has_back(t)
                    if has_xprep(t):
                        x_squares(t + 1, h + u, 1 - u)
                    if has_front(t) and not (known(t) and t == 0):
                        evac(t, u, 0)
                    if back:
                        if known(t) and b == 0:
                            act.wait_ge(s_qk, 4)
                        need(act, s_t1, b * 3 + 1)
                        for g in range(KVH):
                            rows = slice(g * HD, (g + 1) * HD)
                            act.activation(qs[rows, g].rearrange("p j t -> p (j t)"), bank[4][rows, :],
                                           ACT.Copy, scale=qkin[rows, 0:1]).then_inc(s_qT, 1)
                        need(act, s_t1, b * 3 + 2)
                        for g in range(KVH):
                            rows = slice(g * HD, (g + 1) * HD)
                            for half in range(2):
                                last = act.activation(ks[1 - u][half * HD:(half + 1) * HD, g], bank[5][rows, 0:P],
                                                      ACT.Copy, scale=qkin[rows, 1:2])
                        last.then_inc(s_kh, 1)
                        need(act, s_t1, b * 3 + 3)
                        act.activation(gT[:, :, :].rearrange("p j t -> p (j t)"), bank[6][:, :],
                                       ACT.Copy).then_inc(s_gT, 1)
                        need(act, s_pvo, b)
                        act.activation(vbuf[1 - u][:, 0], pr[:, VC:VC + P], ACT.Copy, scale=qkin[:, 1:2]
                                       ).then_inc(s_vh, 1)
                    if has_xprep(t):
                        x_table(t + 1)
                    if has_front(t):
                        if known(t) and t == 0:
                            act.wait_ge(s_gain, 2)
                            act.wait_ge(s_const, 16 * NCONST)
                        need(act, s_ub, (t + 1) * 16)
                        act.activation(unit[:, :], unit[:, :], ACT.Square, scale=gain[:, bass.ds(t, 1)],
                                       accum_out=usq[:, bass.ds(t, 1)]).then_inc(s_usq, 1)
                    if back:
                        need(act, s_slm, b * 2 + 2)
                        act.activation(sil, sil, ACT.Exp).then_inc(s_slt, 1)
                        need(act, s_slt, b * 2 + 1)
                        act.activation(sil, sil, ACT.Ln, bias=1.0).then_inc(s_slt, 1)
                        if known(t) and t == NBLK:
                            split_piece(act, 0, ACT_K, ())
                        if not (known(t) and b == 0):
                            for g in range(KVH):
                                need(act, s_sc, b * 4 + (2, 4)[g])
                                act.activation(scs[:, g * GRP:(g + 1) * GRP, :].rearrange("p h k -> p (h k)"),
                                               bank[(5, 7)[g]][:, :], ACT.Copy).then_inc(s_pv0, 1)
                        need(act, s_spm, b + 1)
                        act.activation(sp_, sp_, ACT.Exp).then_inc(s_spt, 1)
                        need(act, s_spt, b * 2 + 1)
                        act.activation(sp_, sp_, ACT.Ln, bias=1.0).then_inc(s_spt, 1)
                        need(act, s_sm, b * 3 + 3)
                        act.activation(es[:, :], dsk[:, :], ACT.Exp).then_inc(s_es, 1)
                        for hd in range(HEADS):
                            act.activation(scs[:, hd, :], scs[:, hd, :], ACT.Exp, bias=nm[:, hd:hd + 1],
                                           scale=ssc[:, 0:1], accum_out=rsum[:, hd:hd + 1]).then_inc(s_ex, 1)
                    if has_front(t) and not (known(t) and t == 0):
                        evac(t, u, 2)
                    if back:
                        for g in range(KVH):
                            need(act, s_pt, b * 2 + 1 + g)
                            act.activation(ptc[:, 0, g * GRP:(g + 1) * GRP].rearrange("p h k -> p (h k)"),
                                           bank[(4, 6)[g]][:, :], ACT.Copy, scale=PSCALE).then_inc(s_pth, 1)
                        need(act, s_dif, b * 4 + 4)
                        need(act, s_gq, b * 5)
                        need(act, s_gk, b * 3)
                        need(act, s_st, b * 4)
                        for o, i, sc in ((e1, d1, 1), (e2, d1, -1), (e3, d3, 1), (e4, d4, -1),
                                         (e5k, d5, -1)):
                            act.activation(o, i, ACT.Exp, scale=sc / 16.0).then_inc(s_e, 1)
                        act.activation(e5q.rearrange("p (a c) -> p a c", a=2), cum[:, :, 1, :], ACT.Exp,
                                       scale=1 / 16.0).then_inc(s_e, 1)
                        need(act, s_sll, b * 2 + 2)
                        act.activation(sil, sil, ACT.Exp, scale=-1.0).then_inc(s_sle, 1)
                        if known(t) and t == NBLK:
                            split_piece(act, 1, ACT_K, ())
                    if has_front(t):
                        evac(t, u, 4)
                    if back:
                        need(act, s_kt, t)
                        act.activation(k2[:, :, :].rearrange("p a t -> p (a t)"), bank[4][:, 0:256],
                                       ACT.Copy).then_inc(s_k2, 1)
                        if known(t) and t == NBLK:
                            for i in (2, 3):
                                split_piece(act, i, ACT_K, ())
                    if back:
                        need(act, s_go, t)
                        act.activation(og[:, :, :].rearrange("p h v -> p (h v)"), bank[5][:, :],
                                       ACT.Copy).then_inc(s_og, 1)
                        need(act, s_og, t)
                        for hd in range(BH):
                            act.activation(junk[:, hd * BV:(hd + 1) * BV], og[:, hd, :], ACT.Square,
                                           accum_out=ss4[:, hd:hd + 1]).then_inc(s_gss, 1)
                        rsqrt_table(act, s_gv, t, s_gt, b * 2, var4[:, :], ln4[:, :], y4[:, :])
                        if known(t) and t == NBLK:
                            for i in range(4, NPRE):
                                split_piece(act, i, ACT_K, ())

                steps(act, step)

            @block.tensor
            def _(pe):
                def chunk(t, u, c):
                    a, b = CHUNKS[c]
                    if c == 0:
                        need(pe, s_hT, (t + 1) * 16)
                    if known(t) and t == 0:
                        for s in s_wlo:
                            pe.wait_ge(s, c + 1)
                    if c >= 2:
                        need(pe, (s_evA, s_evD)[c % 2], t * 3 + c // 2)
                    else:
                        need(pe, (s_evA, s_evD)[c % 2], t * 3)
                    o = bank[c % 2][:, 0:b - a]
                    n = 0
                    for k in range(KT):
                        for l, r in ((0, wh), (0, wl), (1, wh)):
                            last = pe.matmul(o, hT[u][:, l, k, :], r[:, k, a:b], start=n == 0,
                                             stop=n == 3 * KT - 1)
                            n += 1
                    last.then_inc(s_pj, 1)

                def qk_turn(t, b, pr):
                    need(pe, s_rp, t * 2)
                    need(pe, s_k2, b)
                    for j in range(GRP):
                        last = pe.transpose(bank[4][:, j * P:(j + 1) * P], pr[:, j * P:(j + 1) * P], ident[:, :])
                    last.then_inc(s_t1, 1)
                    need(pe, s_og, b)
                    pe.transpose(bank[5][:, 0:P], pr[:, KC:KC + P], ident[:, :])
                    pe.transpose(bank[5][0:RANK, P:2 * P], pr[:, ALC:NA], ident[:, :]).then_inc(s_t1, 1)
                    need(pe, s_st, b * 4)
                    for j in range(4):
                        last = pe.transpose(bank[6][:, j * P:(j + 1) * P], pr[:, QBC + j * P:QBC + (j + 1) * P],
                                            ident[:, :])
                    last.then_inc(s_t1, 1)

                def logits(t, b):
                    need(pe, s_kT, t * 2)
                    need(pe, s_zs, b * 2)
                    for p in range(2):
                        last = pe.matmul(bank[2][:, p * P:(p + 1) * P], wal[:, p * P:(p + 1) * P], aT[:, :],
                                         start=True, stop=True)
                    last.then_inc(s_z, 1)

                def score(o, g, rows, j, v):
                    pe.matmul(o, qs[:, g, j, :], ks[v][:, g, :], start=True, stop=False)
                    return pe.matmul(o, qs[rows, g, j, :], kl[v][rows, :], start=False, stop=True)

                def scores(t, b, u):
                    need(pe, s_ql, t * 2)
                    need(pe, s_gT, t)
                    need(pe, s_br, b * 2)
                    for g in range(KVH):
                        rows = slice(g * HD, (g + 1) * HD)
                        for bk, v in (((4, 6)[g], 1 - u), ((5, 7)[g], u)):
                            for j in range(GRP):
                                last = score(bank[bk][:, j * P:(j + 1) * P], g, rows, j, v)
                            last.then_inc(s_sc, 1)

                def scores0(t):
                    need(pe, s_ql, t * 2)
                    need(pe, s_gT, t)
                    for g in range(KVH):
                        rows = slice(g * HD, (g + 1) * HD)
                        for j in range(GRP):
                            last = score(bank[(4, 6)[g]][:, j * P:(j + 1) * P], g, rows, j, 0)
                        last.then_inc(s_sc, 2)

                def probs_turn(t, b):
                    for g in range(KVH):
                        need(pe, s_ex, b * 8 + 4 * g + 4)
                        for j in range(GRP):
                            last = pe.transpose(bank[(4, 6)[g]][:, j * P:(j + 1) * P], scs[:, g * GRP + j, :],
                                                ident[:, :])
                        last.then_inc(s_pt, 1)

                def gla_scores(t, b):
                    need(pe, s_gq, t * 5)
                    need(pe, s_gk, t * 3)
                    if not (known(t) and b == 0):
                        need(pe, s_pv0, t * 2 - 1)
                    for p in range(2):
                        o = bank[5][:, p * 256:(p + 1) * 256]
                        pe.matmul(o, k1[:, p, :], q1[:, p, :, :].rearrange("p h t -> p (h t)"),
                                  start=True, stop=True)
                        o = o.rearrange("p (h t) -> p h t", h=2)[0:CH, :, CH:P]
                        last = pe.matmul(o, k5[:, p, :], q5[:, p, :, :], start=True, stop=True)
                    last.then_inc(s_at, 1)

                def values(t, b, u):
                    need(pe, s_ptm, t * 4)
                    need(pe, s_vb, t)
                    if not (known(t) and b == 0):
                        need(pe, s_pv0, t * 2)
                    for hd in range(HEADS):
                        g = hd // GRP
                        o = bank[7][:, hd * HD:(hd + 1) * HD]
                        first = known(t) and b == 0
                        cols = slice(g * HD, (g + 1) * HD)
                        sides = [(ptc, 1 - u)] if first else [(ptc, 1 - u), (ptp, u)]
                        for n, (pt, w) in enumerate(sides):
                            for l, v in ((0, 0), (0, 1), (1, 0)):
                                last = pe.matmul(o, pt[:, l, hd, :], vbuf[w][:, v, cols],
                                                 start=n == l == v == 0, stop=n == len(sides) - 1 and l == 1)
                    last.then_inc(s_pvo, 1)

                def keys_turn(t):
                    for p in range(2):
                        last = pe.transpose(bank[4][:, p * P:(p + 1) * P], k4[:, p, :], ident[:, :])
                    last.then_inc(s_kt, 1)

                def gla_out(t, b, pr):
                    need(pe, s_am, t)
                    need(pe, s_st, b * 4)
                    v = pr[:, VBC:VBC + BH * BV]
                    for p in range(2):
                        pe.matmul(bank[5][:, p * 256:(p + 1) * 256], q3[:, p, :],
                                  state[:, p].rearrange("p h v -> p (h v)"), start=p == 0, stop=False,
                                  skip_group_check=True)
                    for hd in range(BH):
                        last = pe.matmul(bank[5][:, hd * BV:(hd + 1) * BV], att[:, hd, :],
                                         v[:, hd * BV:(hd + 1) * BV], start=False, stop=hd == BH - 1,
                                         skip_group_check=True)
                    last.then_inc(s_go, 1)
                    need(pe, s_k2, t)
                    for p in range(2):
                        last = pe.matmul(bank[6][:, p * 256:(p + 1) * 256], k2[:, p, :],
                                         v[:, p * 256:(p + 1) * 256], start=True, stop=True)
                    last.then_inc(s_inc, 1)

                pe.wait_ge(s_msk, 5)

                def step(t, h, u):
                    b, pr = t - 1, proj[1 - u]
                    front, back = has_front(t), has_back(t)
                    if front:
                        chunk(t, u, 0)
                    if back:
                        if known(t) and b == 0:
                            pe.wait_ge(s_const, 16 * NCONST)
                            pe.wait_ge(s_zero, 7)
                        qk_turn(t, b, pr)
                    if front:
                        chunk(t, u, 1)
                    if back:
                        logits(t, b)
                        if known(t) and b == 0:
                            scores0(t)
                        else:
                            scores(t, b, u)
                    if front:
                        chunk(t, u, 2)
                    if front:
                        chunk(t, u, 3)
                    if back:
                        probs_turn(t, b)
                    if front:
                        chunk(t, u, 4)
                    if back:
                        values(t, b, u)
                        gla_scores(t, b)
                        keys_turn(t)
                    if front:
                        chunk(t, u, 5)
                    if back:
                        gla_out(t, b, pr)

                steps(pe, step)
                pe.wait_ge(s_hb[0], 16)
                for a in range(2):
                    pe.wait_ge((s_evA, s_evD)[a], NBLK * 3)
                    pieces_split(pe, GA + a, 0)
                    gate_products(pe, hb0, 0, a)

            @block.vector
            def _(dve):
                count = [0]

                def link(ins):
                    ins.then_inc(s_rope, 1)
                    count[0] += 1
                    dve.wait_ge(s_rope, count[0])

                n2, n1, n0 = turns

                def angles():
                    inv_freq = np.exp(np.float32(-np.log(THETA)) * np.arange(HALF, dtype=np.float32)
                                      * np.float32(1.0 / HALF)).astype(np.float32)
                    dve.wait_ge(s_pos, 16)
                    link(dve.tensor_copy(pos_f, pos_i))
                    a3 = ang.rearrange("p (n i) -> p n i", i=HALF)
                    for i in range(HALF):
                        ins = dve.tensor_scalar(a3[:, :, i], pos_f, float(inv_freq[i]), None, ALU.mult)
                    link(ins)

                def whole_turns():
                    link(dve.tensor_scalar(n0, ang, float(1 / (2 * np.pi)), None, ALU.mult))
                    link(dve.tensor_scalar(n2, n0, 2.0 ** -22, MAGIC, ALU.mult, ALU.add))
                    link(dve.tensor_scalar(n2, n2, MAGIC, None, ALU.subtract))
                    link(dve.scalar_tensor_tensor(n0, n2, -2.0 ** 22, n0, ALU.mult, ALU.add))
                    link(dve.tensor_scalar(n1, n0, 2.0 ** -11, MAGIC, ALU.mult, ALU.add))
                    link(dve.tensor_scalar(n1, n1, MAGIC, None, ALU.subtract))
                    link(dve.scalar_tensor_tensor(n0, n1, -2.0 ** 11, n0, ALU.mult, ALU.add))
                    link(dve.tensor_scalar(n0, n0, MAGIC, None, ALU.add))
                    link(dve.tensor_scalar(n0, n0, MAGIC, None, ALU.subtract))

                def take_turns_off():
                    for c in two_pi_parts():
                        for n, w in ((n2, 2.0 ** 22), (n1, 2.0 ** 11), (n0, 1.0)):
                            link(dve.scalar_tensor_tensor(ang, n, -w * c, ang, ALU.mult, ALU.add))

                def sine_arguments():
                    pi = float(np.nextafter(np.float32(np.pi), np.float32(0)))
                    link(dve.tensor_scalar(ang, ang, pi, -pi, ALU.min, ALU.max))
                    link(dve.scalar_tensor_tensor(n2, ang, -1.0, ang, ALU.mult, ALU.max))
                    link(dve.tensor_scalar(n2, n2, -1.0, float(np.pi / 2), ALU.mult, ALU.add))
                    assert count[0] == 2 + 2 * ROPE_OPS + 3

                def x_start(n):
                    rsqrt_start(dve, s_xss, n + 1, s_xv, ss[:, :], var[:, :], D)

                def x_split(n, u):
                    rsqrt_newton(dve, s_xt, n * 2, s_xn, n * 4, var[:, :], y0[:, :], nt[:, 0:1], rstd[:, :])
                    need(dve, s_xn, n * 4 + 4)
                    need(dve, s_hT, n * 16)
                    dve.tensor_scalar(x16[:, 0], xin[u][:, :], rstd[:, 0:1], None, ALU.mult).then_inc(s_x16, 1)
                    need(dve, s_x16, n * 2 + 1)
                    dve.scalar_tensor_tensor(x16[:, 1], xin[u][:, :], rstd[:, 0:1], x16[:, 0], ALU.mult,
                                             ALU.subtract).then_inc(s_x16, 1)

                def evac(t, u, c):
                    a, b = CHUNKS[c]
                    dve.wait_ge(s_pj, t * NCH + (c + 1))
                    if c == 1:
                        need(dve, s_inc, t - 1)
                        need(dve, s_gat, t - 1)
                    dve.tensor_scalar(proj[u][:, a:b], bank[1][:, 0:b - a], wscale[:, c:c + 1], None,
                                      ALU.mult).then_inc(s_evD, 1)

                dve.memset(tick[:, :], 0.0)
                x_start(0)
                x_split(0, 0)
                dve.wait_ge(s_gin, 16)
                for n in range(NCH):
                    chunk_sum(dve, n)
                    chunk_scale(dve, n)
                    chunk_hi(dve, n, DVE_HI)
                    if n == 3:
                        x_start(1)
                    if n in (3, 5):
                        evac(0, 0, n - 2)
                    chunk_lo(dve, n)
                    if n == 3:
                        x_split(1, 1)
                    if n == 0:
                        angles()
                    elif n in (1, 3):
                        whole_turns()
                    elif n in (2, 4):
                        take_turns_off()
                    else:
                        sine_arguments()
                dve.tensor_scalar(qkin[:, :], winv[:, 0:2], 2.0 ** -4, None, ALU.mult).then_inc(s_qk, 1)
                dve.tensor_scalar(ssh[:, :], wscale[:, 0:2], 2.0 ** 4, None, ALU.mult).then_inc(s_qk, 1)
                dve.tensor_scalar(pvsc[:, :], wscale[:, 1:2], 2.0 ** 4 / PSCALE, None, ALU.mult)
                dve.wait_ge(s_qk, 2)
                dve.tensor_tensor(ssc[:, :], ssh[:, 0:1], ssh[:, 1:2], ALU.mult).then_inc(s_qk, 1)
                dve.wait_ge(s_qk, 3)
                dve.tensor_scalar(ssc[:, :], ssc[:, :], HD ** -0.5, None, ALU.mult).then_inc(s_qk, 1)

                def wait_carrier():
                    dve.tensor_copy(tick[:, 0:1], tick[:, 1:2])

                def softmax_shift(t, b, first):
                    for g in range(KVH):
                        hs = slice(g * GRP, (g + 1) * GRP)
                        if first:
                            dve.memset(scs[:, hs, :], NEG).then_inc(s_pv0, 1)
                        need(dve, s_pv0, t * 2 - 1 + g)
                        need(dve, s_sc, b * 4 + 1 + 2 * g)
                        wait_carrier()
                        dve.copy_predicated(scs[:, hs, :],
                                            tri[:, :].bitcast(U32).unsqueeze(1).broadcast_to([P, GRP, P]),
                                            bank[(4, 6)[g]][:, :].rearrange("p (h k) -> p h k", h=GRP)
                                            ).then_inc(s_sel, 1)
                        need(dve, s_sel, b * 2 + 1 + g)
                        dve.tensor_reduce(mx[:, hs], scs[:, hs, :], AX.X, ALU.max).then_inc(s_mx, 1)
                    need(dve, s_mx, t * 2)
                    dve.scalar_tensor_tensor(mm[:, :], mx[:, :], ssc[:, 0:1], sinks[:, :], ALU.mult,
                                             ALU.max).then_inc(s_sm, 1)
                    need(dve, s_sm, b * 3 + 1)
                    dve.tensor_scalar(nm[:, :], mm[:, :], -1.0, None, ALU.mult).then_inc(s_sm, 1)
                    dve.tensor_tensor(dsk[:, :], sinks[:, :], mm[:, :], ALU.subtract).then_inc(s_sm, 1)

                def gate_sums(t, b):
                    need(dve, s_spt, b * 2 + 2)
                    dve.scalar_tensor_tensor(gsp, sp_, -1.0, zs, ALU.mult, ALU.min).then_inc(s_sp, 1)
                    need(dve, s_sp, t)
                    dve.tensor_tensor_scan(cum[:, :, :, :].rearrange("p a b c -> p (a b c)"),
                                           seg[:, :, :].rearrange("p a c -> p (a c)"), gsp, 0.0,
                                           ALU.mult, ALU.add).then_inc(s_cum, 1)
                    need(dve, s_cum, t)
                    c4 = cum[:, :, :, :].rearrange("p a b c -> p (a b) c")
                    dve.tensor_copy(carry[:, :, 1:2], cum[:, :, 0, CH - 1:CH]).then_inc(s_car, 1)
                    dve.tensor_tensor(d1.rearrange("p (a c) -> p a c", a=4), c4,
                                      c4[:, :, CH // 2 - 1:CH // 2].broadcast_to([P, 4, CH]),
                                      ALU.subtract).then_inc(s_dif, 1)
                    dve.tensor_tensor(d5.rearrange("p (a c) -> p a c", a=2), cum[:, :, 0, :],
                                      cum[:, :, 0, CH - 1:CH].broadcast_to([P, 2, CH]),
                                      ALU.subtract).then_inc(s_dif, 1)
                    need(dve, s_car, t)
                    dve.tensor_tensor(d3.rearrange("p (a c) -> p a c", a=4), c4,
                                      carry[:, :, :].rearrange("p a b -> p (a b)").unsqueeze(2)
                                      .broadcast_to([P, 4, CH]), ALU.add).then_inc(s_dif, 1)
                    need(dve, s_dif, b * 4 + 3)
                    d3v = d3.rearrange("p (a c) -> p a c", a=2)
                    dve.tensor_tensor(d4.rearrange("p (a c) -> p a c", a=2), d3v,
                                      d3v[:, :, P - 1:P].broadcast_to([P, 2, P]),
                                      ALU.subtract).then_inc(s_dif, 1)

                def gla_factors(t, b):
                    need(dve, s_gT, t)
                    need(dve, s_e, t * 6)
                    need(dve, s_inc, b)
                    v = lambda e: e.rearrange("p (a c) -> p a c", a=2)
                    sc = BK ** -0.5
                    for hh in range(2):
                        r = slice(hh * BK, (hh + 1) * BK)
                        dve.scalar_tensor_tensor(q1[r, :, hh, :], gT[r, 0:2, :], sc, v(e1)[r], ALU.mult,
                                                 ALU.mult).then_inc(s_gq, 1)
                        dve.scalar_tensor_tensor(q5[r, :, hh, :], gT[r, 0:2, CH:P], sc, v(e5q)[r], ALU.mult,
                                                 ALU.mult).then_inc(s_gq, 1)
                    dve.scalar_tensor_tensor(q3[:, :, :], gT[:, 0:2, :], sc, v(e3), ALU.mult,
                                             ALU.mult).then_inc(s_gq, 1)

                def probs_mask(t, b):
                    for g in range(KVH):
                        hs = slice(g * GRP, (g + 1) * GRP)
                        need(dve, s_pth, b * 2 + 1 + g)
                        dve.scalar_tensor_tensor(ptc[:, 1, hs], bank[(4, 6)[g]][:, :]
                                                 .rearrange("p (h k) -> p h k", h=GRP), PSCALE, ptc[:, 0, hs],
                                                 ALU.mult, ALU.subtract).then_inc(s_ptl, 1)
                    for g in range(KVH):
                        hs = slice(g * GRP, (g + 1) * GRP)
                        need(dve, s_ptl, b * 2 + 1 + g)
                        for dst, m in ((ptp, triN16), (ptc, triT16)):
                            for a in range(2):
                                last = dve.tensor_tensor(dst[:, a, hs], ptc[:, a, hs],
                                                         m[:, :].unsqueeze(1).broadcast_to([P, GRP, P]), ALU.mult)
                            last.then_inc(s_ptm, 1)

                def outputs(t, b):
                    need(dve, s_gn, t * 4)
                    dve.tensor_tensor(brn[:, 512:].rearrange("p (h d) -> p h d", h=BH), og[:, :, :],
                                      r4[:, :].unsqueeze(2).broadcast_to([P, BH, BV]),
                                      ALU.mult).then_inc(s_br, 1)
                    need(dve, s_br, t * 2)
                    need(dve, s_sl, t * 2)
                    dve.tensor_tensor(brn, brn, sil, ALU.mult).then_inc(s_gat, 1)
                    need(dve, s_gat, t)
                    b2 = brn.rearrange("p (a n) -> p a n", a=2)
                    osc = oscale[:, bass.ds(b, 1), :].rearrange("p a b -> p (a b)")
                    dve.tensor_reduce(omax[:, :], b2, AX.X, ALU.max, apply_absolute_value=True
                                      ).then_inc(s_om, 1)
                    need(dve, s_om, b * 5 + 1)
                    dve.tensor_scalar(omax[:, :], omax[:, :], 1e-30, None, ALU.max).then_inc(s_om, 1)
                    need(dve, s_om, b * 5 + 2)
                    dve.tensor_scalar(omax[:, :].bitcast(U32), omax[:, :].bitcast(U32), 0x7F800000, None,
                                      ALU.bitwise_and).then_inc(s_om, 1)
                    need(dve, s_om, b * 5 + 3)
                    dve.tensor_scalar(opow[:, :], omax[:, :], 2.0 ** -10, None, ALU.mult).then_inc(s_om, 1)
                    need(dve, s_om, b * 5 + 4)
                    dve.tensor_copy(osc, opow[:, :])
                    dve.reciprocal(oinv[:, :], opow[:, :]).then_inc(s_om, 1)
                    need(dve, s_om, t * 5)
                    need(dve, s_ost, b * 16)
                    for a in range(2):
                        dve.tensor_scalar(o16[:, 0, a * 512:(a + 1) * 512], b2[:, a], oinv[:, a:a + 1],
                                          None, ALU.mult).then_inc(s_o16, 1)
                    need(dve, s_o16, b * 4 + 2)
                    for a in range(2):
                        dve.scalar_tensor_tensor(o16[:, 1, a * 512:(a + 1) * 512], b2[:, a],
                                                 oinv[:, a:a + 1], o16[:, 0, a * 512:(a + 1) * 512],
                                                 ALU.mult, ALU.subtract).then_inc(s_o16, 1)

                def step(t, h, u):
                    b, pr = t - 1, proj[1 - u]
                    front, back = has_front(t), has_back(t)
                    first = known(t) and b == 0
                    if has_xprep(t):
                        x_start(t + 1)
                    if back:
                        if first:
                            dve.wait_ge(s_zero, 7)
                            dve.wait_ge(s_msk, 5)
                        need(dve, s_kh, t)
                        dve.tensor_copy(aT[:, :], bank[5][0:RANK, P:2 * P]).then_inc(s_kT, 1)
                        for g in range(KVH):
                            rows = slice(g * HD, (g + 1) * HD)
                            last = dve.scalar_tensor_tensor(kl[1 - u][rows, :], bank[5][rows, 0:P],
                                                            qkin[rows, 1:2], ks[1 - u][rows, g], ALU.mult,
                                                            ALU.subtract)
                        last.then_inc(s_kT, 1)
                        need(dve, s_qT, t * 2)
                        for g in range(KVH):
                            rows = slice(g * HD, (g + 1) * HD)
                            other = slice((1 - g) * HD, (2 - g) * HD)
                            dve.scalar_tensor_tensor(qs[other, g].rearrange("p j t -> p (j t)"), bank[4][rows, :],
                                                     qkin[rows, 0:1],
                                                     qs[rows, g].rearrange("p j t -> p (j t)"), ALU.mult,
                                                     ALU.subtract).then_inc(s_ql, 1)
                        dve.wait_ge(s_evA, t * 3)
                        dve.wait_ge(s_evD, t * 3)
                        need(dve, s_gat, b)
                        for n, c in enumerate((ZAC, ZBC)):
                            dve.tensor_scalar(sil[:, n * 512:(n + 1) * 512], pr[:, c:c + 512], -1.0, BIG_ARG,
                                              ALU.mult, ALU.min).then_inc(s_slm, 1)
                        if known(t) and t == NBLK:
                            unit_scales(dve)
                        need(dve, s_slt, b * 2 + 2)
                        for n, c in enumerate((ZAC, ZBC)):
                            dve.scalar_tensor_tensor(sil[:, n * 512:(n + 1) * 512], pr[:, c:c + 512], -1.0,
                                                     sil[:, n * 512:(n + 1) * 512], ALU.mult,
                                                     ALU.max).then_inc(s_sll, 1)
                    if front and not (known(t) and t == 0):
                        evac(t, u, 1)
                    if back:
                        need(dve, s_z, t)
                        for p in range(2):
                            dve.tensor_scalar(zs[:, p * P:(p + 1) * P], bank[2][:, p * P:(p + 1) * P],
                                              bal[:, p:p + 1], None, ALU.add).then_inc(s_zs, 1)
                        need(dve, s_zs, t * 2)
                        dve.tensor_scalar(sp_, zs, -1.0, BIG_ARG, ALU.mult, ALU.min).then_inc(s_spm, 1)
                        softmax_shift(t, b, first)
                    if has_xprep(t):
                        x_split(t + 1, 1 - u)
                    if back:
                        gate_sums(t, b)
                        if known(t) and t == NBLK:
                            split_piece(dve, 0, DVE_K, (0, 1, 2))
                        need(dve, s_es, t)
                        need(dve, s_ex, t * 8)
                        dve.tensor_tensor(den[:, :], rsum[:, :], es[:, :], ALU.add).then_inc(s_den, 1)
                        need(dve, s_den, b * 2 + 1)
                        dve.reciprocal(rden[:, :], den[:, :]).then_inc(s_den, 1)
                        need(dve, s_vh, t)
                        dve.scalar_tensor_tensor(vbuf[1 - u][:, 1], pr[:, VC:VC + P], qkin[:, 1:2],
                                                 vbuf[1 - u][:, 0], ALU.mult, ALU.subtract).then_inc(s_vb, 1)
                        probs_mask(t, b)
                        gla_factors(t, b)
                        if known(t) and t == NBLK:
                            split_piece(dve, 1, DVE_K, (0, 1, 2))
                    if front and not (known(t) and t == 0):
                        evac(t, u, 3)
                    if back:
                        need(dve, s_pvo, t)
                        need(dve, s_den, t * 2)
                        dve.scalar_tensor_tensor(brn[:, 0:512].rearrange("p (h d) -> p h d", h=HEADS),
                                                 bank[7][:, :].rearrange("p (h d) -> p h d", h=HEADS),
                                                 pvsc[:, 0:1],
                                                 rden[:, :].unsqueeze(2).broadcast_to([P, HEADS, HD]),
                                                 ALU.mult, ALU.mult).then_inc(s_br, 1)
                        need(dve, s_at, t)
                        wait_carrier()
                        dve.copy_predicated(att[:, :, :],
                                            triT[:, :].bitcast(U32).unsqueeze(1).broadcast_to([P, BH, P]),
                                            bank[5][:, :].rearrange("p (h t) -> p h t", h=BH)).then_inc(s_am, 1)
                        if known(t) and t == NBLK:
                            for i in (2, 3):
                                split_piece(dve, i, DVE_K, (0, 1, 2))
                    if front:
                        evac(t, u, 5)
                    if back:
                        need(dve, s_inc, t)
                        for p in range(2):
                            for hh in range(2):
                                r = slice(hh * BK, (hh + 1) * BK)
                                dve.scalar_tensor_tensor(
                                    state[r, p, hh, :], state[r, p, hh, :],
                                    e3[r, p * P + P - 1:p * P + P],
                                    bank[6][r, p * 256 + hh * BV:p * 256 + (hh + 1) * BV],
                                    ALU.mult, ALU.add).then_inc(s_st, 1)
                        rsqrt_start(dve, s_gss, t * 4, s_gv, ss4[:, :], var4[:, :], BV)
                        rsqrt_newton(dve, s_gt, b * 2, s_gn, b * 4, var4[:, :], y4[:, :], nt4[:, :], r4[:, :])
                        outputs(t, b)

                steps(dve, step)
                for i in range(4, NPRE):
                    split_piece(dve, i, DVE_K, (0, 1, 2))

        with ExitStack() as bctx:
            def sc_(name, shape, dt=F32):
                return sb(name, shape, dt, bctx)

            fin = [tiles[:, 0, 0:D], tiles[:, 0, D:2 * D]]
            res = tiles[:, 1, 0:D]
            mT = fp16_parts(tiles[:, 1, D:2 * D])
            sg = [[sc_(f"sg{j}{a}", [P, 512])[:, :] for a in range(2)] for j in range(2)]
            ta = sc_("ta", [P, 512])[:, :]
            tb = sc_("tb", [P, 512])[:, :]
            gfin = sc_("gfin", [P, D])[:, :]
            mg = sc_("mg", [P, D])[:, :]
            wa1 = sc_("wa1", [P, 2, BH, D], F16)
            wo = sc_("wo", [P, 2, KT, D], F16)
            late[:] = [wa1, wo]
            hb = [hb0, sc_("hb1", [P, 2, KT, P], F16)]
            ob = [ob0, sc_("ob1", [P, 2, KT, P], F16)]
            xb = [sc_(f"xb{i}", [P, D]) for i in range(2)]
            m16 = sc_("m16", [P, 2, D], F16)
            junkb = sc_("junkb", [P, D], F16)
            ysc = sc_("ysc", [P, 2])
            mmax = sc_("mmax", [P, 1])
            msc = sc_("msc", [P, 1])
            minv = sc_("minv", [P, 1])
            rsc = sc_("rsc", [P, 1])

            s_xb = [sem("xb_even"), sem("xb_odd")]
            s_hh = [sem("hb_head_even"), sem("hb_head_odd")]
            s_gf = sem("gfin_loaded")
            s_gm = sem("gates_clamped")
            s_gx = sem("gate_tables")
            s_gl = sem("gates_softplus")
            s_sg = sem("gates_sigmoid")
            s_y = sem("branch_products")
            s_ys = sem("branch_scales")
            s_yt = sem("branches_merging")
            s_mg = sem("merged")
            s_ms = sem("merged_scales")
            s_m16 = sem("merged_split")
            s_mT = sem("merged_transposed")
            s_rs = sem("out_scales")
            s_w = sem("out_products")
            s_r = sem("residual_added")
            s_fss = sem("final_square_sum")
            s_fv = sem("final_var")
            s_ft = sem("final_rsqrt_table")
            s_fn = sem("final_rsqrt_newton")
            s_fin = sem("finished")
            s_out = [sem("stored_even"), sem("stored_odd")]

            def stepsb(eng, step):
                for t in range(3):
                    step(t, t // 2, t % 2)
                with eng.Fori(0, (NBLK - 4) // 2) as i:
                    step(i * 2 + 3, i + 1, 1)
                    step(i * 2 + 4, i + 2, 0)
                step(NBLK - 1, NBLK // 2 - 1, 1)
                step(NBLK, NBLK // 2, 0)

            def frontb(t):
                return not isinstance(t, int) or t < NBLK

            def last_front(t):
                return isinstance(t, int) and t == NBLK - 1

            def tailb(t):
                return not isinstance(t, int) or t >= 1

            block = bctx.enter_context(nc.Block())

            @block.sync
            def _(sp):
                def load_head(t, u):
                    sp.dma_start(hb[u][:, 0, 0, :], hts[bass.ds(t, 1), :, 0:P].rearrange("a p n -> (a p) n")
                                 ).then_inc(s_hh[u], 16)

                def load_rest(t, u):
                    sp.dma_start(hb[u][:, :, :, :].rearrange("p a k t -> p (a k t)")[:, P:],
                                 hts[bass.ds(t, 1), :, P:].rearrange("a p n -> (a p) n")
                                 ).then_inc(s_hb[u], 16)

                def load_outputs(t, u):
                    sp.dma_start(ob[u][:, :, :, :].rearrange("p a k t -> p (a k) t"),
                                 ots[bass.ds(t, 1)].rearrange("a p n -> (a p) n"), transpose=True
                                 ).then_inc(s_ob[u], 16)

                def load_x(t, u):
                    need(sp, s_r, (t - 1) * 2)
                    sp.dma_start(xb[u][:, :], x[bass.ds(t * P, P), :]).then_inc(s_xb[u], 16)

                def turn_merged():
                    sp.dma_start(mT[:, :, :, :].rearrange("p a k t -> p (a k) t"),
                                 m16[:, :, :].rearrange("p a n -> p (a n)"), transpose=True).then_inc(s_mT, 16)

                load_x(0, 0)
                load_head(1, 1)
                load_rest(1, 1)
                load_outputs(1, 1)
                load_x(1, 1)
                for i in range(NPRE + 3, NP_):
                    load_piece(sp, i)
                sp.dma_start(gfin, g_final.partition_broadcast(P)).then_inc(s_gf, 16)

                def step(t, h, u):
                    loads = not isinstance(t, int) or 2 <= t + 1 < NBLK
                    if tailb(t):
                        need(sp, s_m16, t * 2)
                    if loads:
                        load_head(t + 1, 1 - u)
                    if tailb(t):
                        if isinstance(t, int) and t == 1:
                            for s in s_plo:
                                sp.wait_ge(s, 14)
                        if isinstance(t, int) and t == NBLK:
                            sp.wait_ge(s_w, (t - 1) * 2)
                        turn_merged()
                    if loads:
                        load_rest(t + 1, 1 - u)
                        load_outputs(t + 1, 1 - u)
                        load_x(t + 1, 1 - u)
                    if tailb(t):
                        need(sp, s_fin, t)
                        sp.dma_start(out[bass.ds((t - 1) * P, P), :], fin[1 - u]).then_inc(s_out[1 - u], 16)

                stepsb(sp, step)
                for s in s_out:
                    sp.wait_ge(s, 16 * (NBLK // 2))

            @block.gpsimd
            def _(pool):
                def merge_sum(t, j):
                    need(pool, s_yt, t * 4 + 2 * j + 2)
                    need(pool, s_m16, t * 2)
                    pool.tensor_tensor(mg[:, j * 512:(j + 1) * 512], ta, tb, ALU.add).then_inc(s_mg, 1)

                def step(t, h, u):
                    if isinstance(t, int) and t == 0:
                        for i in range(NPRE, NP_):
                            split_piece_pool(pool, i)
                            if i in (8, 12):
                                merge_sum(0, i // 12)
                    elif frontb(t):
                        for j in range(2):
                            merge_sum(t, j)

                stepsb(pool, step)

            @block.scalar
            def _(act):
                act.preload_act_table_set("natural_log_exp_and_others")

                def sigmoids(t, j):
                    for a in range(2):
                        n = 2 * j + a
                        need(act, s_gm, t * 4 + n + 1)
                        act.activation(sg[j][a], sg[j][a], ACT.Exp).then_inc(s_gx, 1)
                        need(act, s_gx, t * 8 + 2 * n + 1)
                        act.activation(sg[j][a], sg[j][a], ACT.Ln, bias=1.0).then_inc(s_gx, 1)
                    for a in range(2):
                        need(act, s_gl, t * 4 + 2 * j + a + 1)
                        act.activation(sg[j][a], sg[j][a], ACT.Exp, scale=-1.0).then_inc(s_sg, 1)

                def step(t, h, u):
                    if isinstance(t, int) and t == 0:
                        sigmoids(0, 0)
                        for i in range(NPRE, NP_):
                            split_piece(act, i, ACT_K, ())
                            if i == 11:
                                sigmoids(0, 1)
                        return
                    if frontb(t):
                        sigmoids(t, 0)
                        sigmoids(t, 1)
                    if tailb(t):
                        need(act, s_r, t * 2)
                        act.activation(junkb[:, :], res, ACT.Square, accum_out=ss[:, :]).then_inc(s_fss, 1)
                        rsqrt_table(act, s_fv, t, s_ft, (t - 1) * 2, var[:, :], lnv[:, :], y0[:, :])

                stepsb(act, step)

            @block.tensor
            def _(pe):
                def gate(t, u, j, a):
                    if isinstance(t, int) and t == 0:
                        if j == 0:
                            return
                        pieces_split(pe, GA + a, j)
                    n = 2 * j + a
                    need(pe, s_gl, t * 4 + n - 1 if n >= 2 else (t - 1) * 4 + n + 3)
                    gate_products(pe, hb[u], j, a)

                def branch(t, u, j, a):
                    if isinstance(t, int) and t == 0:
                        pieces_split(pe, OA + a, j)
                    n = 2 * j + a
                    need(pe, s_yt, t * 4 + n - 1 if n >= 2 else (t - 1) * 4 + n + 3)
                    for i in range(3 * BH):
                        k, s = divmod(i, 3)
                        l, r = ((0, 0), (0, 1), (1, 0))[s]
                        last = pe.matmul(bank[2 + a][:, :], ob[u][:, l, a * BH + k, :],
                                         (wa0, wa1)[a][:, r, k, j * 512:(j + 1) * 512], start=i == 0,
                                         stop=i == 3 * BH - 1)
                    last.then_inc(s_y, 1)

                def final(t, j):
                    if isinstance(t, int) and t == 1:
                        pieces_split(pe, WO, j)
                    need(pe, s_mT, t * 16)
                    need(pe, s_r, (t - 1) * 2)
                    for i in range(3 * KT):
                        k, s = divmod(i, 3)
                        l, r = ((0, 0), (0, 1), (1, 0))[s]
                        last = pe.matmul(bank[6 + j][:, :], mT[:, l, k, :], wo[:, r, k, j * 512:(j + 1) * 512],
                                         start=i == 0, stop=i == 3 * KT - 1)
                    last.then_inc(s_w, 1)

                def step(t, h, u):
                    if frontb(t):
                        need(pe, s_hh[u], 16 * (h + u))
                        need(pe, s_hb[u], 16 * h + 16)
                        gate(t, u, 0, 0)
                        gate(t, u, 0, 1)
                    if frontb(t):
                        need(pe, s_ob[u], 16 * h + 16)
                        branch(t, u, 0, 0)
                        branch(t, u, 0, 1)
                    if tailb(t) and not last_front(t):
                        final(t, 0)
                        final(t, 1)
                    if frontb(t):
                        for a in range(2):
                            gate(t, u, 1, a)
                        for a in range(2):
                            branch(t, u, 1, a)
                    if last_front(t):
                        final(t, 0)
                        final(t, 1)

                stepsb(pe, step)

            @block.vector
            def _(dve):
                def softplus_gates(t, j):
                    for a in range(2):
                        n = 2 * j + a
                        need(dve, s_g, t * 4 + n + 1)
                        need(dve, s_yt, (t - 1) * 4 + n + 1)
                        ng = ngs[:, a:a + 1]
                        dve.tensor_scalar(sg[j][a], bank[a][:, :], ng, BIG_ARG, ALU.mult,
                                          ALU.min).then_inc(s_gm, 1)
                    for a in range(2):
                        n = 2 * j + a
                        ng = ngs[:, a:a + 1]
                        need(dve, s_gx, t * 8 + 2 * n + 2)
                        dve.scalar_tensor_tensor(sg[j][a], bank[a][:, :], ng, sg[j][a], ALU.mult,
                                                 ALU.max).then_inc(s_gl, 1)

                def merge(t, j):
                    for a, o in ((0, ta), (1, tb)):
                        n = 2 * j + a
                        need(dve, s_y, t * 4 + n + 1)
                        need(dve, s_sg, t * 4 + n + 1)
                        need(dve, s_mg, t * 2 + j)
                        dve.scalar_tensor_tensor(o, bank[2 + a][:, :], ysc[:, a:a + 1], sg[j][a], ALU.mult,
                                                 ALU.mult).then_inc(s_yt, 1)

                def split_merged(t):
                    need(dve, s_mg, t * 2 + 2)
                    dve.tensor_reduce(mmax[:, :], mg, AX.X, ALU.max, apply_absolute_value=True
                                      ).then_inc(s_ms, 1)
                    need(dve, s_ms, t * 5 + 1)
                    dve.tensor_scalar(mmax[:, :], mmax[:, :], 1e-30, None, ALU.max).then_inc(s_ms, 1)
                    need(dve, s_ms, t * 5 + 2)
                    dve.tensor_scalar(mmax[:, :].bitcast(U32), mmax[:, :].bitcast(U32), 0x7F800000, None,
                                      ALU.bitwise_and).then_inc(s_ms, 1)
                    need(dve, s_ms, t * 5 + 3)
                    dve.tensor_scalar(msc[:, :], mmax[:, :], 2.0 ** -10, None, ALU.mult).then_inc(s_ms, 1)
                    need(dve, s_ms, t * 5 + 4)
                    dve.reciprocal(minv[:, :], msc[:, :]).then_inc(s_ms, 1)
                    need(dve, s_ms, t * 5 + 5)
                    need(dve, s_mT, t * 16)
                    dve.tensor_scalar(m16[:, 0], mg, minv[:, 0:1], None, ALU.mult).then_inc(s_m16, 1)
                    need(dve, s_m16, t * 2 + 1)
                    dve.scalar_tensor_tensor(m16[:, 1], mg, minv[:, 0:1], m16[:, 0], ALU.mult,
                                             ALU.subtract).then_inc(s_m16, 1)

                def branch_scales(t):
                    dve.tensor_tensor(ysc[:, :], oscale[:, bass.ds(t, 1), :].rearrange("p a b -> p (a b)"),
                                      uscale[:, OA:OB + 1], ALU.mult).then_inc(s_ys, 1)
                    need(dve, s_ys, t + 1)

                def add_residual(t, h, u):
                    need(dve, s_rs, t)
                    need(dve, s_xb[1 - u], 16 * (h + u))
                    need(dve, s_fn, (t - 1) * 4)
                    need(dve, s_fin, t - 1)
                    for j in range(2):
                        need(dve, s_w, (t - 1) * 2 + j + 1)
                        dve.scalar_tensor_tensor(res[:, j * 512:(j + 1) * 512], bank[6 + j][:, :],
                                                 rsc[:, 0:1], xb[1 - u][:, j * 512:(j + 1) * 512],
                                                 ALU.mult, ALU.add).then_inc(s_r, 1)

                def step0():
                    softplus_gates(0, 0)
                    for i in range(NPRE, NP_):
                        split_piece(dve, i, DVE_K, (0, 1, 2))
                        if i == 8:
                            branch_scales(0)
                            merge(0, 0)
                        elif i == 11:
                            softplus_gates(0, 1)
                        elif i == 12:
                            merge(0, 1)
                        elif i == 13:
                            split_merged(0)

                def step(t, h, u):
                    if isinstance(t, int) and t == 0:
                        step0()
                        return
                    front, tail = frontb(t), tailb(t)
                    if front:
                        softplus_gates(t, 0)
                        branch_scales(t)
                        merge(t, 0)
                    if tail:
                        dve.tensor_tensor(rsc[:, :], uscale[:, WO:WO + 1], msc[:, :], ALU.mult).then_inc(s_rs, 1)
                    if tail and not last_front(t):
                        add_residual(t, h, u)
                    if front:
                        softplus_gates(t, 1)
                        merge(t, 1)
                        split_merged(t)
                    if last_front(t):
                        add_residual(t, h, u)
                    if tail:
                        rsqrt_start(dve, s_fss, t, s_fv, ss[:, :], var[:, :], D)
                        rsqrt_newton(dve, s_ft, (t - 1) * 2, s_fn, (t - 1) * 4, var[:, :], y0[:, :],
                                     nt[:, 0:1], rstd[:, :])
                        need(dve, s_fn, t * 4)
                        need(dve, s_out[1 - u], 16 * (h - 1 + u))
                        if isinstance(t, int) and t == 1:
                            dve.wait_ge(s_gf, 16)
                        dve.scalar_tensor_tensor(fin[1 - u], res, rstd[:, 0:1], gfin, ALU.mult,
                                                 ALU.mult).then_inc(s_fin, 1)

                stepsb(dve, step)


_INS = ["x", "positions", "g_in", "w_branch", "w_units", "w_alpha_up", "b_alpha", "attn_sinks",
        "g_gla_norm", "g_final"]


def kernel(**inputs):
    import numpy as _np
    import concourse.bacc as _bacc
    from concourse import mybir as _mybir
    from concourse.bass_utils import run_bass_kernel_spmd as _run

    nc = _bacc.Bacc("TRN2", target_bir_lowering=False, num_devices=1)
    arrays, args = {}, []
    laid = {k: _np.asarray(v) if k == "g_final" else _np.asarray(v)[0] for k, v in inputs.items()}
    for k in ("positions", "g_in", "g_gla_norm", "b_alpha"):
        laid[k] = laid[k].reshape(-1, P).T
    w_in = laid["w_in"]
    laid["w_branch"] = w_in[:, :NA]
    laid["w_units"] = _np.concatenate([w_in[:, NA:NA + D], w_in[:, NA + D:], laid["w_out_a"],
                                       laid["w_out_b"], laid["w_o"]]).reshape(NU, P, D)
    for name in _INS:
        a = _np.ascontiguousarray(laid[name])
        arrays[f"in_{name}_dram"] = a
        args.append(nc.dram_tensor(f"in_{name}_dram", a.shape, _mybir.dt.from_np(a.dtype),
                                   kind="ExternalInput").ap())
    out = nc.dram_tensor("out_0_dram", (SEQ, D), _mybir.dt.float32, kind="ExternalOutput").ap()
    hybrid_block(nc, *args, out)
    r = _run(nc, [arrays], core_ids=[0])
    return r.results[0]["out_0_dram"].reshape(1, SEQ, D)
```
